# Optimizing a Trainium2 kernel written in Bass

```python
import jax, jax.numpy as jnp
from jax import lax
import numpy as np

D_MODEL = 2048
BATCH = 1
SEQ = 256
DEPTH = 1

N_META = 16
D_FF = 5632
FFN_RES = 0.5
EPS = 1e-6
DSA_HEADS = 8
DSA_HEAD_DIM = 128
DSA_WIDTH = DSA_HEADS * DSA_HEAD_DIM
IDX_HEADS = 16
IDX_DIM = 64
TOPK_MAX = 256
Q_BLOCK = 128
GLA_HEADS = 4
GLA_DK = 128
GLA_DV = 256
GLA_KEY_WIDTH = GLA_HEADS * GLA_DK
GLA_WIDTH = GLA_HEADS * GLA_DV
GLA_GATE_RANK = 16
GLA_TAU = 16.0
GLA_CHUNK = 64
MIX_WIDTH = DSA_WIDTH + GLA_WIDTH
IN_SPLITS = (DSA_WIDTH, DSA_WIDTH, DSA_WIDTH,
             IDX_HEADS * IDX_DIM, IDX_DIM, IDX_HEADS,
             GLA_KEY_WIDTH, GLA_KEY_WIDTH, GLA_WIDTH,
             GLA_GATE_RANK, GLA_WIDTH)
IN_WIDTH = sum(IN_SPLITS)


def rms_norm(x, g):
    x32 = x.astype(jnp.float32)
    y = x32 * lax.rsqrt(jnp.mean(x32 * x32, axis=-1, keepdims=True) + EPS)
    return (y * g.astype(jnp.float32)).astype(x.dtype)

def swiglu(x, w_gate, w_up, w_down):
    return (jax.nn.silu(x @ w_gate) * (x @ w_up)) @ w_down

def dsa_attention(q, k, v, q_idx, k_idx, w_idx, top_k):
    b, t, nh, dh = q.shape
    n_blk = -(-t // Q_BLOCK)
    t_pad = n_blk * Q_BLOCK

    def blocks(a):
        a = jnp.pad(a, [(0, 0), (0, t_pad - t)] + [(0, 0)] * (a.ndim - 2))
        a = a.reshape((b, n_blk, Q_BLOCK) + a.shape[2:])
        return jnp.moveaxis(a, 1, 0)

    pos_q = jnp.arange(t_pad, dtype=jnp.int32).reshape(n_blk, Q_BLOCK)
    key_pos = jnp.arange(t, dtype=jnp.int32)
    scale = DSA_HEAD_DIM ** -0.5
    gather = jax.vmap(lambda a, i: a[i])

    def one_block(args):
        qb, qib, wb, pq = args
        logits = jnp.einsum('bqhd,bsd->bqhs', qib, k_idx)
        score = jnp.einsum('bqhs,bqh->bqs', jax.nn.relu(logits), wb).astype(jnp.float32)
        causal = key_pos[None, :] <= pq[:, None]
        score = jnp.where(causal[None], score, -jnp.inf)
        _, sel = lax.top_k(score, top_k)
        valid = sel <= pq[None, :, None]
        ks = gather(k, sel)
        vs = gather(v, sel)
        s = jnp.einsum('bqhd,bqkhd->bhqk', qb, ks).astype(jnp.float32) * scale
        s = jnp.where(valid[:, None], s, -1e30)
        p = jax.nn.softmax(s, axis=-1).astype(v.dtype)
        return jnp.einsum('bhqk,bqkhd->bqhd', p, vs)

    out = lax.map(one_block, (blocks(q), blocks(q_idx), blocks(w_idx), pos_q))
    out = jnp.moveaxis(out, 0, 1).reshape(b, t_pad, nh, dh)
    return out[:, :t]

def gla_chunked(q, k, v, log_g):
    b, t, h, dk = q.shape
    dv = v.shape[-1]
    lead = GLA_CHUNK - N_META
    f32 = jnp.float32

    def prep(a):
        a = jnp.pad(a, [(0, 0), (lead, 0), (0, 0), (0, 0)])
        n = a.shape[1] // GLA_CHUNK
        a = a.reshape(b, n, GLA_CHUNK, h, a.shape[-1])
        return jnp.moveaxis(a, 1, 0)

    causal = jnp.tril(jnp.ones((GLA_CHUNK, GLA_CHUNK), dtype=bool))[None, :, :, None, None]

    def step(state, inp):
        qi, ki, vi, gi = inp
        qf, kf, vf = qi.astype(f32), ki.astype(f32), vi.astype(f32)
        bcum = jnp.cumsum(gi.astype(f32), axis=1)
        o_inter = jnp.einsum('bchk,bhkv->bchv', qf * jnp.exp(bcum), state)
        diff = bcum[:, :, None] - bcum[:, None, :]
        decay = jnp.exp(jnp.where(causal, diff, -jnp.inf))
        attn = jnp.einsum('bihk,bjhk,bijhk->bhij', qf, kf, decay)
        o_intra = jnp.einsum('bhij,bjhv->bihv', attn, vf)
        b_last = bcum[:, -1]
        k_dec = kf * jnp.exp(b_last[:, None] - bcum)
        state = state * jnp.exp(b_last)[..., None] + jnp.einsum('bchk,bchv->bhkv', k_dec, vf)
        return state, (o_inter + o_intra).astype(v.dtype)

    state0 = jnp.zeros((b, h, dk, dv), f32)
    _, out = lax.scan(step, state0, (prep(q), prep(k), prep(v), prep(log_g)))
    out = jnp.moveaxis(out, 0, 1).reshape(b, lead + t, h, dv)
    return out[:, lead:]

def hybrid_mixer(h, w_in, w_gate_up, b_gate, gla_norm_g, w_out, top_k):
    b, t, _ = h.shape
    proj = h @ w_in
    (dq, dk_, dv_, iq, ik, iw, gq, gk, gv, g_low, g_out) = jnp.split(
        proj, np.cumsum(IN_SPLITS)[:-1].tolist(), axis=-1)
    dq = dq.reshape(b, t, DSA_HEADS, DSA_HEAD_DIM)
    dk_ = dk_.reshape(b, t, DSA_HEADS, DSA_HEAD_DIM)
    dv_ = dv_.reshape(b, t, DSA_HEADS, DSA_HEAD_DIM)
    iq = iq.reshape(b, t, IDX_HEADS, IDX_DIM) * (IDX_DIM ** -0.5)
    iw = iw * (IDX_HEADS ** -0.5)
    o_dsa = dsa_attention(dq, dk_, dv_, iq, ik, iw, top_k).reshape(b, t, DSA_WIDTH)
    gq = gq.reshape(b, t, GLA_HEADS, GLA_DK) * (GLA_DK ** -0.5)
    gk = gk.reshape(b, t, GLA_HEADS, GLA_DK)
    gv = gv.reshape(b, t, GLA_HEADS, GLA_DV)
    gate_logit = (g_low @ w_gate_up + b_gate).astype(jnp.float32)
    log_g = (jax.nn.log_sigmoid(gate_logit) / GLA_TAU).reshape(b, t, GLA_HEADS, GLA_DK)
    o_gla = gla_chunked(gq, gk, gv, log_g)
    o_gla = rms_norm(o_gla, gla_norm_g) * jax.nn.silu(g_out.reshape(b, t, GLA_HEADS, GLA_DV))
    o_gla = o_gla.reshape(b, t, GLA_WIDTH)
    return jnp.concatenate([o_dsa, o_gla], axis=-1) @ w_out

def first_inputs(seed: int = 0) -> dict:
    key = jax.random.key(seed)
    ks = jax.random.split(key, 20)
    f32 = jnp.float32

    def w(k, shape, fan_in):
        return jax.random.normal(k, shape, f32) * (fan_in ** -0.5)

    def gain(k, shape):
        return 1.0 + 0.02 * jax.random.normal(k, shape, f32)

    L = DEPTH
    return {
        "x": jax.random.normal(ks[0], (BATCH, SEQ, D_MODEL), f32),
        "meta_tokens": jax.random.normal(ks[1], (N_META, D_MODEL), f32),
        "ffn1_pre_g": gain(ks[2], (L, D_MODEL)),
        "ffn1_w_gate": w(ks[3], (L, D_MODEL, D_FF), D_MODEL),
        "ffn1_w_up": w(ks[4], (L, D_MODEL, D_FF), D_MODEL),
        "ffn1_w_down": w(ks[5], (L, D_FF, D_MODEL), D_FF),
        "ffn1_post_g": gain(ks[6], (L, D_MODEL)),
        "mix_pre_g": gain(ks[7], (L, D_MODEL)),
        "w_in": w(ks[8], (L, D_MODEL, IN_WIDTH), D_MODEL),
        "w_gate_up": w(ks[9], (L, GLA_GATE_RANK, GLA_KEY_WIDTH), GLA_GATE_RANK),
        "b_gate": 0.01 * jax.random.normal(ks[10], (L, GLA_KEY_WIDTH), f32),
        "gla_norm_g": gain(ks[11], (L, GLA_DV)),
        "w_out": w(ks[12], (L, MIX_WIDTH, D_MODEL), MIX_WIDTH),
        "mix_post_g": gain(ks[13], (L, D_MODEL)),
        "ffn2_pre_g": gain(ks[14], (L, D_MODEL)),
        "ffn2_w_gate": w(ks[15], (L, D_MODEL, D_FF), D_MODEL),
        "ffn2_w_up": w(ks[16], (L, D_MODEL, D_FF), D_MODEL),
        "ffn2_w_down": w(ks[17], (L, D_FF, D_MODEL), D_FF),
        "ffn2_post_g": gain(ks[18], (L, D_MODEL)),
    }

def first_block(x, meta_tokens, ffn1_pre_g, ffn1_w_gate, ffn1_w_up, ffn1_w_down, ffn1_post_g,
              mix_pre_g, w_in, w_gate_up, b_gate, gla_norm_g, w_out, mix_post_g,
              ffn2_pre_g, ffn2_w_gate, ffn2_w_up, ffn2_w_down, ffn2_post_g):
    b = x.shape[0]
    top_k = min(TOPK_MAX, SEQ // 4)
    meta = jnp.broadcast_to(meta_tokens[None].astype(x.dtype), (b, N_META, x.shape[-1]))
    hs = jnp.concatenate([meta, x], axis=1)
    for l in range(DEPTH):
        f = swiglu(rms_norm(hs, ffn1_pre_g[l]), ffn1_w_gate[l], ffn1_w_up[l], ffn1_w_down[l])
        hs = hs + FFN_RES * rms_norm(f, ffn1_post_g[l])
        m = hybrid_mixer(rms_norm(hs, mix_pre_g[l]), w_in[l], w_gate_up[l], b_gate[l],
                         gla_norm_g[l], w_out[l], top_k)
        hs = hs + rms_norm(m, mix_post_g[l])
        f = swiglu(rms_norm(hs, ffn2_pre_g[l]), ffn2_w_gate[l], ffn2_w_up[l], ffn2_w_down[l])
        hs = hs + FFN_RES * rms_norm(f, ffn2_post_g[l])
    return hs[:, N_META:]


CHUNK = 64
D_RWKV = D_MODEL // 2
D_HGRN = D_MODEL - D_RWKV
RWKV_HEAD = 64
RWKV_HEADS = D_RWKV // RWKV_HEAD
DECAY_RANK = max(32, int(round(1.8 * D_RWKV ** 0.5 / 32)) * 32)
A_RANK = max(32, int(round(1.8 * D_RWKV ** 0.5 / 32)) * 32)
VRES_RANK = max(32, int(round(1.3 * D_RWKV ** 0.5 / 32)) * 32)
HGRN_EXPAND = 128
HGRN_HEADS = D_HGRN // HGRN_EXPAND
HGRN_HEAD_V = D_HGRN // HGRN_HEADS
RWKV_COLS = 4 * D_RWKV + DECAY_RANK + A_RANK
HGRN_COLS = 4 * D_HGRN
IN_COLS = RWKV_COLS + HGRN_COLS
ALPHA = (2 * DEPTH) ** 0.25
BETA = (8 * DEPTH) ** -0.25
LN_EPS = 1e-5
GN_EPS = 64e-5
RMS_EPS = 1e-5
LB_FLOOR = 1e-30


def _heads(t, n):
    return t.reshape(t.shape[:-1] + (-1, n))

def _layer_norm(x, w, b):
    x = x.astype(jnp.float32)
    mu = jnp.mean(x, -1, keepdims=True)
    var = jnp.mean(jnp.square(x - mu), -1, keepdims=True)
    return (x - mu) * lax.rsqrt(var + LN_EPS) * w + b

def _token_shift(y, mu):
    y_prev = jnp.pad(y, ((0, 0), (1, 0), (0, 0)))[:, :-1]
    return y + mu * (y_prev - y)

def _rwkv7_scan(r, w, k, v, a_vec, b_vec):
    Bsz, T, H, N = r.shape

    def step(S, inp):
        r_t, w_t, k_t, v_t, a_t, b_t = inp
        sa = jnp.einsum('bhij,bhj->bhi', S, a_t)
        S = S * w_t[:, :, None, :] + sa[..., None] * b_t[:, :, None, :] + v_t[..., None] * k_t[:, :, None, :]
        return S, jnp.einsum('bhij,bhj->bhi', S, r_t)

    S0 = jnp.zeros((Bsz, H, N, N), jnp.float32)
    xs = tuple(jnp.moveaxis(t, 1, 0) for t in (r, w, k, v, a_vec, b_vec))
    _, o = lax.scan(step, S0, xs)
    return jnp.moveaxis(o, 0, 1)

def _rwkv7_branch(rw, v_first, w0, w_up, a0, a_up, k_k, k_a, r_k, gn_w, gn_b, v_mix):
    r, k, v, z, wd, ad = jnp.split(
        rw, [D_RWKV, 2 * D_RWKV, 3 * D_RWKV, 4 * D_RWKV, 4 * D_RWKV + DECAY_RANK], axis=-1)
    w_raw = w0 + jnp.tanh(wd) @ w_up
    decay = jnp.exp(-jnp.exp(-jax.nn.softplus(-w_raw) - 0.5))
    a = jax.nn.sigmoid(a0 + ad @ a_up)
    if v_mix is None:
        v_first = v
    else:
        v0, v_down, v_up = v_mix
        v = v + (v_first - v) * jax.nn.sigmoid(v0 + (v @ v_down) @ v_up)
    kk = _heads(k * k_k, RWKV_HEAD)
    kk = kk / jnp.maximum(jnp.sqrt(jnp.sum(kk * kk, -1, keepdims=True)), 1e-12)
    k = k * (1.0 + (a - 1.0) * k_a)
    rh, kh, vh = _heads(r, RWKV_HEAD), _heads(k, RWKV_HEAD), _heads(v, RWKV_HEAD)
    ah = _heads(a, RWKV_HEAD)
    o = _rwkv7_scan(rh, _heads(decay, RWKV_HEAD), kh, vh, -kk, kk * ah)
    mu = jnp.mean(o, -1, keepdims=True)
    var = jnp.mean(jnp.square(o - mu), -1, keepdims=True)
    o = (o - mu) * lax.rsqrt(var + GN_EPS) * _heads(gn_w, RWKV_HEAD) + _heads(gn_b, RWKV_HEAD)
    o = o + jnp.sum(rh * kh * _heads(r_k, RWKV_HEAD), -1, keepdims=True) * vh
    return o.reshape(rw.shape[:-1] + (D_RWKV,)) * jax.nn.silu(z), v_first

def _hgrn2_chunkwise(q, log_f, k, i):
    Bsz, T, H, DK = q.shape
    DV = i.shape[-1]
    NC = T // CHUNK

    def to_chunks(t):
        return jnp.moveaxis(t.reshape(Bsz, NC, CHUNK, H, t.shape[-1]), 1, 0)

    causal = jnp.tril(jnp.ones((CHUNK, CHUNK), bool))[None, :, :, None, None]

    def step(S, inp):
        q_c, lf_c, k_c, i_c = inp
        b = jnp.cumsum(lf_c, axis=1)
        diff = b[:, :, None] - b[:, None, :]
        decay = jnp.where(causal, jnp.exp(jnp.where(causal, diff, 0.0)), 0.0)
        att = jnp.einsum('btshd,bshd->btsh', q_c[:, :, None] * decay, k_c)
        o_intra = jnp.einsum('btsh,bshv->bthv', att, i_c)
        o_inter = jnp.einsum('bthd,bhdv->bthv', q_c * jnp.exp(b), S)
        b_last = b[:, -1]
        k_dec = k_c * jnp.exp(b_last[:, None] - b)
        S = S * jnp.exp(b_last)[..., None] + jnp.einsum('bshd,bshv->bhdv', k_dec, i_c)
        return S, o_intra + o_inter

    S0 = jnp.zeros((Bsz, H, DK, DV), jnp.float32)
    _, o = lax.scan(step, S0, (to_chunks(q), to_chunks(log_f), to_chunks(k), to_chunks(i)))
    return jnp.moveaxis(o, 0, 1).reshape(Bsz, T, H, DV)

def _hgrn2_branch(hg, lb, g_norm_w):
    q, f_raw, i_in, z = jnp.split(hg, 4, axis=-1)
    q = jax.nn.silu(q)
    log_lb = jnp.log(jnp.maximum(lb, LB_FLOOR))
    log_f = jnp.logaddexp(log_lb, jnp.log1p(-lb) + jax.nn.log_sigmoid(f_raw))
    k = (1.0 - lb) * jax.nn.sigmoid(-f_raw)
    o = _hgrn2_chunkwise(_heads(q, HGRN_EXPAND), _heads(log_f, HGRN_EXPAND),
                         _heads(k, HGRN_EXPAND), _heads(i_in, HGRN_HEAD_V))
    o = o * lax.rsqrt(jnp.mean(o * o, -1, keepdims=True) + RMS_EPS)
    return o.reshape(hg.shape[:-1] + (D_HGRN,)) * g_norm_w * jax.nn.silu(z)

def second_inputs(seed: int = 0) -> dict:
    key = jax.random.key(seed)
    ks = jax.random.split(key, 24)
    L, L1 = DEPTH, DEPTH - 1

    def nrm(k, shape, s):
        return s * jax.random.normal(k, shape, jnp.float32)

    x = nrm(ks[0], (BATCH, SEQ, D_MODEL), 1.0)
    col_scale = jnp.concatenate([
        jnp.ones((2 * D_RWKV,), jnp.float32), jnp.full((D_RWKV,), BETA, jnp.float32),
        jnp.ones((D_RWKV + DECAY_RANK + A_RANK,), jnp.float32),
        jnp.ones((2 * D_HGRN,), jnp.float32), jnp.full((D_HGRN,), BETA, jnp.float32),
        jnp.ones((D_HGRN,), jnp.float32)])
    w_in = nrm(ks[1], (L, D_MODEL, IN_COLS), D_MODEL ** -0.5) * col_scale
    shift_mu = jax.random.uniform(ks[2], (L, RWKV_COLS), jnp.float32)
    ramp = (jnp.arange(D_RWKV, dtype=jnp.float32) / (D_RWKV - 1)) ** 0.85
    w_decay0 = -6.0 + 5.0 * ramp + nrm(ks[3], (L, D_RWKV), 0.1)
    w_decay_up = nrm(ks[4], (L, DECAY_RANK, D_RWKV), 0.3 * DECAY_RANK ** -0.5)
    a0 = nrm(ks[5], (L, D_RWKV), 0.1)
    a_up = nrm(ks[6], (L, A_RANK, D_RWKV), 0.3 * A_RANK ** -0.5)
    k_k = 0.85 + nrm(ks[7], (L, D_RWKV), 0.05)
    k_a = 1.0 + nrm(ks[8], (L, D_RWKV), 0.05)
    r_k = nrm(ks[9], (L, D_RWKV), 0.1)
    ln_x_w = 1.0 + nrm(ks[10], (L, D_RWKV), 0.05)
    ln_x_b = nrm(ks[11], (L, D_RWKV), 0.02)
    v_mix0 = 1.0 + nrm(ks[12], (L1, D_RWKV), 0.1)
    v_mix_down = nrm(ks[13], (L1, D_RWKV, VRES_RANK), D_RWKV ** -0.5)
    v_mix_up = nrm(ks[14], (L1, VRES_RANK, D_RWKV), 0.3 * VRES_RANK ** -0.5)
    lb_logits = nrm(ks[15], (L, D_HGRN), 0.5)
    g_norm_w = 1.0 + nrm(ks[16], (L, D_HGRN), 0.05)
    w_out = nrm(ks[17], (L, D_MODEL, D_MODEL), BETA * D_MODEL ** -0.5)
    ln_w = 1.0 + nrm(ks[18], (L, D_MODEL), 0.05)
    ln_b = nrm(ks[19], (L, D_MODEL), 0.02)
    return {"x": x, "w_in": w_in, "shift_mu": shift_mu, "w_decay0": w_decay0,
            "w_decay_up": w_decay_up, "a0": a0, "a_up": a_up, "k_k": k_k, "k_a": k_a,
            "r_k": r_k, "ln_x_w": ln_x_w, "ln_x_b": ln_x_b, "v_mix0": v_mix0,
            "v_mix_down": v_mix_down, "v_mix_up": v_mix_up, "lb_logits": lb_logits,
            "g_norm_w": g_norm_w, "w_out": w_out, "ln_w": ln_w, "ln_b": ln_b}

def second_block(x, w_in, shift_mu, w_decay0, w_decay_up, a0, a_up, k_k, k_a, r_k, ln_x_w, ln_x_b,
              v_mix0, v_mix_down, v_mix_up, lb_logits, g_norm_w, w_out, ln_w, ln_b):
    out_dtype = x.dtype
    lb_sm = jax.nn.softmax(lb_logits.astype(jnp.float32), axis=0)
    lower_bounds = jnp.cumsum(lb_sm, axis=0) - lb_sm[0]
    h = x.astype(jnp.float32)
    v_first = None
    for l in range(DEPTH):
        proj = jnp.einsum('btd,dc->btc', h, w_in[l].astype(jnp.float32))
        rw = _token_shift(proj[..., :RWKV_COLS], shift_mu[l])
        hg = proj[..., RWKV_COLS:]
        v_mix = None if l == 0 else (v_mix0[l - 1], v_mix_down[l - 1], v_mix_up[l - 1])
        o_rwkv, v_first = _rwkv7_branch(rw, v_first, w_decay0[l], w_decay_up[l], a0[l], a_up[l],
                                        k_k[l], k_a[l], r_k[l], ln_x_w[l], ln_x_b[l], v_mix)
        o_hgrn = _hgrn2_branch(hg, lower_bounds[l], g_norm_w[l])
        y = jnp.einsum('btc,cd->btd', jnp.concatenate([o_rwkv, o_hgrn], axis=-1), w_out[l])
        h = _layer_norm(ALPHA * h + y, ln_w[l], ln_b[l])
    return h.astype(out_dtype)


def setup_inputs(seed=0):
    out = dict(first_inputs(seed))
    for name, value in second_inputs(seed + 1).items():
        if name != "x":
            out[name + "_2"] = value
    return out


def reference(
    x, meta_tokens, ffn1_pre_g, ffn1_w_gate, ffn1_w_up, ffn1_w_down, ffn1_post_g, mix_pre_g,
    w_in, w_gate_up, b_gate, gla_norm_g, w_out, mix_post_g, ffn2_pre_g, ffn2_w_gate, ffn2_w_up,
    ffn2_w_down, ffn2_post_g, w_in_2, shift_mu_2, w_decay0_2, w_decay_up_2, a0_2, a_up_2, k_k_2,
    k_a_2, r_k_2, ln_x_w_2, ln_x_b_2, v_mix0_2, v_mix_down_2, v_mix_up_2, lb_logits_2,
    g_norm_w_2, w_out_2, ln_w_2, ln_b_2,
):
    x = first_block(
        x, meta_tokens, ffn1_pre_g, ffn1_w_gate, ffn1_w_up, ffn1_w_down, ffn1_post_g, mix_pre_g,
        w_in, w_gate_up, b_gate, gla_norm_g, w_out, mix_post_g, ffn2_pre_g, ffn2_w_gate,
        ffn2_w_up, ffn2_w_down, ffn2_post_g,
    )
    return second_block(
        x, w_in_2, shift_mu_2, w_decay0_2, w_decay_up_2, a0_2, a_up_2, k_k_2, k_a_2, r_k_2,
        ln_x_w_2, ln_x_b_2, v_mix0_2, v_mix_down_2, v_mix_up_2, lb_logits_2, g_norm_w_2,
        w_out_2, ln_w_2, ln_b_2,
    )


_drawn_inputs = setup_inputs


def setup_inputs(seed=0):
    import zlib

    import numpy as np

    out = dict(_drawn_inputs(seed))
    spreads = {}
    factors = {'b_gate': 8.0,
     'gla_norm_g': 3.945,
     'mix_post_g': 3.616,
     'ffn2_pre_g': 5.612,
     'ffn2_post_g': 8.0,
     'w_decay_up_2': 8.0,
     'a0_2': 6.233,
     'k_k_2': 200.0,
     'k_a_2': 5.042,
     'ln_x_w_2': 54.256,
     'ln_x_b_2': 200.0,
     'g_norm_w_2': 40.088,
     'ln_b_2': 2.809}
    for name, (base, spread) in spreads.items():
        noise = np.random.default_rng([zlib.crc32(name.encode()), seed]).standard_normal(out[name].shape)
        drawn = base * np.exp(spread * noise) if base else spread * noise
        out[name] = __import__('jax').numpy.asarray(drawn.astype(out[name].dtype))
    for name, factor in factors.items():
        out[name] = (out[name] * factor).astype(out[name].dtype)
    return out
```

```python
from contextlib import ExitStack

import concourse.bass as bass
from concourse import mybir
import numpy as np

ALU = mybir.AluOpType
ACT = mybir.ActivationFunctionType
AX = mybir.AxisListType
F32 = mybir.dt.float32
F32R = mybir.dt.float32r
U8 = mybir.dt.uint8

P = 128
D = 2048
DC = D // P
N_META = 16
SEQ = 256
T1 = N_META + SEQ
D_FF = 5632
FT = D_FF // P
TILES = [(0, 128), (128, 128), (256, 16)]
EPS = 1e-6

DSA_HEADS = 8
IDX_HEADS = 16
IDX_DIM = 64
TOP_K = min(256, SEQ // 4)
GLA_HEADS = 4
GLA_DV = 256
GLA_TAU = 16.0

RAW = 4
SPLIT = 2
MASKED = -1.0e30
TAKEN = -3.0e38


class Signal:

    def __init__(self, nc, ctx, name):
        self.sem = ctx.enter_context(nc.semaphore(name))
        self.n = 0

    def on(self, instruction, by=1):
        instruction.then_inc(self.sem, by)
        self.n += by
        return instruction


class Machine:

    def __init__(self, nc, ctx):
        self.nc, self.ctx = nc, ctx
        self.signals = {}
        self.unit = 0
        self.group = 0
        self.pairs = 0

    def sb(self, name, shape, dt=F32, ctx=None, side="left"):
        return (ctx or self.ctx).enter_context(self.nc.sbuf_tensor(name, shape, dt, side=side))

    def sig(self, name):
        if name not in self.signals:
            self.signals[name] = Signal(self.nc, self.ctx, name)
        return self.signals[name]

    def open_x(self, name):
        self.x_scope = self.ctx.enter_context(ExitStack())
        self.x_hi, self.x_lo = (self.sb(f"{name}_{part}", [P, DC, T1], F32R, self.x_scope, "right") for part in ("hi", "lo"))

    def close_x(self):
        self.x_scope.close()
        self.x_hi = self.x_lo = None

    def block(self):
        return self.nc.Block(no_gpsimd_drain=True)


def load_unit(m, sp, unit, stage, rel, u):
    src = stage.source(rel, u)
    dst = m.raw[:, unit % RAW, 0:stage.chunks * P].rearrange("p (k c) -> p k c", c=P)
    sp.dma_start(dst, src.rearrange("(k p) c -> p k c", p=P)).then_inc(m.raw_loaded[unit % RAW], 16)


def dense(m, stage, following):
    n0, g0 = m.unit, m.group
    count = stage.count
    per_body = 4
    loops = count // per_body - 1
    rest = range(max(loops, 0) * per_body, count)
    T = stage.T

    def over(eng, body):
        if loops >= 1:
            with eng.Fori(0, loops) as i:
                for u in range(per_body):
                    body(i, u)
        for rel in rest:
            body(rel // per_body, rel % per_body)

    def is_last(i, u):
        return isinstance(i, int) and i * per_body + u == count - 1

    with m.block() as block:

        @block.sync
        def _(sp):
            def load(i, u):
                sp.wait_ge(m.lo_ready, n0 + 4 * i + u + 1)
                load_unit(m, sp, n0 + u, stage, 4 * i + u + RAW, u)

            if loops >= 1:
                with sp.Fori(0, loops) as i:
                    for u in range(per_body):
                        load(i, u)
            for rel in rest:
                if rel + RAW < count:
                    load(rel // per_body, rel % per_body)
            if following is not None:
                for k in range(RAW):
                    n = n0 + count + k
                    sp.wait_ge(m.lo_ready, n - RAW + 1)
                    load_unit(m, sp, n, following, k, k)

        @block.scalar
        def _(act):
            def high(i, u, chunks):
                n = n0 + u
                act.wait_ge(m.raw_loaded[n % RAW], 16 * (n // RAW + 1) + 16 * i)
                act.wait_ge(m.units_done, n + 4 * i + 1)
                act.activation(m.w_hi[:, n % SPLIT, 0:chunks * P], m.raw[:, n % RAW, 0:chunks * P],
                               ACT.Copy).then_inc(m.hi_ready, 1)

            def step(i, u):
                if not is_last(i, u):
                    high(i, u + 1, stage.chunks)
                elif following is not None:
                    high(i, u + 1, following.chunks)
                stage.evacuate_act(act, i, u)

            if n0 == 0:
                high(0, 0, stage.chunks)
            over(act, step)

        @block.vector
        def _(dve):
            def low(i, u, chunks):
                n = n0 + u
                dve.wait_ge(m.hi_ready, n + 4 * i + 1)
                dve.tensor_tensor(m.w_lo[:, n % SPLIT, 0:chunks * P], m.raw[:, n % RAW, 0:chunks * P],
                                  m.w_hi[:, n % SPLIT, 0:chunks * P].bitcast(F32),
                                  ALU.subtract).then_inc(m.lo_ready, 1)

            def step(i, u):
                if not is_last(i, u):
                    low(i, u + 1, stage.chunks)
                elif following is not None:
                    low(i, u + 1, following.chunks)
                stage.evacuate_dve(dve, i, u)

            if n0 == 0:
                low(0, 0, stage.chunks)
            over(dve, step)

        if stage.evacuate_pool is not None:

            @block.gpsimd
            def _(pool):
                over(pool, lambda i, u: stage.evacuate_pool(pool, i, u))
                pool.wait_ge(m.hidden_split, m.pairs + stage.pairs + 2)

        @block.tensor
        def _(pe):
            def multiply(i, u):
                n = n0 + u
                bank, start, stop = stage.bank(u)
                group = g0 + u // stage.per_group
                out = m.ps[:, 2 * (group % 2) + bank, 0:T]
                pe.wait_ge(m.lo_ready, n + 4 * i + 1)
                if u % stage.per_group == 0:
                    pe.wait_ge(m.banks_free, group + (per_body // stage.per_group) * i + 1)
                x_hi, x_lo = stage.moving(u)
                for k in range(stage.chunks):
                    w_hi = m.w_hi[:, n % SPLIT, k * P:(k + 1) * P]
                    w_lo = m.w_lo[:, n % SPLIT, k * P:(k + 1) * P]
                    first, last = start and k == 0, stop and k == stage.chunks - 1
                    pe.matmul(out, w_hi, x_hi[:, k, 0:T], start=first, stop=False)
                    pe.matmul(out, w_hi, x_lo[:, k, 0:T], start=False, stop=False)
                    mm = pe.matmul(out, w_lo, x_hi[:, k, 0:T], start=False, stop=last)
                mm.then_inc(m.units_done, 1)

            over(pe, multiply)

    m.unit += count
    m.group += count // stage.per_group
    m.pairs += stage.pairs


class Project:

    per_group, evacuate_pool, pairs = 1, None, 0

    def __init__(self, m, weights, first_column, count, T, out, first_out=0):
        self.m, self.w, self.c0, self.count, self.T = m, weights, first_column, count, T
        self.out, self.first_out = out, first_out
        self.chunks = DC
        self.g0 = None

    def source(self, rel, u):
        return self.w[0:DC * P, bass.ds(self.c0 + rel * P, P)]

    def moving(self, u):
        return self.m.x_hi, self.m.x_lo

    def bank(self, u):
        return 0, True, True

    def evacuate_act(self, act, i, u):
        m, n0, g0 = self.m, self.m.unit, self.m.group
        act.wait_ge(m.units_done, n0 + 4 * i + u + 1 + SPLIT)
        dst = self.out[:, bass.ds(self.first_out + 4 * i + u, 1), 0:self.T]
        act.activation(dst.rearrange("p a t -> p (a t)"), m.ps[:, 2 * ((g0 + u) % 2), 0:self.T],
                       ACT.Copy).then_inc(m.banks_free, 1)

    def evacuate_dve(self, dve, i, u):
        pass


class GateUp:

    per_group, pairs = 2, FT // 2

    def __init__(self, m, w_gate, w_up, half, T, h_hi, h_lo, silu, hidden):
        self.m, self.wg, self.wu, self.half, self.T = m, w_gate, w_up, half, T
        self.h_hi, self.h_lo = h_hi, h_lo
        self.silu, self.hidden = silu, hidden
        self.chunks, self.count = DC, FT

    def source(self, rel, u):
        w = self.wu if u % 2 else self.wg
        first = self.half * (FT // 2) * P
        return w[:, bass.ds(first + (rel - u % 2) * (P // 2), P)]

    def moving(self, u):
        return self.m.x_hi, self.m.x_lo

    def bank(self, u):
        return u % 2, True, True

    def evacuate_act(self, act, i, u):
        m, n0, g0 = self.m, self.m.unit, self.m.group
        if u % 2 == 0:
            group = g0 + u // 2
            act.wait_ge(m.units_done, n0 + 4 * i + u + 1 + SPLIT)
            act.wait_ge(m.banks_free, group + 2 * i + 1)
            act.activation(self.silu[:, group % 2, 0:self.T], m.ps[:, 2 * (group % 2), 0:self.T],
                           ACT.Silu).then_inc(m.silu_ready, 1)

    def evacuate_dve(self, dve, i, u):
        m, n0, g0 = self.m, self.m.unit, self.m.group
        if u % 2 == 1:
            group, pair = g0 + u // 2, m.pairs + u // 2
            dve.wait_ge(m.units_done, n0 + 4 * i + u + 1 + SPLIT)
            dve.wait_ge(m.silu_ready, pair + 2 * i + 1)
            dve.wait_ge(m.hidden_split, pair + 2 * i + 1)
            dve.tensor_tensor(self.hidden[:, pair % 2, 0:self.T], self.silu[:, group % 2, 0:self.T],
                              m.ps[:, 2 * (group % 2) + 1, 0:self.T], ALU.mult).then_inc(m.banks_free, 1)

    def evacuate_pool(self, pool, i, u):
        m, g0 = self.m, self.m.group
        if u % 2 == 1:
            group, pair = g0 + u // 2, m.pairs + u // 2
            hidden = self.hidden[:, pair % 2, 0:self.T]
            hi = self.h_hi[:, bass.ds(2 * i + u // 2, 1), 0:self.T].rearrange("p a t -> p (a t)")
            lo = self.h_lo[:, bass.ds(2 * i + u // 2, 1), 0:self.T].rearrange("p a t -> p (a t)")
            pool.wait_ge(m.banks_free, group + 2 * i + 1 + 2)
            pool.tensor_copy(hi, hidden).then_inc(m.hidden_hi, 1)
            pool.wait_ge(m.hidden_hi, pair + 2 * i + 1)
            pool.tensor_tensor(lo, hidden, hi.bitcast(F32), ALU.subtract).then_inc(m.hidden_split, 1)


class Down:

    per_group, evacuate_pool, pairs = 2, None, 0

    def __init__(self, m, w_down, half, h_hi, h_lo, T, y):
        self.m, self.w, self.half, self.T, self.y = m, w_down, half, T, y
        self.h = (h_hi, h_lo)
        self.chunks, self.count = FT // 4, 2 * DC

    def source(self, rel, u):
        first = (self.half * 2 + u % 2) * self.chunks * P
        cols = bass.ds((rel - u % 2) * (P // 2), P)
        return self.w[first:first + self.chunks * P, cols]

    def moving(self, u):
        a = (u % 2) * self.chunks
        return tuple(h[:, a:a + self.chunks, 0:self.T] for h in self.h)

    def bank(self, u):
        return 0, u % 2 == 0, u % 2 == 1

    def evacuate_act(self, act, i, u):
        if self.half == 0 and u % 2 == 1:
            self.evacuate(act, i, u)

    def evacuate_dve(self, dve, i, u):
        if self.half == 1 and u % 2 == 1:
            self.evacuate(dve, i, u)

    def evacuate(self, eng, i, u):
        m, n0, g0 = self.m, self.m.unit, self.m.group
        group = g0 + u // 2
        eng.wait_ge(m.units_done, n0 + 4 * i + u + 1 + SPLIT)
        y = self.y[:, bass.ds(2 * i + u // 2, 1), 0:self.T].rearrange("p a t -> p (a t)")
        psum = m.ps[:, 2 * (group % 2), 0:self.T]
        if self.half == 0:
            done = eng.activation(y, psum, ACT.Copy)
        else:
            done = eng.tensor_tensor(y, psum, y, ALU.add)
        done.then_inc(m.banks_free, 1)


LEVELS = [64, 32, 16, 8, 4, 2, 1]


def make_masks(m):
    made = m.sig("masks_made")
    with ExitStack() as scope:
        full = m.sb("masks_full", [P, len(LEVELS) + 1, P], ctx=scope)
        with m.block() as block:

            @block.gpsimd
            def _(pool):
                made.on(pool.memset(full[:, :, :], 0.0))
                pool.wait_ge(made.sem, made.n)
                for level, h in enumerate(LEVELS):
                    view = full[:, level, :].rearrange("p (n a h) -> p n a h", a=2, h=h)[:, :, 1, :]
                    made.on(pool.memset(view, 1.0))
                    blocks = P // (2 * h)
                    for base, sign in ((0, 1), (h - 1, -1)):
                        pool.wait_ge(made.sem, made.n)
                        made.on(pool.affine_select(out=view, in_=view, compare_op=ALU.is_ge, fill=0.0, base=base,
                                                   pattern=[[-2 * h * sign, blocks]] * (blocks > 1) + [[0, h]] * (h > 1),
                                                   channel_multiplier=sign))
                made.on(pool.tensor_copy(full[:, len(LEVELS), :], m.ident[:, :]))
                pool.wait_ge(made.sem, made.n)
                made.on(pool.tensor_copy(m.masks[:, :, :], full[:, :, :]))
                pool.wait_ge(made.sem, made.n)


def to_tokens(m, source, chunks, tiles, tokens, name):
    turned = m.sig("chunks_turned")
    copied = [m.sig("turned_copied_act"), m.sig("turned_copied_dve")]
    groups = [(j, c) for j in range(len(tiles)) for c in range(0, chunks, 4)]
    turned0, copied0 = turned.n, [c.n for c in copied]
    with m.block() as block:

        @block.tensor
        def _(pe):
            for g, (j, c0) in enumerate(groups):
                t0, n = tiles[j]
                if g >= 4:
                    pe.wait_ge(copied[g % 2].sem, copied0[g % 2] + (g - 4) // 2 + 1)
                for c in range(4):
                    mm = pe.transpose(m.ps[0:n, g % 4, c * P:(c + 1) * P], source[:, c0 + c, t0:t0 + n],
                                      m.ident[:, :])
                turned.on(mm)

        def copy(eng, parity):
            for g, (j, c0) in enumerate(groups):
                if g % 2 == parity:
                    n = tiles[j][1]
                    dst, src = tokens[0:n, j, c0 * P:(c0 + 4) * P], m.ps[0:n, g % 4, :]
                    eng.wait_ge(turned.sem, turned0 + g + 1)
                    done = eng.activation(dst, src, ACT.Copy) if parity == 0 else eng.tensor_copy(dst, src)
                    copied[parity].on(done)

        @block.scalar
        def _(act):
            copy(act, 0)

        @block.vector
        def _(dve):
            copy(dve, 1)


def index_scores(m, proj, scores, scope):
    ik2 = m.sb("idx_keys", [P, T1], ctx=scope)
    weights = m.sb("idx_weights", [P, len(TILES), IDX_HEADS], ctx=scope)
    rectified = m.sb("idx_rectified", [P, 2, T1], ctx=scope)
    keys, turned, scaled = m.sig("idx_keys_copied"), m.sig("idx_weights_turned"), m.sig("idx_weights_scaled")
    made, relued, added = m.sig("idx_logits_made"), m.sig("idx_relued"), m.sig("idx_added")
    masked = m.sig("idx_masked")
    with m.block() as block:

        @block.scalar
        def _(act):
            keys.on(act.activation(ik2[0:IDX_DIM, :], proj[0:IDX_DIM, 32, :], ACT.Copy))
            keys.on(act.activation(ik2[IDX_DIM:P, :], proj[0:IDX_DIM, 32, :], ACT.Copy))

        @block.tensor
        def _(pe):
            w = proj[IDX_DIM:IDX_DIM + IDX_HEADS, 32, :]
            for j, (t0, n) in enumerate(TILES):
                mm = pe.matmul(m.ps[0:n, 7, j * 32:j * 32 + IDX_HEADS], w[:, t0:t0 + n],
                               m.ident[IDX_DIM:IDX_DIM + IDX_HEADS, IDX_DIM:IDX_DIM + IDX_HEADS],
                               start=True, stop=True)
            turned.on(mm)

        @block.vector
        def _(dve):
            dve.wait_ge(turned.sem, turned.n)
            for j, (t0, n) in enumerate(TILES):
                scaled.on(dve.tensor_scalar(weights[0:n, j, :], m.ps[0:n, 7, j * 32:j * 32 + IDX_HEADS],
                                            float(IDX_HEADS) ** -0.5, None, ALU.mult))

    order = [(j, h) for j in range(len(TILES)) for h in range(IDX_HEADS)]
    made0, relued0, added0 = made.n, relued.n, added.n
    with m.block() as block:

        @block.tensor
        def _(pe):
            for x, (j, h) in enumerate(order):
                (t0, n), half = TILES[j], (h % 2) * IDX_DIM
                if x >= 4:
                    pe.wait_ge(relued.sem, relued0 + x - 3)
                made.on(pe.matmul(m.ps[0:n, x % 4, 0:t0 + n], proj[half:half + IDX_DIM, 24 + h // 2, t0:t0 + n],
                                  ik2[half:half + IDX_DIM, 0:t0 + n], start=True, stop=True))

        @block.scalar
        def _(act):
            for x, (j, h) in enumerate(order):
                t0, n = TILES[j]
                act.wait_ge(made.sem, made0 + x + 1)
                if x >= 2:
                    act.wait_ge(added.sem, added0 + x - 1)
                relued.on(act.activation(rectified[0:n, x % 2, 0:t0 + n], m.ps[0:n, x % 4, 0:t0 + n], ACT.Relu,
                                         scale=float(IDX_DIM) ** -0.5))

        @block.vector
        def _(dve):
            for x, (j, h) in enumerate(order):
                t0, n = TILES[j]
                src, acc = rectified[0:n, x % 2, 0:t0 + n], scores[0:n, j, 0:t0 + n]
                dve.wait_ge(relued.sem, relued0 + x + 1)
                if h == 0:
                    added.on(dve.tensor_scalar(acc, src, weights[0:n, j, h:h + 1], None, ALU.mult))
                else:
                    dve.wait_ge(added.sem, added0 + x)
                    added.on(dve.scalar_tensor_tensor(acc, src, weights[0:n, j, h:h + 1], acc, ALU.mult, ALU.add))

        @block.gpsimd
        def _(pool):
            for j, (t0, n) in enumerate(TILES):
                acc = scores[0:n, j, 0:t0 + n]
                pool.wait_ge(added.sem, added0 + (j + 1) * IDX_HEADS)
                masked.on(pool.affine_select(out=acc, in_=acc, compare_op=ALU.is_ge, fill=MASKED, base=t0,
                                             pattern=[[-1, t0 + n]], channel_multiplier=1))
            pool.wait_ge(masked.sem, masked.n)


def select_keys(m, scores, bias, scope):
    best = m.sb("topk_best", [P, len(TILES), 8], ctx=scope)
    found, flagged, biased = m.sig("topk_steps"), m.sig("topk_flagged"), m.sig("topk_biased")
    with m.block() as block:

        @block.vector
        def _(dve):
            for j, (t0, n) in enumerate(TILES):
                row, top = scores[0:n, j, 0:t0 + n], best[0:n, j, :]
                for _ in range(TOP_K // 8):
                    if found.n:
                        dve.wait_ge(found.sem, found.n)
                    found.on(dve.max(top, row))
                    dve.wait_ge(found.sem, found.n)
                    found.on(dve.match_replace(row, top, row, TAKEN))
                dve.wait_ge(found.sem, found.n)
                flagged.on(dve.tensor_scalar(bias[0:n, j, 0:t0 + n], row, TAKEN, 1.0, ALU.is_equal, ALU.subtract))

        @block.gpsimd
        def _(pool):
            for j, (t0, n) in enumerate(TILES):
                row = bias[0:n, j, 0:t0 + n]
                pool.wait_ge(flagged.sem, j + 1)
                biased.on(pool.tensor_scalar(row, row, -MASKED, None, ALU.mult))
                pool.wait_ge(biased.sem, biased.n)
                biased.on(pool.affine_select(out=row, in_=row, compare_op=ALU.is_ge, fill=MASKED, base=t0,
                                             pattern=[[-1, t0 + n]], channel_multiplier=1))
            pool.wait_ge(biased.sem, biased.n)


def attend(m, proj, v_tokens, bias, o, scope):
    H = DSA_HEADS
    logits = m.sb("attn_logits", [P, H, T1], ctx=scope)
    turned_p = m.sb("attn_turned", [P, len(TILES), H, P], ctx=scope)
    small = m.sb("attn_small", [P, 4, H], ctx=scope)
    negated, total, inverse = small[:, 1, :], small[:, 2, :], small[:, 3, :]
    made, biased, peaked = m.sig("attn_products"), m.sig("attn_biased"), m.sig("attn_peaks")
    exped, inverted, normed = m.sig("attn_exps"), m.sig("attn_inverted"), m.sig("attn_normed")
    turned, copied, out_made, out_copied = (m.sig("attn_turned"), m.sig("attn_turned_copied"),
                                            m.sig("attn_outputs"), m.sig("attn_outputs_copied"))
    for j, (t0, n) in enumerate(TILES):
        N = t0 + n
        base = {s: s.n for s in (made, biased, peaked, exped, inverted, normed, turned, copied, out_made,
                                 out_copied)}
        groups = [(half, i) for half in range(2) for i in range(j + 1)]
        with m.block() as block:

            @block.tensor
            def _(pe):
                for h in range(H):
                    if h >= 4:
                        pe.wait_ge(biased.sem, base[biased] + h - 3)
                    made.on(pe.matmul(m.ps[0:n, h % 4, 0:N], proj[:, h, t0:t0 + n], proj[:, H + h, 0:N],
                                      start=True, stop=True))
                for g, (half, i) in enumerate(groups):
                    s0, sn = TILES[i]
                    if g >= 2:
                        pe.wait_ge(copied.sem, base[copied] + g - 1)
                    for h in range(4 * half, 4 * half + 4):
                        pe.wait_ge(normed.sem, base[normed] + h + 1)
                        mm = pe.transpose(m.ps[0:sn, 4 + g % 2, (h % 4) * P:(h % 4) * P + n],
                                          logits[0:n, h, s0:s0 + sn], m.ident[0:n, 0:n])
                    turned.on(mm)
                for half in range(2):
                    pe.wait_ge(copied.sem, base[copied] + (half + 1) * (j + 1))
                    for h in range(4 * half, 4 * half + 4):
                        for i in range(j + 1):
                            sn = TILES[i][1]
                            mm = pe.matmul(m.ps[:, 6 + half, (h % 4) * P:(h % 4) * P + n],
                                           v_tokens[0:sn, i, h * P:(h + 1) * P], turned_p[0:sn, i, h, 0:n],
                                           start=i == 0, stop=i == j)
                    out_made.on(mm)

            @block.vector
            def _(dve):
                for h in range(H):
                    dve.wait_ge(made.sem, base[made] + h + 1)
                    biased.on(dve.scalar_tensor_tensor(logits[0:n, h, 0:N], m.ps[0:n, h % 4, 0:N],
                                                       float(P) ** -0.5, bias[0:n, j, 0:N], ALU.mult, ALU.add))
                dve.wait_ge(biased.sem, biased.n)
                peaked.on(dve.tensor_reduce(small[0:n, 0, :], logits[0:n, :, 0:N], AX.X, ALU.max))
                dve.wait_ge(peaked.sem, peaked.n)
                peaked.on(dve.tensor_scalar(negated[0:n, :], small[0:n, 0, :], -1.0, None, ALU.mult))
                for half in range(2):
                    dve.wait_ge(exped.sem, base[exped] + 4 * half + 4)
                    inverted.on(dve.reciprocal(inverse[0:n, 4 * half:4 * half + 4],
                                               total[0:n, 4 * half:4 * half + 4]))
                    dve.wait_ge(inverted.sem, inverted.n)
                    for h in range(4 * half, 4 * half + 4):
                        normed.on(dve.tensor_scalar(logits[0:n, h, 0:N], logits[0:n, h, 0:N],
                                                    inverse[0:n, h:h + 1], None, ALU.mult))
                for half in range(2):
                    dve.wait_ge(out_made.sem, base[out_made] + half + 1)
                    out_copied.on(dve.tensor_copy(
                        o[:, 4 * half:4 * half + 4, t0:t0 + n],
                        m.ps[:, 6 + half, :].rearrange("p (h q) -> p h q", h=4)[:, :, 0:n]))

            @block.scalar
            def _(act):
                act.wait_ge(peaked.sem, base[peaked] + 2)
                for h in range(H):
                    exped.on(act.activation(logits[0:n, h, 0:N], logits[0:n, h, 0:N], ACT.Exp,
                                            bias=negated[0:n, h:h + 1], accum_out=total[0:n, h:h + 1]))
                for g, (half, i) in enumerate(groups):
                    sn = TILES[i][1]
                    act.wait_ge(turned.sem, base[turned] + g + 1)
                    copied.on(act.activation(
                        turned_p[0:sn, i, 4 * half:4 * half + 4, 0:n],
                        m.ps[0:sn, 4 + g % 2, :].rearrange("p (h q) -> p h q", h=4)[:, :, 0:n], ACT.Copy))


def decay_attention(m, name, q, k, b, T, v_tokens, v0, dv_chunks, out, out0):
    H = 4
    tiles = TILES[0:2] if T == SEQ else TILES
    L = len(LEVELS)
    diff_q, diff_k, exped = m.sig("decay_diff_later"), m.sig("decay_diff_earlier"), m.sig("decay_exps")
    q_made, k_made, paired, chosen = (m.sig("decayed_q"), m.sig("decayed_k"), m.sig("decay_pairs"),
                                      m.sig("decay_chosen"))
    cleared = m.sig("decay_cleared")
    with ExitStack() as scope:
        a = m.sb(f"{name}_a", [P, 2, H, P], ctx=scope)
        a_tail = m.sb(f"{name}_a_tail", [16, H, 16], ctx=scope)
        e = m.sb(f"{name}_e", [P, 2, H, T], ctx=scope)
        qe = m.sb(f"{name}_qe", [P, 2, H, T], ctx=scope)
        ke = m.sb(f"{name}_ke", [P, 2, H, T], ctx=scope)
        base = {s: s.n for s in (diff_q, diff_k, exped, q_made, k_made, paired, chosen)}

        def span(level):
            h = LEVELS[level]
            n = T if T % (2 * h) == 0 else SEQ
            v = b[:, :, 0:n].rearrange("p g (n a h) -> p g n a h", a=2, h=h)
            d = e[:, level % 2, :, 0:n].rearrange("p g (n a h) -> p g n a h", a=2, h=h)
            edge = v[:, :, :, 0, h - 1:h].broadcast_to([P, H, n // (2 * h), h])
            return n, v, d, edge

        with m.block() as block:

            @block.tensor
            def _(pe):
                for level in range(L + 1):
                    if level < L:
                        pe.wait_ge(q_made.sem, base[q_made] + level + 1)
                        pe.wait_ge(k_made.sem, base[k_made] + level + 1)
                        n, lhs, rhs = span(level)[0], ke[:, level % 2, :, :], qe[:, level % 2, :, :]
                    else:
                        n, lhs, rhs = T, k, q
                    if level >= 2:
                        pe.wait_ge(chosen.sem, base[chosen] + 3 * (level - 1))
                    for j, (t0, tn) in enumerate(tiles):
                        if t0 >= n:
                            continue
                        for h in range(H):
                            mm = pe.matmul(m.ps[0:tn, 4 * (level % 2) + j, h * tn:(h + 1) * tn],
                                           lhs[:, h, t0:t0 + tn], rhs[:, h, t0:t0 + tn], start=True, stop=True)
                    paired.on(mm)

            @block.vector
            def _(dve):
                def diff(level):
                    n, v, d, edge = span(level)
                    if level >= 2:
                        dve.wait_ge(q_made.sem, base[q_made] + level - 1)
                        dve.wait_ge(k_made.sem, base[k_made] + level - 1)
                    diff_q.on(dve.tensor_tensor(d[:, :, :, 1, :], v[:, :, :, 1, :], edge, ALU.subtract))

                def choose(level):
                    n = T if level == L else span(level)[0]
                    dve.wait_ge(paired.sem, base[paired] + level + 1)
                    if level == 0:
                        dve.wait_ge(cleared.sem, cleared.n + 2)
                    else:
                        dve.wait_ge(chosen.sem, base[chosen] + 3 * level)
                    for j in range(3):
                        if j < len(tiles) and tiles[j][0] < n:
                            tn = tiles[j][1]
                            dst = a[:, j, :, :] if j < 2 else a_tail[:, :, :]
                            mask = m.masks[0:tn, level:level + 1, 0:tn].broadcast_to([tn, H, tn])
                            src = m.ps[0:tn, 4 * (level % 2) + j, 0:H * tn].rearrange("p (h t) -> p h t", h=H)
                            chosen.on(dve.copy_predicated(dst, mask, src))
                        else:
                            chosen.on(dve.engine_nop())

                diff(0)
                for level in range(L):
                    if level + 1 < L:
                        diff(level + 1)
                    n = span(level)[0]
                    dve.wait_ge(exped.sem, base[exped] + level + 1)
                    if level >= 2:
                        dve.wait_ge(paired.sem, base[paired] + level - 1)
                    q_made.on(dve.tensor_tensor(qe[:, level % 2, :, 0:n], q[:, :, 0:n], e[:, level % 2, :, 0:n],
                                                ALU.mult))
                    if level >= 1:
                        choose(level - 1)
                choose(L - 1)
                choose(L)

            @block.gpsimd
            def _(pool):
                cleared.on(pool.memset(a[:, :, :, :], 0.0))
                cleared.on(pool.memset(a_tail[:, :, :], 0.0))

                def diff(level):
                    n, v, d, edge = span(level)
                    if level >= 2:
                        pool.wait_ge(q_made.sem, base[q_made] + level - 1)
                        pool.wait_ge(k_made.sem, base[k_made] + level - 1)
                    diff_k.on(pool.tensor_tensor(d[:, :, :, 0, :], edge, v[:, :, :, 0, :], ALU.subtract))

                diff(0)
                for level in range(L):
                    if level + 1 < L:
                        diff(level + 1)
                    n = span(level)[0]
                    pool.wait_ge(exped.sem, base[exped] + level + 1)
                    if level >= 2:
                        pool.wait_ge(paired.sem, base[paired] + level - 1)
                    k_made.on(pool.tensor_tensor(ke[:, level % 2, :, 0:n], k[:, :, 0:n], e[:, level % 2, :, 0:n],
                                                 ALU.mult))
                pool.wait_ge(k_made.sem, k_made.n)

            @block.scalar
            def _(act):
                for level in range(L):
                    n = span(level)[0]
                    act.wait_ge(diff_q.sem, base[diff_q] + level + 1)
                    act.wait_ge(diff_k.sem, base[diff_k] + level + 1)
                    exped.on(act.activation(e[:, level % 2, :, 0:n], e[:, level % 2, :, 0:n], ACT.Exp))

        a_next = m.sb(f"{name}_a_next", [P, H, P], ctx=scope)
        a_last = m.sb(f"{name}_a_last", [P, 2, H, 16], ctx=scope)
        kx, qx, kx_far = ke[:, 0, :, :], qe[:, 0, :, :], ke[:, 1, :, 0:P]
        far = m.sb(f"{name}_far", [P, H], ctx=scope)
        n_early = P * (len(tiles) - 1)
        n_late = T - P
        three = len(tiles) == 3
        base = {s: s.n for s in (exped, q_made, k_made, paired, chosen)}
        with m.block() as block:

            @block.scalar
            def _(act):
                exped.on(act.activation(e[:, 1, :, 0:n_late], b[:, :, P:T], ACT.Exp))
                for i in range(len(tiles) - 1):
                    for h in range(H):
                        exped.on(act.activation(e[:, 0, h, i * P:(i + 1) * P], b[:, h, i * P:(i + 1) * P], ACT.Exp,
                                                bias=b[:, h, (i + 1) * P - 1:(i + 1) * P], scale=-1.0))
                if three:
                    exped.on(act.activation(far[:, :], b[:, :, 2 * P - 1], ACT.Exp))

            @block.vector
            def _(dve):
                dve.wait_ge(exped.sem, base[exped] + 1)
                q_made.on(dve.tensor_tensor(qx[:, :, 0:n_late], q[:, :, P:T], e[:, 1, :, 0:n_late], ALU.mult))
                dve.wait_ge(exped.sem, base[exped] + 1 + H * (len(tiles) - 1) + three)
                k_made.on(dve.tensor_tensor(kx[:, :, 0:n_early], k[:, :, 0:n_early], e[:, 0, :, 0:n_early], ALU.mult))
                if three:
                    dve.wait_ge(k_made.sem, k_made.n)
                    k_made.on(dve.tensor_tensor(kx_far, kx[:, :, 0:P],
                                                far[:, :].rearrange("p (h a) -> p h a", a=1).broadcast_to([P, H, P]),
                                                ALU.mult))
                dve.wait_ge(paired.sem, base[paired] + 1)
                chosen.on(dve.tensor_copy(a_next[:, :, :].rearrange("p h t -> p (h t)"), m.ps[:, 0, :]))
                if three:
                    chosen.on(dve.tensor_copy(a_last[:, :, :, :].rearrange("p i h t -> p (i h t)"),
                                              m.ps[:, 1, 0:2 * H * 16]))
                for g in range(len(tiles) * dv_chunks):
                    j, c = g // dv_chunks, g % dv_chunks
                    t0, tn = tiles[j]
                    dve.wait_ge(paired.sem, base[paired] + 2 + g)
                    dst = out[:, out0:out0 + H * dv_chunks, t0:t0 + tn]
                    dst = dst.rearrange("p (h c) t -> p h c t", c=dv_chunks)[:, :, c, :]
                    chosen.on(dve.tensor_copy(dst, m.ps[:, 2 + g, 0:H * tn].rearrange("p (h t) -> p h t", h=H)))

            @block.tensor
            def _(pe):
                pe.wait_ge(q_made.sem, base[q_made] + 1)
                pe.wait_ge(k_made.sem, base[k_made] + 1 + three)
                for h in range(H):
                    mm = pe.matmul(m.ps[:, 0, h * P:(h + 1) * P], kx[:, h, 0:P], qx[:, h, 0:P], start=True, stop=True)
                if three:
                    for h in range(H):
                        pe.matmul(m.ps[:, 1, h * 16:(h + 1) * 16], kx_far[:, h, :], qx[:, h, P:P + 16],
                                  start=True, stop=True)
                        mm = pe.matmul(m.ps[:, 1, (H + h) * 16:(H + h + 1) * 16], kx[:, h, P:2 * P],
                                       qx[:, h, P:P + 16], start=True, stop=True)
                paired.on(mm)
                pe.wait_ge(chosen.sem, base[chosen] + 1 + three)
                for g in range(len(tiles) * dv_chunks):
                    j, c = g // dv_chunks, g % dv_chunks
                    tn = tiles[j][1]
                    for h in range(H):
                        for i in range(j + 1):
                            sn = tiles[i][1]
                            if i == j:
                                pairs = a[:, j, h, :] if j < 2 else a_tail[:, h, :]
                            else:
                                pairs = a_next[:, h, :] if j == 1 else a_last[:, i, h, :]
                            col = v0 + (h * dv_chunks + c) * P
                            mm = pe.matmul(m.ps[:, 2 + g, h * tn:(h + 1) * tn], v_tokens[0:sn, i, col:col + P],
                                           pairs, start=i == 0, stop=i == j)
                    paired.on(mm)


def gla(m, dram, proj, gates, v_tokens, scope):
    H = GLA_HEADS
    b = m.sb("gla_log_decay", [P, H, T1], ctx=scope)
    steps, made, logs = m.sig("gla_steps"), m.sig("gla_gate_logits"), m.sig("gla_logs")
    base = {s: s.n for s in (steps, made, logs)}
    bias = column(m, "b_gate")
    with ExitStack() as inner:
        up = m.sb("gla_gate_up", [16, H * P], ctx=inner)
        size = m.sb("gla_gate_size", [P, H, T1], ctx=inner)
        loaded = m.sig("gla_gate_up_loaded")
        with m.block() as block:

            @block.sync
            def _(sp):
                loaded.on(sp.dma_start(up[:, :], dram["w_gate_up"][0]), 16)

            @block.tensor
            def _(pe):
                pe.wait_ge(loaded.sem, 16)
                for h in range(H):
                    made.on(pe.matmul(m.ps[:, h, 0:T1], up[:, h * P:(h + 1) * P], proj[0:16, 16, :],
                                      start=True, stop=True))

            @block.vector
            def _(dve):
                for h in range(H):
                    dve.wait_ge(made.sem, base[made] + h + 1)
                    steps.on(dve.tensor_scalar(b[:, h, :], m.ps[:, h, 0:T1], bias[:, h:h + 1], None, ALU.add))
                dve.wait_ge(steps.sem, base[steps] + 4)
                steps.on(dve.scalar_tensor_tensor(size[:, :, :], b[:, :, :], -1.0, b[:, :, :], ALU.mult, ALU.max))
                dve.wait_ge(logs.sem, base[logs] + 2)
                steps.on(dve.scalar_tensor_tensor(b[:, :, :], b[:, :, :], 0.0, size[:, :, :], ALU.min, ALU.subtract))
                dve.wait_ge(steps.sem, base[steps] + 6)
                steps.on(dve.tensor_scalar(b[:, :, :], b[:, :, :], 1.0 / GLA_TAU, None, ALU.mult))
                dve.wait_ge(steps.sem, base[steps] + 7)
                steps.on(dve.tensor_scalar(proj[:, 0:H, :], proj[:, 0:H, :], float(P) ** -0.5, None, ALU.mult))
                running_sums(dve, m, b, H, TILES, steps)

            @block.scalar
            def _(act):
                act.wait_ge(steps.sem, base[steps] + 5)
                logs.on(act.activation(size[:, :, :], size[:, :, :], ACT.Exp, scale=-1.0))
                act.wait_ge(logs.sem, base[logs] + 1)
                logs.on(act.activation(size[:, :, :], size[:, :, :], ACT.Ln, bias=1.0))
    decay_attention(m, "gla", proj[:, 0:H, :], proj[:, H:2 * H, :], b, T1, v_tokens, 0, 2, proj, 8)


def running_sums(dve, m, b, heads, tiles, steps):
    for h in range(heads):
        for t0, n in tiles:
            steps.on(dve.tensor_tensor_scan(b[:, h, t0:t0 + n], m.ones[:, 0:n], b[:, h, t0:t0 + n], 0.0,
                                            ALU.mult, ALU.add))


def norm_heads(m, name, o, o0, chunks, per_head, reducer, eps, T, gain, per_head_gain, gates, gate0, t0=0):
    squared, summed, scaled = m.sig("head_squares"), m.sig("head_sums"), m.sig("head_norm_steps")
    rooted, gated = m.sig("head_roots"), m.sig("head_gates")
    base = {s: s.n for s in (squared, summed, scaled, rooted, gated)}
    heads = chunks // per_head
    o = o[:, o0:o0 + chunks, 0:T]
    with ExitStack() as scope:
        sq = m.sb(f"{name}_head_squares", [P, chunks, T], ctx=scope)
        inv = m.sb(f"{name}_head_rstd", [P, heads, T], ctx=scope)
        with m.block() as block:

            @block.scalar
            def _(act):
                squared.on(act.activation(sq[:, :, :], o, ACT.Square))
                gated.on(act.activation(gates[:, gate0:gate0 + chunks, 0:T], gates[:, gate0:gate0 + chunks, 0:T],
                                        ACT.Silu))
                act.wait_ge(scaled.sem, base[scaled] + heads)
                rooted.on(act.activation(inv[:, :, :], inv[:, :, :], ACT.Sqrt))

            @block.tensor
            def _(pe):
                pe.wait_ge(squared.sem, base[squared] + 1)
                for h in range(heads):
                    for c in range(per_head):
                        mm = pe.matmul(m.ps[:, h, 0:T], reducer, sq[:, h * per_head + c, :], start=c == 0,
                                       stop=c == per_head - 1)
                    summed.on(mm)

            @block.vector
            def _(dve):
                for h in range(heads):
                    dve.wait_ge(summed.sem, base[summed] + h + 1)
                    scaled.on(dve.tensor_scalar(inv[:, h, :], m.ps[:, h, 0:T], 1.0 / (per_head * P), eps,
                                                ALU.mult, ALU.add))
                dve.wait_ge(rooted.sem, base[rooted] + 1)
                scaled.on(dve.reciprocal(inv[:, :, :], inv[:, :, :]))
                dve.wait_ge(scaled.sem, scaled.n)
                for c in range(chunks):
                    g = gain[:, c % per_head:c % per_head + 1] if per_head_gain else gain[:, c:c + 1]
                    scaled.on(dve.scalar_tensor_tensor(o[:, c, :], o[:, c, :], g, inv[:, c // per_head, :],
                                                       ALU.mult, ALU.mult))
                dve.wait_ge(gated.sem, base[gated] + 1)
                dve.wait_ge(scaled.sem, scaled.n)
                scaled.on(dve.tensor_tensor(o, o, gates[:, gate0:gate0 + chunks, 0:T], ALU.mult))


D_RWKV = D // 2
PAIRS = D_RWKV // P
HEAD = 64
CHUNK = 64
RANK = 64
GN_EPS = 64e-5
RMS_EPS = 1e-5
LN_EPS = 1e-5
LB_FLOOR = 1e-30
ALPHA = 2.0 ** 0.25
DECAY = float(np.exp(-0.5))
STEPS = [level for level in reversed(range(len(LEVELS))) if 2 * LEVELS[level] <= CHUNK]


def lane(e):
    return slice(e * HEAD, (e + 1) * HEAD)


class Masks64:

    def __init__(self, m, scope):
        n = len(STEPS)
        self.all = m.sb("masks64", [P, n + 3, CHUNK], ctx=scope)
        self.heads = m.sb("same_head", [P, P], ctx=scope)
        made, filled = m.sig("masks64_made"), m.sig("same_head_made")
        with m.block() as block:

            @block.vector
            def _(dve):
                for x, level in enumerate(STEPS + [None, None, len(LEVELS)]):
                    if level is None:
                        continue
                    for e in range(2):
                        made.on(dve.tensor_copy(self.all[lane(e), x, :], m.masks[lane(e), level, lane(e)]))

            @block.gpsimd
            def _(pool):
                filled.on(pool.memset(self.all[:, n:n + 2, :], 1.0))
                filled.on(pool.memset(self.heads[:, :], 0.0))
                pool.wait_ge(filled.sem, filled.n)
                filled.on(pool.memset(self.heads[lane(0), lane(0)], 1.0))
                filled.on(pool.memset(self.heads[lane(1), lane(1)], 1.0))
                pool.wait_ge(filled.sem, filled.n)
                for e in range(2):
                    for x, bound in ((n, -1), (n + 1, 0)):
                        view = self.all[lane(e), x, :]
                        filled.on(pool.affine_select(out=view, in_=view, compare_op=ALU.is_ge, fill=0.0, base=bound,
                                                     pattern=[[1, CHUNK]], channel_multiplier=-1))
                pool.wait_ge(filled.sem, filled.n)
        self.strict, self.causal, self.equal = n, n + 1, n + 2

    def wide(self, x):
        return self.all[:, x:x + 1, :].broadcast_to([P, PAIRS, CHUNK])


def token_shift(m, y, tiles, mu):
    differed, shifted = m.sig("shift_differences"), m.sig("shifted")
    base, d0 = shifted.n, differed.n
    with ExitStack() as scope:
        d = m.sb("shift_d", [P, 8, SEQ], ctx=scope)
        with m.block() as block:

            @block.gpsimd
            def _(pool):
                for c in range(tiles):
                    if c >= 8:
                        pool.wait_ge(shifted.sem, base + c - 7)
                    differed.on(pool.tensor_tensor(d[:, c % 8, 1:SEQ], y[:, c, 0:SEQ - 1], y[:, c, 1:SEQ],
                                                   ALU.subtract))
                    differed.on(pool.tensor_scalar(d[:, c % 8, 0:1], y[:, c, 0:1], -1.0, None, ALU.mult))
                pool.wait_ge(differed.sem, differed.n)

            @block.vector
            def _(dve):
                for c in range(tiles):
                    dve.wait_ge(differed.sem, d0 + 2 * c + 2)
                    shifted.on(dve.scalar_tensor_tensor(y[:, c, :], d[:, c % 8, :], mu[:, c:c + 1], y[:, c, :],
                                                        ALU.mult, ALU.add))


def head_sums(pe, m, reducer, x, first_bank, summed):
    for g in range(PAIRS // 2):
        summed.on(pe.matmul(m.ps[:, first_bank + g, :], reducer, x[:, 2 * g:2 * g + 2, :], start=True, stop=True))


def sums_view(m, first_bank):
    return m.ps[:, first_bank:first_bank + PAIRS // 2, :]


def halves(x):
    return x.rearrange("p (g a) t -> p g (a t)", a=2)


def wide_column(col):
    return col.rearrange("p (c a) -> p c a", a=1).broadcast_to([P, PAIRS, SEQ])


def rwkv_vectors(m, dram, proj, masks, sums, alpha, beta, bonus, tmp):
    col = {n: column(m, n + "_2") for n in ("w_decay0", "a0", "k_k", "k_a", "r_k")}
    loaded, tanhed = m.sig("lora_loaded"), m.sig("lora_tanh")
    made, gated, steps = m.sig("lora_made"), m.sig("rwkv_gates"), m.sig("rwkv_steps")
    summed, act_steps = m.sig("rwkv_head_sums"), m.sig("rwkv_act_steps")
    r, k, v = proj[:, 0:PAIRS, :], proj[:, PAIRS:2 * PAIRS, :], proj[:, 2 * PAIRS:3 * PAIRS, :]
    with ExitStack() as scope:
        up = m.sb("lora_up", [P, D_RWKV], ctx=scope)
        small = m.sb("rwkv_small", [P, PAIRS], ctx=scope)
        base = {s: s.n for s in (made, gated, steps, summed, act_steps)}
        with m.block() as block:

            @block.sync
            def _(sp):
                loaded.on(sp.dma_start(up[lane(0), :], dram["w_decay_up_2"][0]), 16)
                loaded.on(sp.dma_start(up[lane(1), :], dram["a_up_2"][0]), 16)

            @block.scalar
            def _(act):
                tanhed.on(act.activation(proj[lane(0), 32, :], proj[lane(0), 32, :], ACT.Tanh))
                for x in range(2 * PAIRS):
                    c, dst, bias = x // 2, (sums, beta)[x % 2], (col["w_decay0"], col["a0"])[x % 2]
                    act.wait_ge(made.sem, base[made] + x + 1)
                    gated.on(act.activation(dst[:, c, :], m.ps[:, x % 4, 0:SEQ], ACT.Sigmoid, bias=bias[:, c:c + 1]))

            @block.tensor
            def _(pe):
                pe.wait_ge(loaded.sem, loaded.n)
                pe.wait_ge(tanhed.sem, tanhed.n)
                for x in range(2 * PAIRS):
                    c, e = x // 2, x % 2
                    if x >= 4:
                        pe.wait_ge(gated.sem, base[gated] + x - 3)
                    made.on(pe.matmul(m.ps[:, x % 4, 0:SEQ], up[lane(e), c * P:(c + 1) * P], proj[lane(e), 32, :],
                                      start=True, stop=True))

            @block.vector
            def _(dve):
                steps.on(dve.tensor_tensor(alpha[:, :, :], k, wide_column(col["k_k"]), ALU.mult))
                dve.wait_ge(steps.sem, base[steps] + 1)
                steps.on(dve.tensor_tensor(tmp[:, :, :], alpha[:, :, :], alpha[:, :, :], ALU.mult))
                steps.on(dve.tensor_scalar(small[:, :], col["k_a"], -1.0, 1.0, ALU.mult, ALU.add))

        base = {s: s.n for s in (steps, summed, act_steps)}
        with m.block() as block:

            @block.tensor
            def _(pe):
                head_sums(pe, m, masks.heads[:, :], tmp, 0, summed)
                pe.wait_ge(steps.sem, base[steps] + 5)
                head_sums(pe, m, masks.heads[:, :], bonus, 4, summed)

            @block.scalar
            def _(act):
                act.wait_ge(summed.sem, base[summed] + 4)
                act_steps.on(act.activation(halves(tmp[:, :, :]), sums_view(m, 0), ACT.Sqrt))

            @block.vector
            def _(dve):
                def step(ins):
                    steps.on(ins)
                    dve.wait_ge(steps.sem, steps.n)

                step(dve.tensor_tensor(bonus[:, :, :], beta[:, :, :], wide_column(col["k_a"]), ALU.mult))
                step(dve.tensor_tensor(bonus[:, :, :], bonus[:, :, :], wide_column(small[:, :]), ALU.add))
                step(dve.tensor_tensor(k, k, bonus[:, :, :], ALU.mult))
                step(dve.tensor_tensor(bonus[:, :, :], r, k, ALU.mult))
                step(dve.tensor_tensor(bonus[:, :, :], bonus[:, :, :], wide_column(col["r_k"]), ALU.mult))
                dve.wait_ge(act_steps.sem, base[act_steps] + 1)
                step(dve.tensor_scalar(tmp[:, :, :], tmp[:, :, :], 1e-12, None, ALU.max))
                step(dve.reciprocal(tmp[:, :, :], tmp[:, :, :]))
                step(dve.tensor_tensor(alpha[:, :, :], alpha[:, :, :], tmp[:, :, :], ALU.mult))
                step(dve.tensor_tensor(beta[:, :, :], beta[:, :, :], alpha[:, :, :], ALU.mult))


def rwkv_decays(m, proj, sums, alpha, beta, bonus, tmp, last):
    steps, act_steps = m.sig("rwkv_steps"), m.sig("rwkv_act_steps")
    r, k, v = proj[:, 0:PAIRS, :], proj[:, PAIRS:2 * PAIRS, :], proj[:, 2 * PAIRS:3 * PAIRS, :]
    base = {s: s.n for s in (steps, act_steps)}
    with m.block() as block:

        @block.vector
        def _(dve):
            steps.on(dve.tensor_copy(tmp[:, :, :], sums[:, :, :]))
            dve.wait_ge(steps.sem, steps.n)
            running_sums(dve, m, sums, PAIRS, [(t, CHUNK) for t in range(0, SEQ, CHUNK)], steps)
            dve.wait_ge(steps.sem, steps.n)
            steps.on(dve.tensor_tensor(tmp[:, :, :], sums[:, :, :], tmp[:, :, :], ALU.subtract))
            exclusive = steps.n
            steps.on(dve.tensor_tensor(halves(bonus[:, :, :]), halves(v), sums_view(m, 4), ALU.mult))
            dve.wait_ge(act_steps.sem, base[act_steps] + 1)
            steps.on(dve.scalar_tensor_tensor(alpha[:, :, :], alpha[:, :, :], -1.0, tmp[:, :, :], ALU.mult, ALU.mult))
            used_alpha = steps.n
            dve.wait_ge(act_steps.sem, base[act_steps] + 2)
            steps.on(dve.tensor_tensor(r, r, tmp[:, :, :], ALU.mult))
            used_r = steps.n
            dve.wait_ge(act_steps.sem, base[act_steps] + 4)
            steps.on(dve.tensor_tensor(k, k, tmp[:, :, :], ALU.mult))
            steps.on(dve.tensor_tensor(beta[:, :, :], beta[:, :, :], tmp[:, :, :], ALU.mult))
            m.marks = (exclusive, used_alpha, used_r)

        @block.scalar
        def _(act):
            exclusive, used_alpha, used_r = m.marks
            act.wait_ge(steps.sem, exclusive)
            act_steps.on(act.activation(tmp[:, :, :], tmp[:, :, :], ACT.Exp, scale=-DECAY))
            act.wait_ge(steps.sem, used_alpha)
            act_steps.on(act.activation(tmp[:, :, :], sums[:, :, :], ACT.Exp, scale=-DECAY))
            act_steps.on(act.activation(last[:, :, :], sums.rearrange("p a (c t) -> p a c t", t=CHUNK)[:, :, :, CHUNK - 1],
                                        ACT.Exp, scale=-DECAY))
            act.wait_ge(steps.sem, used_r)
            act_steps.on(act.activation(tmp[:, :, :], sums[:, :, :], ACT.Exp, scale=DECAY))


class Rwkv:

    def __init__(self, m, scope, proj, last, alpha, beta, masks, out):
        self.m, self.masks, self.last, self.out = m, masks, last, out
        self.r, self.k, self.v = (proj[:, a * PAIRS:(a + 1) * PAIRS, :] for a in range(3))
        self.alpha, self.beta = alpha, beta

        def tile(name, n=2):
            return m.sb(f"rwkv_{name}", [P, n, PAIRS, CHUNK], ctx=scope)

        self.tok = {name: tile(f"{name}_tokens") for name in ("beta", "k", "v")}
        self.lb, self.lk, self.mb, self.mk = (tile(x) for x in ("lb", "lk", "mb", "mk"))
        self.level, self.x, self.xt, self.y = (tile(x) for x in ("level", "x", "xt", "y"))
        self.rhs, self.sa, self.state = (tile(x, 1)[:, 0] for x in ("rhs", "sa", "state"))
        self.fresh = self.rhs

    def flat(self, x):
        return x.rearrange("p a b -> p (a b)")

    def bank(self, b):
        return self.m.ps[:, b, :].rearrange("p (a b) -> p a b", b=CHUNK)

    def heads(self, pe, bank, terms, signal):
        for pair in range(PAIRS):
            for e in range(2):
                for x, (lhs, rhs) in enumerate(terms):
                    mm = pe.matmul(self.bank(bank)[lane(e), pair, :], lhs(e, pair), rhs(e, pair), start=x == 0,
                                   stop=x == len(terms) - 1)
        return signal.on(mm)

    def prepare(self, first):
        m, masks = self.m, self.masks
        made, kept = m.sig("rwkv_products"), m.sig("rwkv_kept")
        copied = m.sig("rwkv_turned")
        ident = m.ident

        def part(x, c):
            t0 = (first + c) * CHUNK
            return lambda e, p: x[lane(e), p, t0:t0 + CHUNK]

        def held(x, c):
            return lambda e, p: x[lane(e), c, p, :]

        def unit(e, p):
            return ident[lane(e), lane(e)]

        jobs = []
        for c in range(2):
            jobs += [((part(self.beta, c), part(self.alpha, c)), self.lb[:, c], masks.strict),
                     ((part(self.k, c), part(self.alpha, c)), self.lk[:, c], masks.strict),
                     ((part(self.beta, c), part(self.r, c)), self.mb[:, c], masks.causal),
                     ((part(self.k, c), part(self.r, c)), self.mk[:, c], masks.causal),
                     ((part(self.beta, c), unit), self.tok["beta"][:, c], None),
                     ((part(self.k, c), unit), self.tok["k"][:, c], None),
                     ((part(self.v, c), unit), self.tok["v"][:, c], None)]
        masked = [x for x, job in enumerate(jobs) if job[2] is not None]
        plain = [x for x, job in enumerate(jobs) if job[2] is None]
        base = {s: s.n for s in (made, kept, copied)}
        with m.block() as block:

            @block.tensor
            def _(pe):
                for x, (term, _, mask) in enumerate(jobs):
                    if x >= 8:
                        if jobs[x - 8][2] is not None:
                            pe.wait_ge(kept.sem, base[kept] + masked.index(x - 8) + 1)
                        else:
                            pe.wait_ge(copied.sem, base[copied] + plain.index(x - 8) + 1)
                    self.heads(pe, x % 8, [term], made)

            @block.vector
            def _(dve):
                for x in masked:
                    dve.wait_ge(made.sem, base[made] + x + 1)
                    kept.on(dve.tensor_tensor(jobs[x][1], self.bank(x % 8), masks.wide(jobs[x][2]), ALU.mult))

            @block.scalar
            def _(act):
                for x in plain:
                    act.wait_ge(made.sem, base[made] + x + 1)
                    copied.on(act.activation(jobs[x][1], self.bank(x % 8), ACT.Copy))

        levelled, y_made, y_kept = m.sig("inverse_levels"), m.sig("inverse_y_made"), m.sig("inverse_y_kept")
        grown, x_kept = m.sig("inverse_grown"), m.sig("inverse_kept")
        base = {s: s.n for s in (levelled, y_made, y_kept, grown, x_kept)}
        last = len(STEPS) - 1
        with m.block() as block:

            @block.gpsimd
            def _(pool):
                for s in range(len(STEPS)):
                    for c in range(2):
                        if s >= 1:
                            pool.wait_ge(y_made.sem, base[y_made] + 2 * (s - 1) + c + 1)
                        if s == 1:
                            pool.wait_ge(x_kept.sem, base[x_kept] + 2 * c + 2)
                        levelled.on(pool.tensor_tensor(self.level[:, c], self.lb[:, c], masks.wide(s), ALU.mult))
                pool.wait_ge(levelled.sem, levelled.n)

            @block.tensor
            def _(pe):
                for s in range(len(STEPS)):
                    for c in range(2):
                        pe.wait_ge(levelled.sem, base[levelled] + 2 * s + c + 1)
                        rhs = unit if s == 0 else held(self.x, c)
                        if s >= 1:
                            pe.wait_ge(x_kept.sem, base[x_kept] + 4 * (s - 1) + 2 * c + 2)
                        self.heads(pe, c, [(held(self.level, c), rhs)], y_made)
                    if s == 0:
                        continue
                    for c in range(2):
                        pe.wait_ge(y_kept.sem, base[y_kept] + 2 * (s - 1) + c + 1)
                        if s < last:
                            self.heads(pe, 2 + 2 * c, [(held(self.xt, c), held(self.y, c))], grown)
                        self.heads(pe, 3 + 2 * c, [(held(self.y, c), held(self.xt, c))], grown)

            @block.scalar
            def _(act):
                for s in range(1, len(STEPS)):
                    for c in range(2):
                        act.wait_ge(y_made.sem, base[y_made] + 2 * s + c + 1)
                        y_kept.on(act.activation(self.y[:, c], self.bank(c), ACT.Copy))

            @block.vector
            def _(dve):
                for c in range(2):
                    dve.wait_ge(y_made.sem, base[y_made] + c + 1)
                    x_kept.on(dve.tensor_tensor(self.x[:, c], self.bank(c), masks.wide(masks.equal), ALU.add))
                    x_kept.on(dve.tensor_tensor(self.xt[:, c], self.level[:, c], masks.wide(masks.equal), ALU.add))
                n = base[grown]
                for s in range(1, len(STEPS)):
                    for c in range(2):
                        n += 1 if s == last else 2
                        dve.wait_ge(grown.sem, n)
                        if s < last:
                            x_kept.on(dve.tensor_tensor(self.x[:, c], self.bank(2 + 2 * c), self.x[:, c], ALU.add))
                        else:
                            x_kept.on(dve.engine_nop())
                        x_kept.on(dve.tensor_tensor(self.xt[:, c], self.bank(3 + 2 * c), self.xt[:, c], ALU.add))

    def scan(self, first):
        m = self.m
        made, kept, advanced = m.sig("scan_products"), m.sig("scan_kept"), m.sig("scan_states")
        stored = m.sig("scan_outputs")
        base = {s: s.n for s in (made, kept, advanced, stored)}

        def held(x, c):
            return lambda e, p: x[lane(e), c, p, :]

        def alone(x):
            return lambda e, p: x[lane(e), p, :]

        def part(x, c):
            t0 = (first + c) * CHUNK
            return lambda e, p: x[lane(e), p, t0:t0 + CHUNK]

        with m.block() as block:

            @block.tensor
            def _(pe):
                for c in range(2):
                    if c:
                        pe.wait_ge(advanced.sem, base[advanced] + 2 * c)
                    self.heads(pe, 0, [(part(self.alpha, c), alone(self.state)),
                                       (held(self.lk, c), held(self.tok["v"], c))], made)
                    pe.wait_ge(kept.sem, base[kept] + 2 * c + 1)
                    self.heads(pe, 1, [(held(self.xt, c), alone(self.rhs))], made)
                    pe.wait_ge(kept.sem, base[kept] + 2 * c + 2)
                    self.heads(pe, 2, [(held(self.tok["beta"], c), alone(self.sa)),
                                       (held(self.tok["k"], c), held(self.tok["v"], c))], made)
                    self.heads(pe, 3 + c, [(alone(self.state), part(self.r, c)),
                                           (alone(self.sa), held(self.mb, c)),
                                           (held(self.tok["v"], c), held(self.mk, c))], made)

            @block.scalar
            def _(act):
                for c in range(2):
                    act.wait_ge(made.sem, base[made] + 4 * c + 1)
                    kept.on(act.activation(self.rhs, self.bank(0), ACT.Copy))
                    act.wait_ge(made.sem, base[made] + 4 * c + 2)
                    kept.on(act.activation(self.sa, self.bank(1), ACT.Copy))
                    act.wait_ge(made.sem, base[made] + 4 * c + 4)
                    t0 = (first + c) * CHUNK
                    stored.on(act.activation(self.out[:, :, t0:t0 + CHUNK], self.bank(3 + c), ACT.Copy))

            @block.vector
            def _(dve):
                for c in range(2):
                    dve.wait_ge(made.sem, base[made] + 4 * c + 3)
                    advanced.on(dve.tensor_tensor(self.fresh, self.bank(2), self.state, ALU.add))
                    dve.wait_ge(advanced.sem, base[advanced] + 2 * c + 1)
                    dve.wait_ge(made.sem, base[made] + 4 * c + 4)
                    decay = self.last[:, :, first + c:first + c + 1].broadcast_to([P, PAIRS, CHUNK])
                    advanced.on(dve.tensor_tensor(self.state, self.fresh, decay, ALU.mult))

    def start(self):
        m = self.m
        cleared = m.sig("state_cleared")
        with m.block() as block:

            @block.vector
            def _(dve):
                cleared.on(dve.memset(self.state, 0.0))


def rwkv_finish(m, masks, o, bonus, z, out):
    gn_w, gn_b = column(m, "ln_x_w_2"), column(m, "ln_x_b_2")
    summed, steps, act_steps = m.sig("rwkv_head_sums"), m.sig("rwkv_steps"), m.sig("rwkv_act_steps")
    base = {s: s.n for s in (summed, steps, act_steps)}
    with ExitStack() as scope:
        sq = m.sb("gn_squares", [P, PAIRS, SEQ], ctx=scope)
        with m.block() as block:

            @block.tensor
            def _(pe):
                head_sums(pe, m, masks.heads[:, :], o, 0, summed)
                pe.wait_ge(act_steps.sem, base[act_steps] + 2)
                head_sums(pe, m, masks.heads[:, :], sq, 4, summed)

            @block.scalar
            def _(act):
                act_steps.on(act.activation(z, z, ACT.Silu))
                act.wait_ge(steps.sem, base[steps] + 1)
                act_steps.on(act.activation(sq[:, :, :], o, ACT.Square))
                act.wait_ge(steps.sem, base[steps] + 2)
                act_steps.on(act.activation(sq[:, :, :], sq[:, :, :], ACT.Sqrt))

            @block.vector
            def _(dve):
                dve.wait_ge(summed.sem, base[summed] + 4)
                steps.on(dve.scalar_tensor_tensor(halves(o), sums_view(m, 0), -1.0 / HEAD, halves(o), ALU.mult,
                                                  ALU.add))
                dve.wait_ge(summed.sem, base[summed] + 8)
                steps.on(dve.tensor_scalar(halves(sq[:, :, :]), sums_view(m, 4), 1.0 / HEAD, GN_EPS, ALU.mult,
                                           ALU.add))
                dve.wait_ge(act_steps.sem, base[act_steps] + 3)
                steps.on(dve.reciprocal(sq[:, :, :], sq[:, :, :]))
                dve.wait_ge(steps.sem, steps.n)
                for c in range(PAIRS):
                    steps.on(dve.scalar_tensor_tensor(o[:, c, :], o[:, c, :], gn_w[:, c:c + 1], sq[:, c, :],
                                                      ALU.mult, ALU.mult))
                for c in range(PAIRS):
                    dve.wait_ge(steps.sem, base[steps] + 3 + c + 1)
                    steps.on(dve.scalar_tensor_tensor(o[:, c, :], o[:, c, :], gn_b[:, c:c + 1], bonus[:, c, :],
                                                      ALU.add, ALU.add))
                dve.wait_ge(steps.sem, steps.n)
                steps.on(dve.tensor_tensor(out, o, z, ALU.mult))


def hgrn_gates(m, proj, b, scope):
    logits = column(m, "lb_logits_2")
    steps, act_steps = m.sig("hgrn_steps"), m.sig("hgrn_act_steps")
    f = proj[:, 8:16, :]
    with ExitStack() as inner:
        bound = m.sb("hgrn_bound", [P, 6, PAIRS], ctx=inner)
        size = m.sb("hgrn_size", [P, PAIRS, SEQ], ctx=inner)
        share, lower, log_lower, log_rest, rest = (bound[:, x, :] for x in range(5))
        marks = {}
        with m.block() as block:

            @block.vector
            def _(dve):
                def step(ins, name=None):
                    steps.on(ins)
                    marks[name] = steps.n

                def settled():
                    dve.wait_ge(steps.sem, steps.n)

                def after(n):
                    dve.wait_ge(act_steps.sem, n)

                step(dve.tensor_tensor(share, logits, logits, ALU.subtract), "centred")
                step(dve.scalar_tensor_tensor(size[:, :, :], f, -1.0, f, ALU.mult, ALU.max), "size")
                after(1)
                step(dve.reciprocal(lower, share))
                settled()
                step(dve.tensor_tensor(share, share, lower, ALU.mult))
                settled()
                step(dve.tensor_tensor(lower, share, share, ALU.subtract))
                settled()
                step(dve.tensor_scalar(rest, lower, -1.0, 1.0, ALU.mult, ALU.add))
                step(dve.tensor_scalar(log_lower, lower, LB_FLOOR, None, ALU.max), "floored")
                after(3)
                step(dve.tensor_scalar(log_lower, log_lower, -60.0 * float(np.log(2.0)), None, ALU.add))
                after(5)
                step(dve.scalar_tensor_tensor(b, f, 0.0, size[:, :, :], ALU.min, ALU.subtract))
                settled()
                step(dve.tensor_tensor(b, b, wide_column(log_rest), ALU.add))
                settled()
                step(dve.tensor_tensor(size[:, :, :], b, wide_column(log_lower), ALU.subtract))
                settled()
                step(dve.scalar_tensor_tensor(size[:, :, :], size[:, :, :], -1.0, size[:, :, :], ALU.mult, ALU.min),
                     "difference")
                step(dve.tensor_tensor(b, b, wide_column(log_lower), ALU.max))
                settled()
                after(7)
                step(dve.tensor_tensor(b, b, size[:, :, :], ALU.add))
                settled()
                running_sums(dve, m, b, PAIRS, TILES[0:2], steps)
                after(8)
                step(dve.tensor_tensor(f, f, wide_column(rest), ALU.mult))

            @block.scalar
            def _(act):
                def step(ins):
                    act_steps.on(ins)

                act.wait_ge(steps.sem, marks["centred"])
                step(act.activation(share, share, ACT.Exp))
                act.wait_ge(steps.sem, marks["size"])
                step(act.activation(size[:, :, :], size[:, :, :], ACT.Exp, scale=-1.0))
                act.wait_ge(steps.sem, marks["floored"])
                step(act.activation(log_lower, log_lower, ACT.Ln, scale=2.0 ** 60))
                step(act.activation(log_rest, rest, ACT.Ln))
                act.wait_ge(act_steps.sem, 2)
                step(act.activation(size[:, :, :], size[:, :, :], ACT.Ln, bias=1.0))
                act.wait_ge(steps.sem, marks["difference"])
                step(act.activation(size[:, :, :], size[:, :, :], ACT.Exp))
                act.wait_ge(act_steps.sem, 6)
                step(act.activation(size[:, :, :], size[:, :, :], ACT.Ln, bias=1.0))
                step(act.activation(f, f, ACT.Sigmoid, scale=-1.0))
                step(act.activation(proj[:, 0:8, :], proj[:, 0:8, :], ACT.Silu))


def layer_norm_out(m, y, out):
    w, b = column(m, "ln_w_2"), column(m, "ln_b_2")
    added, squared, summed = m.sig("ln_added"), m.sig("ln_squared"), m.sig("ln_sums")
    steps, rooted, normed, biased = m.sig("ln_steps"), m.sig("ln_rooted"), m.sig("ln_normed"), m.sig("ln_biased")
    turned, copied, stored = m.sig("out_turned"), m.sig("out_copied"), m.sig("stored")
    centred = m.sig("ln_centred")
    T = SEQ
    with ExitStack() as scope:
        sq = m.sb("ln_squares", [P, DC, T], ctx=scope)
        stats = m.sb("ln_stats", [P, 2, T], ctx=scope)
        mean, rstd = stats[:, 0, :], stats[:, 1, :]
        with m.block() as block:

            @block.vector
            def _(dve):
                for c in range(DC):
                    added.on(dve.scalar_tensor_tensor(y[:, c, :], m.r[:, c, N_META:T1], ALPHA, y[:, c, :], ALU.mult,
                                                      ALU.add))
                dve.wait_ge(summed.sem, 1)
                steps.on(dve.tensor_scalar(mean, m.ps[:, 6, 0:T], 1.0 / D, None, ALU.mult))
                dve.wait_ge(steps.sem, 1)
                for c in range(0, DC, 4):
                    centred.on(dve.tensor_tensor(y[:, c:c + 4, :], y[:, c:c + 4, :],
                                                 stats[:, 0:1, :].broadcast_to([P, 4, T]), ALU.subtract))
                dve.wait_ge(summed.sem, 2)
                steps.on(dve.tensor_scalar(rstd, m.ps[:, 7, 0:T], 1.0 / D, LN_EPS, ALU.mult, ALU.add))
                dve.wait_ge(rooted.sem, 1)
                steps.on(dve.reciprocal(rstd, rstd))
                dve.wait_ge(steps.sem, 3)
                for c in range(DC):
                    normed.on(dve.scalar_tensor_tensor(y[:, c, :], y[:, c, :], w[:, c:c + 1], rstd, ALU.mult,
                                                       ALU.mult))

            @block.scalar
            def _(act):
                for c in range(0, DC, 4):
                    act.wait_ge(centred.sem, c // 4 + 1)
                    squared.on(act.activation(sq[:, c:c + 4, :], y[:, c:c + 4, :], ACT.Square))
                act.wait_ge(steps.sem, 2)
                rooted.on(act.activation(rstd, rstd, ACT.Sqrt))
                for c in range(DC):
                    act.wait_ge(normed.sem, c + 1)
                    biased.on(act.activation(y[:, c, :], y[:, c, :], ACT.Identity, bias=b[:, c:c + 1]))

            @block.tensor
            def _(pe):
                for c in range(DC):
                    pe.wait_ge(added.sem, c + 1)
                    mm = pe.matmul(m.ps[:, 6, 0:T], m.ones[:, :], y[:, c, :], start=c == 0, stop=c == DC - 1)
                summed.on(mm)
                for c in range(DC):
                    if c % 4 == 0:
                        pe.wait_ge(squared.sem, c // 4 + 1)
                    mm = pe.matmul(m.ps[:, 7, 0:T], m.ones[:, :], sq[:, c, :], start=c == 0, stop=c == DC - 1)
                summed.on(mm)

        rows = sq[:, :, :].rearrange("p (j a) t -> p j (a t)", j=2)
        with m.block() as block:

            @block.tensor
            def _(pe):
                for g in range(8):
                    j, c0 = g % 2, 4 * (g // 2)
                    for c in range(4):
                        mm = pe.transpose(m.ps[:, g, c * P:(c + 1) * P], y[:, c0 + c, j * P:(j + 1) * P],
                                          m.ident[:, :])
                    turned.on(mm)

            @block.vector
            def _(dve):
                for g in range(8):
                    j, c0 = g % 2, 4 * (g // 2)
                    dve.wait_ge(turned.sem, g + 1)
                    copied.on(dve.tensor_copy(rows[:, j, c0 * P:(c0 + 4) * P], m.ps[:, g, :]))

            @block.sync
            def _(sp):
                for g in range(8):
                    j, c0 = g % 2, 4 * (g // 2)
                    sp.wait_ge(copied.sem, g + 1)
                    stored.on(sp.dma_start(out[0, j * P:(j + 1) * P, c0 * P:(c0 + 4) * P],
                                           rows[:, j, c0 * P:(c0 + 4) * P]), 16)
                sp.wait_ge(stored.sem, stored.n)


def split_features(m, name, source, T, gain=None, scale=None):
    made, high, low = m.sig("x_scaled"), m.sig("x_high"), m.sig("x_low")
    made0, high0 = made.n, high.n
    with ExitStack() as scope:
        tmp = m.sb(f"{name}_scaled", [P, 4, T1], ctx=scope) if gain is not None else None
        low0 = low.n

        def value(c):
            return tmp[:, c % 4, 0:T] if gain is not None else source(c)

        with m.block() as block:
            if gain is not None:

                @block.vector
                def _(dve):
                    for c in range(DC):
                        if c >= 4:
                            dve.wait_ge(low.sem, low0 + c - 3)
                        made.on(dve.scalar_tensor_tensor(tmp[:, c % 4, 0:T], source(c), gain[:, c:c + 1],
                                                         scale[:, 0:T], ALU.mult, ALU.mult))

            @block.scalar
            def _(act):
                for c in range(DC):
                    if gain is not None:
                        act.wait_ge(made.sem, made0 + c + 1)
                    high.on(act.activation(m.x_hi[:, c, 0:T], value(c), ACT.Copy))

            @block.gpsimd
            def _(pool):
                for c in range(DC):
                    pool.wait_ge(high.sem, high0 + c + 1)
                    low.on(pool.tensor_tensor(m.x_lo[:, c, 0:T], value(c),
                                              m.x_hi[:, c, 0:T].bitcast(F32), ALU.subtract))
                pool.wait_ge(low.sem, low.n)


def rms_scale(m, name, source, T, rstd, chunks=DC, eps=EPS):
    squared, summed, scaled = m.sig("squares"), m.sig("square_sums"), m.sig("norm_steps")
    squared0, summed0 = squared.n, summed.n
    total = m.ps[:, 7, 0:T]
    with ExitStack() as scope:
        sq = m.sb(f"{name}_squares", [P, chunks, T1], ctx=scope)
        with m.block() as block:

            @block.scalar
            def _(act):
                for c in range(0, chunks, 4):
                    squared.on(act.activation(sq[:, c:c + 4, 0:T], source[:, c:c + 4, :], ACT.Square))
                act.wait_ge(scaled.sem, scaled.n + 1)
                m.sig("norm_roots").on(act.activation(rstd[:, 0:T], rstd[:, 0:T], ACT.Sqrt))

            @block.tensor
            def _(pe):
                for c in range(chunks):
                    if c % 4 == 0:
                        pe.wait_ge(squared.sem, squared0 + c // 4 + 1)
                    mm = pe.matmul(total, m.ones[:, :], sq[:, c, 0:T], start=c == 0, stop=c == chunks - 1)
                summed.on(mm)

            @block.vector
            def _(dve):
                dve.wait_ge(summed.sem, summed0 + 1)
                scaled.on(dve.tensor_scalar(rstd[:, 0:T], total, 1.0 / (chunks * P), eps, ALU.mult, ALU.add))
                dve.wait_ge(m.sig("norm_roots").sem, m.sig("norm_roots").n)
                scaled.on(dve.reciprocal(rstd[:, 0:T], rstd[:, 0:T]))


def add_normed(m, y, T, gain, rstd, residual):
    made, added = m.sig("update_scaled"), m.sig("residual_added")
    made0 = made.n
    with m.block() as block:

        @block.vector
        def _(dve):
            for c in range(DC):
                made.on(dve.scalar_tensor_tensor(y[:, c, 0:T], y[:, c, 0:T], gain[:, c:c + 1], rstd[:, 0:T],
                                                 ALU.mult, ALU.mult))

        @block.gpsimd
        def _(pool):
            for c in range(0, DC, 2):
                pool.wait_ge(made.sem, made0 + c + 2)
                added.on(pool.tensor_tensor(residual[:, c:c + 2, :], residual[:, c:c + 2, :],
                                            y[:, c:c + 2, 0:T], ALU.add))
                pool.wait_ge(added.sem, added.n)


VECTORS = [
    [("ffn1_pre_g", DC), ("ffn1_post_g", DC), ("mix_pre_g", DC), ("mix_post_g", DC), ("ffn2_pre_g", DC),
     ("ffn2_post_g", DC), ("b_gate", GLA_HEADS), ("gla_norm_g", GLA_DV // P)],
    [("shift_mu_2", 33), ("w_decay0_2", 8), ("a0_2", 8), ("k_k_2", 8), ("k_a_2", 8), ("r_k_2", 8),
     ("ln_x_w_2", 8), ("ln_x_b_2", 8), ("lb_logits_2", 8), ("g_norm_w_2", 8)],
    [("ln_w_2", DC), ("ln_b_2", DC)],
]


def set_up(m, dram, first):
    made, loaded = m.sig("constants_made"), m.sig("tokens_loaded")
    params_loaded, turned, copied = m.sig("params_loaded"), m.sig("tokens_turned"), m.sig("turned_copied")
    loaded0 = loaded.n
    with ExitStack() as scope:
        tokens = m.sb("tokens", [P, 3, D], ctx=scope)
        rows = m.sb("param_rows", [P, 3, P], ctx=scope)
        with m.block() as block:

            @block.sync
            def _(sp):
                head = P - N_META
                meta, x = dram["meta_tokens"], dram["x"][0]
                loaded.on(sp.dma_start(tokens[0:N_META, 0, :], meta), 16)
                loaded.on(sp.dma_start(tokens[N_META:P, 0, :], x[0:head, :]), 16)
                loaded.on(sp.dma_start(tokens[:, 1, :], x[head:head + P, :]), 16)
                loaded.on(sp.dma_start(tokens[0:16, 2, :], x[head + P:SEQ, :]), 16)
                for k in range(RAW):
                    load_unit(m, sp, k, first, k, k)

            @block.scalar
            def _(act):
                act.wait_ge(made.sem, 1)
                for j, group in enumerate(VECTORS):
                    row = 0
                    for name, count in group:
                        src = dram[name][0].rearrange("(r c) -> r c", c=P)
                        params_loaded.on(act.dma_start(rows[row:row + count, j, :], src), 16)
                        m.param[name] = (j, row, count)
                        row += count

            @block.gpsimd
            def _(pool):
                made.on(pool.memset(rows[:, :, :], 0.0))
                made.on(pool.memset(m.ident[:, :], 0.0))
                made.on(pool.memset(m.ones[:, :], 1.0))
                pool.wait_ge(made.sem, 3)
                made.on(pool.affine_select(out=m.ident[:, :], in_=m.ident[:, :], compare_op=ALU.not_equal,
                                           fill=1.0, base=0, pattern=[[-1, P]], channel_multiplier=1))
                pool.wait_ge(made.sem, made.n)
                for _ in range(2):
                    pool.nop().then_inc(m.banks_free, 1)
                    pool.nop().then_inc(m.units_done, 1)
                    pool.nop().then_inc(m.hidden_split, 1)

        ready = loaded.n
        turned0, copied0 = turned.n, copied.n
        with m.block() as block:

            @block.tensor
            def _(pe):
                pe.wait_ge(params_loaded.sem, params_loaded.n)
                for j in range(3):
                    mm = pe.transpose(m.ps[:, 7, j * P:(j + 1) * P], rows[:, j, :], m.ident[:, :])
                turned.on(mm)
                pe.wait_ge(loaded.sem, ready)
                for c in range(DC):
                    if c >= 4:
                        pe.wait_ge(copied.sem, copied0 + c - 4 + 2)
                    for j, (t0, n) in enumerate(TILES):
                        mm = pe.transpose(m.ps[:, c % 4, t0:t0 + n], tokens[0:n, j, c * P:(c + 1) * P],
                                          m.ident[0:n, 0:n])
                    turned.on(mm)

            @block.vector
            def _(dve):
                dve.wait_ge(turned.sem, turned0 + 1)
                copied.on(dve.tensor_copy(m.columns[:, :, :].rearrange("p a b -> p (a b)"),
                                          m.ps[:, 7, 0:3 * P]))
                for c in range(DC):
                    dve.wait_ge(turned.sem, turned0 + c + 2)
                    copied.on(dve.tensor_copy(m.r[:, c, :], m.ps[:, c % 4, 0:T1]))


def column(m, name):
    j, row, count = m.param[name]
    return m.columns[:, j, row:row + count]


def build(nc, dram, out):
    with ExitStack() as ctx:
        m = Machine(nc, ctx)
        m.param = {}
        m.ps = ctx.enter_context(nc.psum_tensor("ps", [P, 8, 512], F32))
        m.r = m.sb("residual", [P, DC, T1])
        m.open_x("x")
        m.raw = m.sb("w_raw", [P, RAW, DC * P])
        m.w_hi = m.sb("w_hi", [P, SPLIT, DC * P], F32R)
        m.w_lo = m.sb("w_lo", [P, SPLIT, DC * P], F32R)
        m.ident = m.sb("ident", [P, P])
        m.ones = m.sb("ones", [P, P])
        m.columns = m.sb("param_columns", [P, 3, P])
        m.rstd = m.sb("rstd", [P, T1])
        m.masks = m.sb("masks", [P, len(LEVELS) + 1, P], U8)

        def sem(name):
            return ctx.enter_context(nc.semaphore(name))

        m.raw_loaded = [sem(f"raw_loaded{i}") for i in range(RAW)]
        m.hi_ready, m.lo_ready = sem("hi_ready"), sem("lo_ready")
        m.units_done = sem("units_done")
        m.banks_free = sem("banks_free")
        m.silu_ready, m.hidden_hi = sem("silu_ready"), sem("hidden_hi")
        m.hidden_split = sem("hidden_split")
        stored = m.sig("stored")

        with ExitStack() as scope:
            ffn1 = Ffn(m, dram, "ffn1", scope, declare=False)
            set_up(m, dram, ffn1.stages[0])
        w_in, w_out = dram["w_in"][0], dram["w_out"][0]
        make_masks(m)
        run_ffn(m, dram, "ffn1", Project(m, w_in, 0, 33, T1, None))

        rms_scale(m, "mix_pre", m.r[:, :, :], T1, m.rstd)
        split_features(m, "mix_pre", lambda c: m.r[:, c, :], T1, column(m, "mix_pre_g"), m.rstd)
        o_dsa_scope = ctx.enter_context(ExitStack())
        o_dsa = m.sb("o_dsa", [P, DSA_HEADS, T1], ctx=o_dsa_scope, side="right")
        gla_first = 4176

        def gla_stage(out):
            return Project(m, w_in, gla_first, 17, T1, out)

        def gate_stage(out):
            return Project(m, w_in, gla_first + 2064, 8, T1, out)

        def out_stage(out, w, T):
            return Project(m, w, 0, DC, T, out)

        with ExitStack() as scope:
            proj = m.sb("dsa_proj", [P, 33, T1], ctx=scope)
            dense(m, Project(m, w_in, 0, 33, T1, proj), gla_stage(None))
            v_tokens = m.sb("dsa_v_tokens", [P, 3, DSA_HEADS * P], ctx=scope)
            bias = m.sb("dsa_bias", [P, 3, T1], ctx=scope)
            to_tokens(m, proj[:, 16:24, :], DSA_HEADS, TILES, v_tokens, "dsa")
            with ExitStack() as inner:
                scores = m.sb("dsa_scores", [P, 3, T1], ctx=inner)
                index_scores(m, proj, scores, inner)
                select_keys(m, scores, bias, inner)
            with ExitStack() as inner:
                attend(m, proj, v_tokens, bias, o_dsa, inner)
        with ExitStack() as scope:
            proj = m.sb("gla_proj", [P, 17, T1], ctx=scope)
            gates = m.sb("gla_gates", [P, 8, T1], ctx=scope)
            dense(m, gla_stage(proj), gate_stage(None))
            dense(m, gate_stage(gates), out_stage(None, w_out, T1))
            v_tokens = m.sb("gla_v_tokens", [P, 3, GLA_HEADS * GLA_DV], ctx=scope)
            to_tokens(m, proj[:, 8:16, :], 8, TILES, v_tokens, "gla")
            gla(m, dram, proj, gates, v_tokens, scope)
            norm_heads(m, "gla", proj, 8, 8, 2, m.ones[:, :], EPS, T1, column(m, "gla_norm_g"), True, gates, 0)
            split_features(m, "mixed", lambda c: o_dsa[:, c, :] if c < 8 else proj[:, c, :], T1)
        o_dsa_scope.close()
        w_in_2, w_out_2 = dram["w_in_2"][0], dram["w_out_2"][0]
        with ExitStack() as scope:
            y = m.sb("mixer_out", [P, DC, T1], ctx=scope)
            with ExitStack() as nothing:
                ffn2 = Ffn(m, dram, "ffn2", nothing, declare=False)
            dense(m, out_stage(y, w_out, T1), ffn2.stages[0])
            rms_scale(m, "mix_post", y[:, :, :], T1, m.rstd)
            add_normed(m, y, T1, column(m, "mix_post_g"), m.rstd, m.r)
        def rwkv_stage(out):
            return Project(m, w_in_2, 0, 33, SEQ, out)

        def hgrn_stage(out):
            return Project(m, w_in_2, 33 * P, 32, SEQ, out)

        run_ffn(m, dram, "ffn2", rwkv_stage(None))
        h = m.r[:, :, N_META:T1]
        with ExitStack() as scope:
            proj = m.sb("rwkv_proj", [P, 33, SEQ], ctx=scope)
            split_features(m, "in_2", lambda c: h[:, c, :], SEQ)
            dense(m, rwkv_stage(proj), hgrn_stage(None))
            m.close_x()
            masks = Masks64(m, scope)
            token_shift(m, proj, 33, column(m, "shift_mu_2"))
            alpha, beta, bonus = (m.sb(f"rwkv_{x}", [P, PAIRS, SEQ], ctx=scope) for x in ("alpha", "beta", "bonus"))
            last = m.sb("rwkv_last_decay", [P, PAIRS, SEQ // CHUNK], ctx=scope)
            with ExitStack() as inner:
                sums, tmp = (m.sb(f"rwkv_{x}", [P, PAIRS, SEQ], ctx=inner) for x in ("sums", "tmp"))
                rwkv_vectors(m, dram, proj, masks, sums, alpha, beta, bonus, tmp)
                rwkv_decays(m, proj, sums, alpha, beta, bonus, tmp, last)
            with ExitStack() as inner:
                o = proj[:, 2 * PAIRS:3 * PAIRS, :]
                scan = Rwkv(m, inner, proj, last, alpha, beta, masks, o)
                scan.start()
                for first in range(0, SEQ // CHUNK, 2):
                    scan.prepare(first)
                    scan.scan(first)
            o_rwkv = m.sb("o_rwkv", [P, PAIRS, SEQ], side="right")
            rwkv_finish(m, masks, o, bonus, proj[:, 3 * PAIRS:4 * PAIRS, :], o_rwkv[:, :, :])
        m.open_x("x_again")
        with ExitStack() as scope:
            split_features(m, "in_2_again", lambda c: h[:, c, :], SEQ)
            proj = m.sb("hgrn_proj", [P, 32, SEQ], ctx=scope)
            dense(m, hgrn_stage(proj), out_stage(None, w_out_2, SEQ))
            with ExitStack() as inner:
                b = m.sb("hgrn_log_decay", [P, 8, SEQ], ctx=inner)
                m.close_x()
                hgrn_gates(m, proj, b[:, :, :], inner)
                tokens = m.sb("hgrn_tokens", [P, 2, D // 2], ctx=inner)
                to_tokens(m, proj[:, 16:24, :], 8, TILES[0:2], tokens, "hgrn")
                for g in range(2):
                    heads = slice(4 * g, 4 * g + 4)
                    decay_attention(m, f"hgrn{g}", proj[:, heads, :], proj[:, 8 + 4 * g:12 + 4 * g, :], b[:, heads, :],
                                    SEQ, tokens, 4 * g * P, 1, proj, 16 + 4 * g)
            norm_heads(m, "hgrn", proj, 16, 8, 1, m.ones[:, :], RMS_EPS, SEQ, column(m, "g_norm_w_2"), False, proj, 24)
            m.open_x("x_out")
            split_features(m, "mixed_2", lambda c: o_rwkv[:, c, :] if c < 8 else proj[:, 8 + c, :], SEQ)
        with ExitStack() as scope:
            y = m.sb("out_2", [P, DC, SEQ], ctx=scope)
            dense(m, out_stage(y, w_out_2, SEQ), None)
            layer_norm_out(m, y, out)


class Ffn:

    def __init__(self, m, dram, name, scope, declare=True):
        self.h_hi = m.sb(f"{name}_h_hi", [P, FT // 2, T1], F32R, scope) if declare else None
        self.h_lo = m.sb(f"{name}_h_lo", [P, FT // 2, T1], F32R, scope) if declare else None
        self.silu = m.sb(f"{name}_silu", [P, 2, T1], ctx=scope) if declare else None
        self.hidden = m.sb(f"{name}_hidden", [P, 2, T1], ctx=scope) if declare else None
        self.y = m.sb(f"{name}_y", [P, DC, T1], ctx=scope) if declare else None
        wg, wu, wd = (dram[f"{name}_w_{x}"][0] for x in ("gate", "up", "down"))
        self.stages = []
        for half in range(2):
            self.stages.append(GateUp(m, wg, wu, half, T1, self.h_hi, self.h_lo,
                                      self.silu, self.hidden))
            self.stages.append(Down(m, wd, half, self.h_hi, self.h_lo, T1, self.y))


def run_ffn(m, dram, name, following):
    rms_scale(m, f"{name}_pre", m.r[:, :, :], T1, m.rstd)
    split_features(m, f"{name}_pre", lambda c: m.r[:, c, :], T1, column(m, f"{name}_pre_g"), m.rstd)
    with ExitStack() as scope:
        ffn = Ffn(m, dram, name, scope)
        for stage, then in zip(ffn.stages, ffn.stages[1:] + [following]):
            dense(m, stage, then)
        rms_scale(m, f"{name}_post", ffn.y[:, :, :], T1, m.rstd)
        halve = m.sig("gain_halved")
        gain = m.sb(f"{name}_half_gain", [P, DC], ctx=scope)
        with m.block() as block:

            @block.vector
            def _(dve):
                halve.on(dve.tensor_scalar(gain[:, :], column(m, f"{name}_post_g"), 0.5, None, ALU.mult))
        add_normed(m, ffn.y, T1, gain, m.rstd, m.r)





def kernel(**inputs):
    import concourse.bacc as _bacc
    from concourse.bass_utils import run_bass_kernel_spmd as _run

    nc = _bacc.Bacc("TRN2", target_bir_lowering=False, num_devices=1)
    arrays, dram = {}, {}
    for name, value in inputs.items():
        if 0 in value.shape:
            continue
        a = np.ascontiguousarray(value)
        arrays[f"in_{name}"] = a
        dram[name] = nc.dram_tensor(f"in_{name}", a.shape, mybir.dt.from_np(a.dtype), kind="ExternalInput").ap()
    out = nc.dram_tensor("out", (1, SEQ, D), F32, kind="ExternalOutput").ap()
    build(nc, dram, out)
    r = _run(nc, [arrays], core_ids=[0])
    return r.results[0]["out"]
```

```python
from contextlib import ExitStack

import concourse.bass as bass
from concourse import mybir
import numpy as np

ALU = mybir.AluOpType
ACT = mybir.ActivationFunctionType
AX = mybir.AxisListType
F32 = mybir.dt.float32
F32R = mybir.dt.float32r
U8 = mybir.dt.uint8

P = 128
D = 2048
DC = D // P
N_META = 16
SEQ = 256
T1 = N_META + SEQ
D_FF = 5632
FT = D_FF // P
TILES = [(0, 128), (128, 128), (256, 16)]
EPS = 1e-6

DSA_HEADS = 8
IDX_HEADS = 16
IDX_DIM = 64
TOP_K = min(256, SEQ // 4)
GLA_HEADS = 4
GLA_DV = 256
GLA_TAU = 16.0

RAW = 4
SPLIT = 2
MASKED = -1.0e30
TAKEN = -3.0e38


class Signal:

    def __init__(self, nc, ctx, name):
        self.sem = ctx.enter_context(nc.semaphore(name))
        self.n = 0

    def on(self, instruction, by=1):
        instruction.then_inc(self.sem, by)
        self.n += by
        return instruction


class Machine:

    def __init__(self, nc, ctx):
        self.nc, self.ctx = nc, ctx
        self.signals = {}
        self.unit = 0
        self.group = 0
        self.pairs = 0
        self.squares = 0

    def sb(self, name, shape, dt=F32, ctx=None, side="left"):
        return (ctx or self.ctx).enter_context(self.nc.sbuf_tensor(name, shape, dt, side=side))

    def sig(self, name):
        if name not in self.signals:
            self.signals[name] = Signal(self.nc, self.ctx, name)
        return self.signals[name]

    def open_x(self, name):
        self.x_scope = self.ctx.enter_context(ExitStack())
        self.x_hi, self.x_lo = (self.sb(f"{name}_{part}", [P, DC, T1], F32R, self.x_scope, "right") for part in ("hi", "lo"))

    def close_x(self):
        self.x_scope.close()
        self.x_hi = self.x_lo = None

    def dense_bank(self, group, bank):
        return self.ps[:, 4 * (group % 2) + 3 - bank, :]

    def block(self):
        return self.nc.Block(no_gpsimd_drain=True)


def load_unit(m, sp, unit, stage, rel, u):
    src = stage.source(rel, u)
    dst = m.raw[:, unit % RAW, 0:stage.chunks * P].rearrange("p (k c) -> p k c", c=P)
    sp.dma_start(dst, src.rearrange("(k p) c -> p k c", p=P)).then_inc(m.raw_loaded[unit % RAW], 16)


class Norm:

    def __init__(self, m, count, T, rstd, eps=EPS):
        self.m, self.count, self.T, self.rstd, self.eps = m, count, T, rstd, eps
        self.n0 = m.squares
        m.squares += count
        self.summed, self.scaled, self.rooted = m.sig("square_sums"), m.sig("mean_squares"), m.sig("roots")
        self.base = {s: s.n for s in (self.summed, self.scaled, self.rooted)}

    def square_act(self, act, source, c):
        m, n = self.m, self.n0 + c
        act.wait_ge(m.squares_free, n + 1)
        act.activation(m.sq[:, n % 2, 0:self.T], source, ACT.Square).then_inc(m.squared, 1)

    def sum_pe(self, pe, c):
        m, n = self.m, self.n0 + c
        pe.wait_ge(m.squared, n + 1)
        pe.matmul(m.ps[:, 5, 0:self.T], m.ones[:, :], m.sq[:, n % 2, 0:self.T], start=c == 0,
                  stop=c == self.count - 1).then_inc(m.squares_free, 1)

    def clear(self, pool):
        cleared = self.m.sig("acc_cleared")
        cleared.on(pool.memset(self.m.acc[:, 0:self.T], 0.0))
        pool.wait_ge(cleared.sem, cleared.n)

    def add_pool(self, pool, source, i, u, per_body):
        m, n, at = self.m, self.n0 + u, per_body * i
        acc, sq = m.acc[:, 0:self.T], m.sq[:, n % 2, 0:self.T]
        pool.tensor_tensor(sq, source, source, ALU.mult).then_inc(m.squared, 1)
        pool.wait_ge(m.squared, n + at + 1)
        pool.wait_ge(m.squares_free, n + at + 2)
        pool.tensor_tensor(acc, acc, sq, ALU.add).then_inc(m.squares_free, 1)

    def finish_pe(self, pe):
        pe.wait_ge(self.m.squares_free, self.n0 + self.count + 2)
        self.summed.on(pe.matmul(self.m.ps[:, 5, 0:self.T], self.m.ones[:, :], self.m.acc[:, 0:self.T],
                                 start=True, stop=True))

    def finish_dve(self, dve, fed):
        if fed:
            dve.wait_ge(self.m.squares_free, self.n0 + self.count + 2)
        else:
            dve.wait_ge(self.summed.sem, self.base[self.summed] + 1)
        self.scaled.on(dve.tensor_scalar(self.rstd[:, 0:self.T], self.m.ps[:, 5, 0:self.T],
                                         1.0 / (self.count * P), self.eps, ALU.mult, ALU.add))
        dve.wait_ge(self.rooted.sem, self.base[self.rooted] + 1)
        self.scaled.on(dve.reciprocal(self.rstd[:, 0:self.T], self.rstd[:, 0:self.T]))
        dve.wait_ge(self.scaled.sem, self.base[self.scaled] + 2)

    def finish_act(self, act):
        act.wait_ge(self.scaled.sem, self.base[self.scaled] + 1)
        self.rooted.on(act.activation(self.rstd[:, 0:self.T], self.rstd[:, 0:self.T], ACT.Sqrt))


class Feed:

    def __init__(self, m, h, T, gain=None, update=None, norm=None):
        self.m, self.h, self.T, self.gain, self.update, self.norm = m, h, T, gain, update, norm
        self.scaled, self.added = m.sig("update_scaled"), m.sig("residual_added")
        self.high, self.low = m.sig("x_high"), m.sig("x_low")
        self.base = {s: s.n for s in (self.scaled, self.added, self.high, self.low)}

    def dve(self, dve, middle):
        base = self.base
        for c in range(DC + 1):
            if self.update is not None and c < DC:
                y, gain, rstd = self.update
                self.scaled.on(dve.scalar_tensor_tensor(y[:, c, 0:self.T], y[:, c, 0:self.T], gain[:, c:c + 1],
                                                        rstd[:, 0:self.T], ALU.mult, ALU.mult))
            if c == DC // 2:
                middle()
            if c >= 1:
                k = c - 1
                dve.wait_ge(self.high.sem, base[self.high] + k + 1)
                hi, lo = (x[:, k, 0:self.T] for x in (self.m.x_hi, self.m.x_lo))
                if self.gain is None:
                    self.low.on(dve.tensor_tensor(lo, self.h(k), hi.bitcast(F32), ALU.subtract))
                else:
                    self.low.on(dve.scalar_tensor_tensor(lo, self.h(k), self.gain[:, k:k + 1],
                                                         hi.bitcast(F32), ALU.mult, ALU.subtract))

    def act(self, act, middle):
        for c in range(DC):
            if self.update is not None:
                act.wait_ge(self.added.sem, self.base[self.added] + c + 1)
            hi = self.m.x_hi[:, c, 0:self.T]
            if self.gain is None:
                self.high.on(act.activation(hi, self.h(c), ACT.Copy))
            else:
                self.high.on(act.activation(hi, self.h(c), ACT.Copy, scale=self.gain[:, c:c + 1]))
            if c == DC // 2:
                middle()
            if self.norm is not None:
                self.norm.square_act(act, self.h(c), c)

    def pool(self, pool):
        for c in range(DC if self.update is not None else 0):
            pool.wait_ge(self.scaled.sem, self.base[self.scaled] + c + 1)
            self.added.on(pool.tensor_tensor(self.h(c), self.h(c), self.update[0][:, c, 0:self.T], ALU.add))
        if self.update is not None:
            pool.wait_ge(self.added.sem, self.added.n)

    def before_chunk(self, pe, k):
        pe.wait_ge(self.low.sem, self.base[self.low] + k + 1)
        if self.norm is not None and k >= 1:
            self.norm.sum_pe(pe, k - 1)


class Ring:

    def __init__(self, m, stage, following):
        self.m, self.stage, self.following = m, stage, following
        self.n0, self.g0, self.count = m.unit, m.group, stage.count
        stage.n0, stage.g0, stage.p0 = m.unit, m.group, m.pairs
        m.unit += stage.count
        m.group += stage.count // stage.per_group
        m.pairs += stage.pairs

    def load(self, sp, i, u):
        m, n = self.m, self.n0 + u
        if isinstance(i, int) and 4 * i + u + RAW >= self.count:
            k = 4 * i + u + RAW - self.count
            if self.following is None:
                return
            stage, rel, parity = self.following, k, k
        else:
            stage, rel, parity = self.stage, 4 * i + u + RAW, u
        sp.wait_ge(m.lo_ready, n + 4 * i + 1)
        load_unit(m, sp, n, stage, rel, parity)

    def next_chunks(self, i, u):
        if isinstance(i, int) and 4 * i + u == self.count - 1:
            return None if self.following is None else self.following.chunks
        return self.stage.chunks

    def high(self, act, i, u, chunks):
        if chunks is None:
            return
        m, n = self.m, self.n0 + u
        act.wait_ge(m.raw_loaded[n % RAW], 16 * (n // RAW + 1) + 16 * i)
        act.wait_ge(m.units_done, n + 4 * i + 1)
        act.activation(m.w_hi[:, n % SPLIT, 0:chunks * P], m.raw[:, n % RAW, 0:chunks * P],
                       ACT.Copy).then_inc(m.hi_ready, 1)

    def low(self, dve, i, u, chunks):
        if chunks is None:
            return
        m, n = self.m, self.n0 + u
        dve.wait_ge(m.hi_ready, n + 4 * i + 1)
        dve.tensor_tensor(m.w_lo[:, n % SPLIT, 0:chunks * P], m.raw[:, n % RAW, 0:chunks * P],
                          m.w_hi[:, n % SPLIT, 0:chunks * P].bitcast(F32), ALU.subtract).then_inc(m.lo_ready, 1)

    def multiply(self, pe, i, u, before_chunk=None):
        m, stage, n, T = self.m, self.stage, self.n0 + u, self.stage.T
        bank, start, stop = stage.bank(u)
        group = self.g0 + u // stage.per_group
        out = m.dense_bank(group, bank)[:, 0:T]
        pe.wait_ge(m.lo_ready, n + 4 * i + 1)
        if u % stage.per_group == 0:
            pe.wait_ge(m.banks_free, group + (4 // stage.per_group) * i + 1)
        x_hi, x_lo = stage.moving(u)
        for k in range(stage.chunks):
            if before_chunk is not None:
                before_chunk(k)
            w_hi = m.w_hi[:, n % SPLIT, k * P:(k + 1) * P]
            w_lo = m.w_lo[:, n % SPLIT, k * P:(k + 1) * P]
            first, last = start and k == 0, stop and k == stage.chunks - 1
            pe.matmul(out, w_hi, x_hi[:, k, 0:T], start=first, stop=False)
            pe.matmul(out, w_hi, x_lo[:, k, 0:T], start=False, stop=False)
            mm = pe.matmul(out, w_lo, x_hi[:, k, 0:T], start=False, stop=last)
        mm.then_inc(m.units_done, 1)


def dense(m, stage, following, feed=None, beside=None):
    ring = Ring(m, stage, following)
    if stage.norm_rstd is not None:
        stage.norm = Norm(m, stage.tiles, stage.T, stage.norm_rstd)
    count = stage.count
    first = 1 if feed is not None else 0
    last = max(count // 4 - 1, first)

    def over(eng, body):
        for u in range(4 * first):
            body(0, u)
        if last > first:
            with eng.Fori(first, last) as i:
                for u in range(4):
                    body(i, u)
        for rel in range(4 * last, count):
            body(rel // 4, rel % 4)

    def beginning(i, u):
        return feed is not None and isinstance(i, int) and (i, u) == (0, 0)

    with m.block() as block:

        @block.sync
        def _(sp):
            over(sp, lambda i, u: ring.load(sp, i, u))

        @block.scalar
        def _(act):
            def step(i, u):
                if not beginning(i, u):
                    ring.high(act, i, u + 1, ring.next_chunks(i, u))
                stage.evacuate_act(act, i, u)

            if ring.n0 == 0:
                ring.high(act, 0, 0, stage.chunks)
            if feed is not None:
                feed.act(act, lambda: ring.high(act, 0, 1, stage.chunks))
                if feed.norm is not None:
                    feed.norm.finish_act(act)
            over(act, step)
            if stage.norm is not None:
                stage.norm.finish_act(act)

        @block.vector
        def _(dve):
            def step(i, u):
                if not beginning(i, u):
                    ring.low(dve, i, u + 1, ring.next_chunks(i, u))
                stage.evacuate_dve(dve, i, u)

            if ring.n0 == 0:
                ring.low(dve, 0, 0, stage.chunks)
            if feed is not None:
                feed.dve(dve, lambda: ring.low(dve, 0, 1, stage.chunks))
                if feed.norm is not None:
                    feed.norm.finish_dve(dve, True)
            over(dve, step)
            if stage.norm is not None:
                stage.norm.finish_dve(dve, False)

        @block.gpsimd
        def _(pool):
            if feed is not None:
                feed.pool(pool)
            if beside is not None:
                beside(pool)
            if stage.norm is not None:
                stage.norm.clear(pool)
            if stage.evacuate_pool is not None:
                over(pool, lambda i, u: stage.evacuate_pool(pool, i, u))
                stage.settle_pool(pool)
            if stage.norm is not None:
                pool.wait_ge(m.squares_free, m.squares + 2)

        @block.tensor
        def _(pe):
            def multiply(i, u):
                if beginning(i, u):
                    ring.multiply(pe, i, u, lambda k: feed.before_chunk(pe, k))
                    if feed.norm is not None:
                        feed.norm.sum_pe(pe, DC - 1)
                else:
                    ring.multiply(pe, i, u)

            over(pe, multiply)
            if stage.norm is not None:
                stage.norm.finish_pe(pe)


class Project:

    per_group, pairs, chunks = 1, 0, DC

    def __init__(self, m, weights, first_column, count, T, out, scale=None, rstd=None):
        self.m, self.w, self.c0, self.count, self.T = m, weights, first_column, count, T
        self.out, self.scale = out, scale
        if rstd is None:
            self.evacuate_pool = None
        self.norm, self.norm_rstd, self.tiles = None, rstd, count

    def source(self, rel, u):
        return self.w[0:DC * P, bass.ds(self.c0 + rel * P, P)]

    def moving(self, u):
        return self.m.x_hi, self.m.x_lo

    def bank(self, u):
        return 0, True, True

    def tile(self, i, u):
        return self.out[:, bass.ds(4 * i + u, 1), 0:self.T].rearrange("p a t -> p (a t)")

    def evacuate_act(self, act, i, u):
        m = self.m
        if self.scale is None:
            act.wait_ge(m.units_done, self.n0 + 4 * i + u + 1 + SPLIT)
            act.activation(self.tile(i, u), m.dense_bank(self.g0 + u, 0)[:, 0:self.T],
                           ACT.Copy).then_inc(m.banks_free, 1)
    def evacuate_dve(self, dve, i, u):
        m = self.m
        if self.scale is not None:
            dve.wait_ge(m.units_done, self.n0 + 4 * i + u + 1 + SPLIT)
            dve.tensor_tensor(self.tile(i, u), m.dense_bank(self.g0 + u, 0)[:, 0:self.T],
                              self.scale[:, 0:self.T], ALU.mult).then_inc(m.banks_free, 1)

    def evacuate_pool(self, pool, i, u):
        pool.wait_ge(self.m.banks_free, self.g0 + 4 * i + u + 1 + 2)
        self.norm.add_pool(pool, self.tile(i, u), i, u, 4)

    def settle_pool(self, pool):
        pass


class Shifted(Project):

    def __init__(self, m, weights, first_column, count, T, out, mu, differences):
        super().__init__(m, weights, first_column, count, T, out)
        self.mu, self.d, self.evacuate_pool = mu, differences, self.difference

    def difference(self, pool, i, u):
        m, d, T = self.m, self.d[:, u % 2, :], self.T
        y = self.tile(i, u)
        pool.wait_ge(m.banks_free, self.g0 + 4 * i + u + 1 + 2)
        pool.wait_ge(m.shift_free, 4 * i + u + 1)
        pool.tensor_tensor(d[:, 0:1], m.zero[:, :], y[:, 0:1], ALU.subtract).then_inc(m.differed, 1)
        pool.tensor_tensor(d[:, 1:T], y[:, 0:T - 1], y[:, 1:T], ALU.subtract).then_inc(m.differed, 1)

    def settle_pool(self, pool):
        pool.wait_ge(self.m.differed, 2 * self.count)

    def evacuate_dve(self, dve, i, u):
        m, y = self.m, self.tile(i, u)
        dve.wait_ge(m.differed, 8 * i + 2 * u + 2)
        mu = self.mu[:, bass.ds(4 * i + u, 1)]
        dve.scalar_tensor_tensor(y, self.d[:, u % 2, :], mu, y, ALU.mult, ALU.add).then_inc(m.shift_free, 1)


class GateUp:

    per_group, pairs, norm, norm_rstd = 2, FT // 2, None, None

    def __init__(self, m, w_gate, w_up, half, T, h_hi, h_lo, silu, hidden, rstd):
        self.m, self.wg, self.wu, self.half, self.T = m, w_gate, w_up, half, T
        self.h_hi, self.h_lo = h_hi, h_lo
        self.silu, self.hidden, self.rstd = silu, hidden, rstd
        self.chunks, self.count = DC, FT

    def source(self, rel, u):
        w = self.wu if u % 2 else self.wg
        first = self.half * (FT // 2) * P
        return w[:, bass.ds(first + (rel - u % 2) * (P // 2), P)]

    def moving(self, u):
        return self.m.x_hi, self.m.x_lo

    def bank(self, u):
        return u % 2, True, True

    def evacuate_act(self, act, i, u):
        m = self.m
        if u % 2 == 1:
            pair = self.p0 + u // 2
            gate = self.silu[:, pair % 2, 0:self.T]
            act.wait_ge(m.gate_scaled, pair + 2 * i + 1)
            act.activation(gate, gate, ACT.Silu).then_inc(m.silu_ready, 1)

    def evacuate_dve(self, dve, i, u):
        m = self.m
        group, pair = self.g0 + u // 2, self.p0 + u // 2
        rstd, hidden = self.rstd[:, 0:self.T], self.hidden[:, pair % 2, 0:self.T]
        gate = self.silu[:, pair % 2, 0:self.T]
        dve.wait_ge(m.units_done, self.n0 + 4 * i + u + 1 + SPLIT)
        if u % 2 == 0:
            dve.wait_ge(m.hidden_split, pair + 2 * i + 1)
            dve.tensor_tensor(gate, m.dense_bank(group, 0)[:, 0:self.T], rstd, ALU.mult).then_inc(m.gate_scaled, 1)
        else:
            dve.tensor_tensor(hidden, m.dense_bank(group, 1)[:, 0:self.T], rstd, ALU.mult).then_inc(m.banks_free, 1)
            dve.wait_ge(m.banks_free, group + 2 * i + 1 + 2)
            dve.wait_ge(m.silu_ready, pair + 2 * i + 1)
            dve.tensor_tensor(hidden, hidden, gate, ALU.mult).then_inc(m.hidden_ready, 1)

    def evacuate_pool(self, pool, i, u):
        m = self.m
        if u % 2 == 1:
            pair = self.p0 + u // 2
            hidden = self.hidden[:, pair % 2, 0:self.T]
            hi = self.h_hi[:, bass.ds(2 * i + u // 2, 1), 0:self.T].rearrange("p a t -> p (a t)")
            lo = self.h_lo[:, bass.ds(2 * i + u // 2, 1), 0:self.T].rearrange("p a t -> p (a t)")
            pool.wait_ge(m.hidden_ready, pair + 2 * i + 1)
            pool.tensor_copy(hi, hidden).then_inc(m.hidden_hi, 1)
            pool.wait_ge(m.hidden_hi, pair + 2 * i + 1)
            pool.tensor_tensor(lo, hidden, hi.bitcast(F32), ALU.subtract).then_inc(m.hidden_split, 1)


    def settle_pool(self, pool):
        pool.wait_ge(self.m.hidden_split, self.m.pairs + 2)


class Down:

    per_group, pairs = 2, 0

    def __init__(self, m, w_down, half, h_hi, h_lo, T, y, rstd=None):
        self.m, self.w, self.half, self.T, self.y = m, w_down, half, T, y
        self.h = (h_hi, h_lo)
        self.chunks, self.count = FT // 4, 2 * DC
        self.norm, self.norm_rstd, self.tiles = None, rstd, DC
        if rstd is None:
            self.evacuate_pool = None

    def source(self, rel, u):
        first = (self.half * 2 + u % 2) * self.chunks * P
        cols = bass.ds((rel - u % 2) * (P // 2), P)
        return self.w[first:first + self.chunks * P, cols]

    def moving(self, u):
        a = (u % 2) * self.chunks
        return tuple(h[:, a:a + self.chunks, 0:self.T] for h in self.h)

    def bank(self, u):
        return 0, u % 2 == 0, u % 2 == 1

    def tile(self, i, u):
        return self.y[:, bass.ds(2 * i + u // 2, 1), 0:self.T].rearrange("p a t -> p (a t)")

    def evacuate_act(self, act, i, u):
        m, group = self.m, self.g0 + u // 2
        if u % 2 == 1 and self.half == 0:
            act.wait_ge(m.units_done, self.n0 + 4 * i + u + 1 + SPLIT)
            act.activation(self.tile(i, u), m.dense_bank(group, 0)[:, 0:self.T], ACT.Copy).then_inc(m.banks_free, 1)

    def evacuate_dve(self, dve, i, u):
        m, group = self.m, self.g0 + u // 2
        if u % 2 == 1 and self.half == 1:
            dve.wait_ge(m.units_done, self.n0 + 4 * i + u + 1 + SPLIT)
            dve.tensor_tensor(self.tile(i, u), m.dense_bank(group, 0)[:, 0:self.T], self.tile(i, u),
                              ALU.add).then_inc(m.banks_free, 1)

    def evacuate_pool(self, pool, i, u):
        if u % 2 == 1:
            pool.wait_ge(self.m.banks_free, self.g0 + u // 2 + 2 * i + 1 + 2)
            self.norm.add_pool(pool, self.tile(i, u), i, u // 2, 2)

    def settle_pool(self, pool):
        pass


QUERIES = [(N_META, P), (N_META + P, P)]
FREE_BANKS = [0, 1, 4, 5, 2, 6]
OUT_BANKS = [4, 5, 2, 6, 0, 1]
LEVELS = [64, 32, 16, 8, 4, 2, 1]


def make_masks(m, pool):
    made, full = m.sig("masks_made"), m.masks_full
    made.on(pool.memset(full[:, :, :], 0.0))
    pool.wait_ge(made.sem, made.n)
    for level, h in enumerate(LEVELS):
        view = full[:, level, :].rearrange("p (n a h) -> p n a h", a=2, h=h)[:, :, 1, :]
        made.on(pool.memset(view, 1.0))
        blocks = P // (2 * h)
        for base, sign in ((0, 1), (h - 1, -1)):
            pool.wait_ge(made.sem, made.n)
            made.on(pool.affine_select(out=view, in_=view, compare_op=ALU.is_ge, fill=0.0, base=base,
                                       pattern=[[-2 * h * sign, blocks]] * (blocks > 1) + [[0, h]] * (h > 1),
                                       channel_multiplier=sign))
    made.on(pool.tensor_copy(full[:, len(LEVELS), :], m.ident[:, :]))
    pool.wait_ge(made.sem, made.n)
    made.on(pool.tensor_copy(m.masks[:, :, :], full[:, :, :]))
    pool.wait_ge(made.sem, made.n)


def to_tokens(m, source, chunks, tiles, tokens, name):
    turned = m.sig("chunks_turned")
    bank = FREE_BANKS
    copied = [m.sig("turned_copied_act"), m.sig("turned_copied_dve")]
    groups = [(j, c) for j in range(len(tiles)) for c in range(0, chunks, 4)]
    turned0, copied0 = turned.n, [c.n for c in copied]
    with m.block() as block:

        @block.tensor
        def _(pe):
            for g, (j, c0) in enumerate(groups):
                t0, n = tiles[j]
                if g >= 4:
                    pe.wait_ge(copied[g % 2].sem, copied0[g % 2] + (g - 4) // 2 + 1)
                for c in range(4):
                    mm = pe.transpose(m.ps[0:n, bank[g % 4], c * P:(c + 1) * P], source[:, c0 + c, t0:t0 + n],
                                      m.ident[:, :])
                turned.on(mm)

        def copy(eng, parity):
            for g, (j, c0) in enumerate(groups):
                if g % 2 == parity:
                    n = tiles[j][1]
                    dst, src = tokens[0:n, j, c0 * P:(c0 + 4) * P], m.ps[0:n, bank[g % 4], :]
                    eng.wait_ge(turned.sem, turned0 + g + 1)
                    done = eng.activation(dst, src, ACT.Copy) if parity == 0 else eng.tensor_copy(dst, src)
                    copied[parity].on(done)

        @block.scalar
        def _(act):
            copy(act, 0)

        @block.vector
        def _(dve):
            copy(dve, 1)


def index_scores(m, proj, scores, scope):
    ik2 = m.sb("idx_keys", [P, T1], ctx=scope)
    weights = m.sb("idx_weights", [P, len(QUERIES), IDX_HEADS], ctx=scope)
    rectified = m.sb("idx_rectified", [P, 2, T1], ctx=scope)
    keys, turned, scaled = m.sig("idx_keys_copied"), m.sig("idx_weights_turned"), m.sig("idx_weights_scaled")
    made, relued, added = m.sig("idx_logits_made"), m.sig("idx_relued"), m.sig("idx_added")
    masked = m.sig("idx_masked")
    with m.block() as block:

        @block.scalar
        def _(act):
            keys.on(act.activation(ik2[0:IDX_DIM, :], proj[0:IDX_DIM, 32, :], ACT.Copy))
            keys.on(act.activation(ik2[IDX_DIM:P, :], proj[0:IDX_DIM, 32, :], ACT.Copy))

        @block.tensor
        def _(pe):
            w = proj[IDX_DIM:IDX_DIM + IDX_HEADS, 32, :]
            for j, (t0, n) in enumerate(QUERIES):
                mm = pe.matmul(m.ps[0:n, 2, j * 32:j * 32 + IDX_HEADS], w[:, t0:t0 + n],
                               m.ident[IDX_DIM:IDX_DIM + IDX_HEADS, IDX_DIM:IDX_DIM + IDX_HEADS],
                               start=True, stop=True)
            turned.on(mm)

        @block.vector
        def _(dve):
            dve.wait_ge(turned.sem, turned.n)
            for j, (t0, n) in enumerate(QUERIES):
                scaled.on(dve.tensor_scalar(weights[0:n, j, :], m.ps[0:n, 2, j * 32:j * 32 + IDX_HEADS],
                                            float(IDX_HEADS) ** -0.5, None, ALU.mult))

    order = [(j, h) for j in range(len(QUERIES)) for h in range(IDX_HEADS)]
    made0, relued0, added0 = made.n, relued.n, added.n
    with m.block() as block:

        @block.tensor
        def _(pe):
            for x, (j, h) in enumerate(order):
                (t0, n), half = QUERIES[j], (h % 2) * IDX_DIM
                if x >= 4:
                    pe.wait_ge(relued.sem, relued0 + x - 3)
                made.on(pe.matmul(m.ps[0:n, FREE_BANKS[x % 4], 0:t0 + n], proj[half:half + IDX_DIM, 24 + h // 2, t0:t0 + n],
                                  ik2[half:half + IDX_DIM, 0:t0 + n], start=True, stop=True))

        @block.scalar
        def _(act):
            for x, (j, h) in enumerate(order):
                t0, n = QUERIES[j]
                act.wait_ge(made.sem, made0 + x + 1)
                if x >= 2:
                    act.wait_ge(added.sem, added0 + x - 1)
                relued.on(act.activation(rectified[0:n, x % 2, 0:t0 + n], m.ps[0:n, FREE_BANKS[x % 4], 0:t0 + n], ACT.Relu,
                                         scale=float(IDX_DIM) ** -0.5))

        @block.vector
        def _(dve):
            for x, (j, h) in enumerate(order):
                t0, n = QUERIES[j]
                src, acc = rectified[0:n, x % 2, 0:t0 + n], scores[0:n, j, 0:t0 + n]
                dve.wait_ge(relued.sem, relued0 + x + 1)
                if h == 0:
                    added.on(dve.tensor_scalar(acc, src, weights[0:n, j, h:h + 1], None, ALU.mult))
                else:
                    dve.wait_ge(added.sem, added0 + x)
                    added.on(dve.scalar_tensor_tensor(acc, src, weights[0:n, j, h:h + 1], acc, ALU.mult, ALU.add))

        @block.gpsimd
        def _(pool):
            for j, (t0, n) in enumerate(QUERIES):
                acc = scores[0:n, j, 0:t0 + n]
                pool.wait_ge(added.sem, added0 + (j + 1) * IDX_HEADS)
                masked.on(pool.affine_select(out=acc, in_=acc, compare_op=ALU.is_ge, fill=MASKED, base=t0,
                                             pattern=[[-1, t0 + n]], channel_multiplier=1))
            pool.wait_ge(masked.sem, masked.n)


def select_keys(m, scores, bias, scope):
    best = m.sb("topk_best", [P, len(QUERIES), 8], ctx=scope)
    found, flagged, biased = m.sig("topk_steps"), m.sig("topk_flagged"), m.sig("topk_biased")
    with m.block() as block:

        @block.vector
        def _(dve):
            for j, (t0, n) in enumerate(QUERIES):
                row, top = scores[0:n, j, 0:t0 + n], best[0:n, j, :]
                for _ in range(TOP_K // 8):
                    if found.n:
                        dve.wait_ge(found.sem, found.n)
                    found.on(dve.max(top, row))
                    dve.wait_ge(found.sem, found.n)
                    found.on(dve.match_replace(row, top, row, TAKEN))
                dve.wait_ge(found.sem, found.n)
                flagged.on(dve.tensor_scalar(bias[0:n, j, 0:t0 + n], row, TAKEN, 1.0, ALU.is_equal, ALU.subtract))

        @block.gpsimd
        def _(pool):
            for j, (t0, n) in enumerate(QUERIES):
                row = bias[0:n, j, 0:t0 + n]
                pool.wait_ge(flagged.sem, j + 1)
                biased.on(pool.tensor_scalar(row, row, -MASKED, None, ALU.mult))
                pool.wait_ge(biased.sem, biased.n)
                biased.on(pool.affine_select(out=row, in_=row, compare_op=ALU.is_ge, fill=MASKED, base=t0,
                                             pattern=[[-1, t0 + n]], channel_multiplier=1))
            pool.wait_ge(biased.sem, biased.n)


def attend(m, proj, v_tokens, bias, o, scope):
    H = DSA_HEADS
    logits = m.sb("attn_logits", [P, H, T1], ctx=scope)
    turned_p = m.sb("attn_turned", [P, len(TILES), H, P], ctx=scope)
    small = m.sb("attn_small", [P, 4, H], ctx=scope)
    negated, total, inverse = small[:, 1, :], small[:, 2, :], small[:, 3, :]
    made, biased, peaked = m.sig("attn_products"), m.sig("attn_biased"), m.sig("attn_peaks")
    exped, inverted, normed = m.sig("attn_exps"), m.sig("attn_inverted"), m.sig("attn_normed")
    turned, copied, out_made, out_copied = (m.sig("attn_turned"), m.sig("attn_turned_copied"),
                                            m.sig("attn_outputs"), m.sig("attn_outputs_copied"))
    for j, (t0, n) in enumerate(QUERIES):
        N = t0 + n
        keys = [(s0, min(P, N - s0)) for s0 in range(0, N, P)]
        q0 = t0 - N_META
        base = {s: s.n for s in (made, biased, peaked, exped, inverted, normed, turned, copied, out_made,
                                 out_copied)}
        groups = [(half, i) for half in range(2) for i in range(len(keys))]
        with m.block() as block:

            @block.tensor
            def _(pe):
                for h in range(H):
                    if h >= 3:
                        pe.wait_ge(biased.sem, base[biased] + h - 2)
                    made.on(pe.matmul(m.ps[0:n, h % 3, 0:N], proj[:, h, t0:t0 + n], proj[:, H + h, 0:N],
                                      start=True, stop=True))
                for g, (half, i) in enumerate(groups):
                    s0, sn = keys[i]
                    if g >= 2:
                        pe.wait_ge(copied.sem, base[copied] + g - 1)
                    for h in range(4 * half, 4 * half + 4):
                        pe.wait_ge(normed.sem, base[normed] + h + 1)
                        mm = pe.transpose(m.ps[0:sn, 4 + g % 2, (h % 4) * P:(h % 4) * P + n],
                                          logits[0:n, h, s0:s0 + sn], m.ident[0:n, 0:n])
                    turned.on(mm)
                for half in range(2):
                    pe.wait_ge(copied.sem, base[copied] + (half + 1) * len(keys))
                    for h in range(4 * half, 4 * half + 4):
                        for i in range(len(keys)):
                            sn = keys[i][1]
                            mm = pe.matmul(m.ps[:, half, (h % 4) * P:(h % 4) * P + n],
                                           v_tokens[0:sn, i, h * P:(h + 1) * P], turned_p[0:sn, i, h, 0:n],
                                           start=i == 0, stop=i == len(keys) - 1)
                    out_made.on(mm)

            @block.vector
            def _(dve):
                for h in range(H):
                    dve.wait_ge(made.sem, base[made] + h + 1)
                    biased.on(dve.scalar_tensor_tensor(logits[0:n, h, 0:N], m.ps[0:n, h % 3, 0:N],
                                                       float(P) ** -0.5, bias[0:n, j, 0:N], ALU.mult, ALU.add))
                dve.wait_ge(biased.sem, biased.n)
                peaked.on(dve.tensor_reduce(small[0:n, 0, :], logits[0:n, :, 0:N], AX.X, ALU.max))
                dve.wait_ge(peaked.sem, peaked.n)
                peaked.on(dve.tensor_scalar(negated[0:n, :], small[0:n, 0, :], -1.0, None, ALU.mult))
                for half in range(2):
                    dve.wait_ge(exped.sem, base[exped] + 4 * half + 4)
                    inverted.on(dve.reciprocal(inverse[0:n, 4 * half:4 * half + 4],
                                               total[0:n, 4 * half:4 * half + 4]))
                    dve.wait_ge(inverted.sem, inverted.n)
                    for h in range(4 * half, 4 * half + 4):
                        normed.on(dve.tensor_scalar(logits[0:n, h, 0:N], logits[0:n, h, 0:N],
                                                    inverse[0:n, h:h + 1], None, ALU.mult))
                for half in range(2):
                    dve.wait_ge(out_made.sem, base[out_made] + half + 1)
                    out_copied.on(dve.tensor_copy(
                        o[:, 4 * half:4 * half + 4, q0:q0 + n],
                        m.ps[:, half, :].rearrange("p (h q) -> p h q", h=4)[:, :, 0:n]))

            @block.scalar
            def _(act):
                act.wait_ge(peaked.sem, base[peaked] + 2)
                for h in range(H):
                    exped.on(act.activation(logits[0:n, h, 0:N], logits[0:n, h, 0:N], ACT.Exp,
                                            bias=negated[0:n, h:h + 1], accum_out=total[0:n, h:h + 1]))
                for g, (half, i) in enumerate(groups):
                    sn = keys[i][1]
                    act.wait_ge(turned.sem, base[turned] + g + 1)
                    copied.on(act.activation(
                        turned_p[0:sn, i, 4 * half:4 * half + 4, 0:n],
                        m.ps[0:sn, 4 + g % 2, :].rearrange("p (h q) -> p h q", h=4)[:, :, 0:n], ACT.Copy))


def decay_attention(m, name, q, k, b, T, v_tokens, v0, dv_chunks, out, out0):
    H = 4
    tiles = TILES[0:2] if T == SEQ else TILES
    L = len(LEVELS)
    diff_q, diff_k, exped = m.sig("decay_diff_later"), m.sig("decay_diff_earlier"), m.sig("decay_exps")
    q_made, k_made, paired, chosen = (m.sig("decayed_q"), m.sig("decayed_k"), m.sig("decay_pairs"),
                                      m.sig("decay_chosen"))
    cleared = m.sig("decay_cleared")
    with ExitStack() as scope:
        a = m.sb(f"{name}_a", [P, 2, H, P], ctx=scope)
        a_tail = m.sb(f"{name}_a_tail", [16, H, 16], ctx=scope)
        e = m.sb(f"{name}_e", [P, 2, H, T], ctx=scope)
        qe = m.sb(f"{name}_qe", [P, 2, H, T], ctx=scope)
        ke = m.sb(f"{name}_ke", [P, 2, H, T], ctx=scope)
        base = {s: s.n for s in (diff_q, diff_k, exped, q_made, k_made, paired, chosen)}

        def span(level):
            h = LEVELS[level]
            n = T if T % (2 * h) == 0 else SEQ
            v = b[:, :, 0:n].rearrange("p g (n a h) -> p g n a h", a=2, h=h)
            d = e[:, level % 2, :, 0:n].rearrange("p g (n a h) -> p g n a h", a=2, h=h)
            edge = v[:, :, :, 0, h - 1:h].broadcast_to([P, H, n // (2 * h), h])
            return n, v, d, edge

        with m.block() as block:

            @block.tensor
            def _(pe):
                for level in range(L + 1):
                    if level < L:
                        pe.wait_ge(q_made.sem, base[q_made] + level + 1)
                        pe.wait_ge(k_made.sem, base[k_made] + level + 1)
                        n, lhs, rhs = span(level)[0], ke[:, level % 2, :, :], qe[:, level % 2, :, :]
                    else:
                        n, lhs, rhs = T, k, q
                    if level >= 2:
                        pe.wait_ge(chosen.sem, base[chosen] + 3 * (level - 1))
                    for j, (t0, tn) in enumerate(tiles):
                        if t0 >= n:
                            continue
                        for h in range(H):
                            mm = pe.matmul(m.ps[0:tn, 4 * (level % 2) + j, h * tn:(h + 1) * tn],
                                           lhs[:, h, t0:t0 + tn], rhs[:, h, t0:t0 + tn], start=True, stop=True)
                    paired.on(mm)

            @block.vector
            def _(dve):
                def diff(level):
                    n, v, d, edge = span(level)
                    if level >= 2:
                        dve.wait_ge(q_made.sem, base[q_made] + level - 1)
                        dve.wait_ge(k_made.sem, base[k_made] + level - 1)
                    diff_q.on(dve.tensor_tensor(d[:, :, :, 1, :], v[:, :, :, 1, :], edge, ALU.subtract))

                def choose(level):
                    n = T if level == L else span(level)[0]
                    dve.wait_ge(paired.sem, base[paired] + level + 1)
                    if level == 0:
                        dve.wait_ge(cleared.sem, cleared.n + 2)
                    else:
                        dve.wait_ge(chosen.sem, base[chosen] + 3 * level)
                    for j in range(3):
                        if j < len(tiles) and tiles[j][0] < n:
                            tn = tiles[j][1]
                            dst = a[:, j, :, :] if j < 2 else a_tail[:, :, :]
                            mask = m.masks[0:tn, level:level + 1, 0:tn].broadcast_to([tn, H, tn])
                            src = m.ps[0:tn, 4 * (level % 2) + j, 0:H * tn].rearrange("p (h t) -> p h t", h=H)
                            chosen.on(dve.copy_predicated(dst, mask, src))
                        else:
                            chosen.on(dve.engine_nop())

                diff(0)
                for level in range(L):
                    if level + 1 < L:
                        diff(level + 1)
                    n = span(level)[0]
                    dve.wait_ge(exped.sem, base[exped] + level + 1)
                    if level >= 2:
                        dve.wait_ge(paired.sem, base[paired] + level - 1)
                    q_made.on(dve.tensor_tensor(qe[:, level % 2, :, 0:n], q[:, :, 0:n], e[:, level % 2, :, 0:n],
                                                ALU.mult))
                    if level >= 1:
                        choose(level - 1)
                choose(L - 1)
                choose(L)

            @block.gpsimd
            def _(pool):
                cleared.on(pool.memset(a[:, :, :, :], 0.0))
                cleared.on(pool.memset(a_tail[:, :, :], 0.0))

                def diff(level):
                    n, v, d, edge = span(level)
                    if level >= 2:
                        pool.wait_ge(q_made.sem, base[q_made] + level - 1)
                        pool.wait_ge(k_made.sem, base[k_made] + level - 1)
                    diff_k.on(pool.tensor_tensor(d[:, :, :, 0, :], edge, v[:, :, :, 0, :], ALU.subtract))

                diff(0)
                for level in range(L):
                    if level + 1 < L:
                        diff(level + 1)
                    n = span(level)[0]
                    pool.wait_ge(exped.sem, base[exped] + level + 1)
                    if level >= 2:
                        pool.wait_ge(paired.sem, base[paired] + level - 1)
                    k_made.on(pool.tensor_tensor(ke[:, level % 2, :, 0:n], k[:, :, 0:n], e[:, level % 2, :, 0:n],
                                                 ALU.mult))
                pool.wait_ge(k_made.sem, k_made.n)

            @block.scalar
            def _(act):
                for level in range(L):
                    n = span(level)[0]
                    act.wait_ge(diff_q.sem, base[diff_q] + level + 1)
                    act.wait_ge(diff_k.sem, base[diff_k] + level + 1)
                    exped.on(act.activation(e[:, level % 2, :, 0:n], e[:, level % 2, :, 0:n], ACT.Exp))

        a_next = m.sb(f"{name}_a_next", [P, H, P], ctx=scope)
        a_last = m.sb(f"{name}_a_last", [P, 2, H, 16], ctx=scope)
        kx, qx, kx_far = ke[:, 0, :, :], qe[:, 0, :, :], ke[:, 1, :, 0:P]
        far = m.sb(f"{name}_far", [P, H], ctx=scope)
        n_early = P * (len(tiles) - 1)
        n_late = T - P
        three = len(tiles) == 3
        base = {s: s.n for s in (exped, q_made, k_made, paired, chosen)}
        with m.block() as block:

            @block.scalar
            def _(act):
                exped.on(act.activation(e[:, 1, :, 0:n_late], b[:, :, P:T], ACT.Exp))
                for i in range(len(tiles) - 1):
                    for h in range(H):
                        exped.on(act.activation(e[:, 0, h, i * P:(i + 1) * P], b[:, h, i * P:(i + 1) * P], ACT.Exp,
                                                bias=b[:, h, (i + 1) * P - 1:(i + 1) * P], scale=-1.0))
                if three:
                    exped.on(act.activation(far[:, :], b[:, :, 2 * P - 1], ACT.Exp))

            @block.vector
            def _(dve):
                dve.wait_ge(exped.sem, base[exped] + 1)
                q_made.on(dve.tensor_tensor(qx[:, :, 0:n_late], q[:, :, P:T], e[:, 1, :, 0:n_late], ALU.mult))
                dve.wait_ge(exped.sem, base[exped] + 1 + H * (len(tiles) - 1) + three)
                k_made.on(dve.tensor_tensor(kx[:, :, 0:n_early], k[:, :, 0:n_early], e[:, 0, :, 0:n_early], ALU.mult))
                if three:
                    dve.wait_ge(k_made.sem, k_made.n)
                    k_made.on(dve.tensor_tensor(kx_far, kx[:, :, 0:P],
                                                far[:, :].rearrange("p (h a) -> p h a", a=1).broadcast_to([P, H, P]),
                                                ALU.mult))
                dve.wait_ge(paired.sem, base[paired] + 1)
                chosen.on(dve.tensor_copy(a_next[:, :, :].rearrange("p h t -> p (h t)"), m.ps[:, 0, :]))
                if three:
                    chosen.on(dve.tensor_copy(a_last[:, :, :, :].rearrange("p i h t -> p (i h t)"),
                                              m.ps[:, 1, 0:2 * H * 16]))
                for g in range(len(tiles) * dv_chunks):
                    j, c = g // dv_chunks, g % dv_chunks
                    t0, tn = tiles[j]
                    dve.wait_ge(paired.sem, base[paired] + 2 + g)
                    dst = out[:, out0:out0 + H * dv_chunks, t0:t0 + tn]
                    dst = dst.rearrange("p (h c) t -> p h c t", c=dv_chunks)[:, :, c, :]
                    chosen.on(dve.tensor_copy(dst, m.ps[:, OUT_BANKS[g], 0:H * tn].rearrange("p (h t) -> p h t", h=H)))

            @block.tensor
            def _(pe):
                pe.wait_ge(q_made.sem, base[q_made] + 1)
                pe.wait_ge(k_made.sem, base[k_made] + 1 + three)
                for h in range(H):
                    mm = pe.matmul(m.ps[:, 0, h * P:(h + 1) * P], kx[:, h, 0:P], qx[:, h, 0:P], start=True, stop=True)
                if three:
                    for h in range(H):
                        pe.matmul(m.ps[:, 1, h * 16:(h + 1) * 16], kx_far[:, h, :], qx[:, h, P:P + 16],
                                  start=True, stop=True)
                        mm = pe.matmul(m.ps[:, 1, (H + h) * 16:(H + h + 1) * 16], kx[:, h, P:2 * P],
                                       qx[:, h, P:P + 16], start=True, stop=True)
                paired.on(mm)
                pe.wait_ge(chosen.sem, base[chosen] + 1 + three)
                for g in range(len(tiles) * dv_chunks):
                    j, c = g // dv_chunks, g % dv_chunks
                    tn = tiles[j][1]
                    for h in range(H):
                        for i in range(j + 1):
                            sn = tiles[i][1]
                            if i == j:
                                pairs = a[:, j, h, :] if j < 2 else a_tail[:, h, :]
                            else:
                                pairs = a_next[:, h, :] if j == 1 else a_last[:, i, h, :]
                            col = v0 + (h * dv_chunks + c) * P
                            mm = pe.matmul(m.ps[:, OUT_BANKS[g], h * tn:(h + 1) * tn], v_tokens[0:sn, i, col:col + P],
                                           pairs, start=i == 0, stop=i == j)
                    paired.on(mm)


def gla(m, dram, proj, gates, v_tokens, scope):
    H = GLA_HEADS
    b = m.sb("gla_log_decay", [P, H, T1], ctx=scope)
    steps, made, logs = m.sig("gla_steps"), m.sig("gla_gate_logits"), m.sig("gla_logs")
    base = {s: s.n for s in (steps, made, logs)}
    bias = column(m, "b_gate")
    with ExitStack() as inner:
        up = m.sb("gla_gate_up", [16, H * P], ctx=inner)
        size = m.sb("gla_gate_size", [P, H, T1], ctx=inner)
        loaded = m.sig("gla_gate_up_loaded")
        with m.block() as block:

            @block.sync
            def _(sp):
                loaded.on(sp.dma_start(up[:, :], dram["w_gate_up"][0]), 16)

            @block.tensor
            def _(pe):
                pe.wait_ge(loaded.sem, 16)
                for h in range(H):
                    made.on(pe.matmul(m.ps[:, h, 0:T1], up[:, h * P:(h + 1) * P], proj[0:16, 16, :],
                                      start=True, stop=True))

            @block.vector
            def _(dve):
                for h in range(H):
                    dve.wait_ge(made.sem, base[made] + h + 1)
                    steps.on(dve.tensor_scalar(b[:, h, :], m.ps[:, h, 0:T1], bias[:, h:h + 1], None, ALU.add))
                dve.wait_ge(steps.sem, base[steps] + 4)
                steps.on(dve.scalar_tensor_tensor(size[:, :, :], b[:, :, :], -1.0, b[:, :, :], ALU.mult, ALU.max))
                dve.wait_ge(logs.sem, base[logs] + 2)
                steps.on(dve.scalar_tensor_tensor(b[:, :, :], b[:, :, :], 0.0, size[:, :, :], ALU.min, ALU.subtract))
                dve.wait_ge(steps.sem, base[steps] + 6)
                steps.on(dve.tensor_scalar(b[:, :, :], b[:, :, :], 1.0 / GLA_TAU, None, ALU.mult))
                dve.wait_ge(steps.sem, base[steps] + 7)
                steps.on(dve.tensor_scalar(proj[:, 0:H, :], proj[:, 0:H, :], float(P) ** -0.5, None, ALU.mult))
                running_sums(dve, m, b, H, TILES, steps)

            @block.scalar
            def _(act):
                act.wait_ge(steps.sem, base[steps] + 5)
                logs.on(act.activation(size[:, :, :], size[:, :, :], ACT.Exp, scale=-1.0))
                act.wait_ge(logs.sem, base[logs] + 1)
                logs.on(act.activation(size[:, :, :], size[:, :, :], ACT.Ln, bias=1.0))
    decay_attention(m, "gla", proj[:, 0:H, :], proj[:, H:2 * H, :], b, T1, v_tokens, 0, 2, proj, 8)


def running_sums(dve, m, b, heads, tiles, steps):
    for h in range(heads):
        for t0, n in tiles:
            steps.on(dve.tensor_tensor_scan(b[:, h, t0:t0 + n], m.ones[:, 0:n], b[:, h, t0:t0 + n], 0.0,
                                            ALU.mult, ALU.add))


def norm_heads(m, name, o, per_head, eps, gain, gates):
    squared, summed, scaled = m.sig("head_squares"), m.sig("head_sums"), m.sig("head_norm_steps")
    rooted, gated = m.sig("head_roots"), m.sig("head_gates")
    base = {s: s.n for s in (squared, summed, scaled, rooted, gated)}
    chunks, T = o.shape[1], o.shape[2]
    heads = chunks // per_head
    cols = gain.shape[1]
    with ExitStack() as scope:
        sq = m.sb(f"{name}_head_squares", [P, chunks, T], ctx=scope)
        inv = m.sb(f"{name}_head_rstd", [P, heads, T], ctx=scope)
        with m.block() as block:

            @block.scalar
            def _(act):
                for h in range(heads):
                    part = slice(h * per_head, (h + 1) * per_head)
                    squared.on(act.activation(sq[:, part, :], o[:, part, :], ACT.Square))
                for h in range(0, heads, 2):
                    act.wait_ge(scaled.sem, base[scaled] + h + 2)
                    rooted.on(act.activation(inv[:, h:h + 2, :], inv[:, h:h + 2, :], ACT.Sqrt))
                for c in range(0, chunks, 2):
                    gated.on(act.activation(gates[:, c:c + 2, :], gates[:, c:c + 2, :], ACT.Silu))

            @block.tensor
            def _(pe):
                for h in range(heads):
                    pe.wait_ge(squared.sem, base[squared] + h + 1)
                    for c in range(per_head):
                        mm = pe.matmul(m.ps[:, h, 0:T], m.ones[:, :], sq[:, h * per_head + c, :], start=c == 0,
                                       stop=c == per_head - 1)
                    summed.on(mm)

            @block.vector
            def _(dve):
                for h in range(heads):
                    dve.wait_ge(summed.sem, base[summed] + h + 1)
                    scaled.on(dve.tensor_scalar(inv[:, h, :], m.ps[:, h, 0:T], 1.0 / (per_head * P), eps,
                                                ALU.mult, ALU.add))
                for h in range(0, heads, 2):
                    dve.wait_ge(rooted.sem, base[rooted] + h // 2 + 1)
                    scaled.on(dve.reciprocal(inv[:, h:h + 2, :], inv[:, h:h + 2, :]))
                    dve.wait_ge(scaled.sem, scaled.n)
                    for c in range(h * per_head, (h + 2) * per_head):
                        x = c % cols
                        scaled.on(dve.scalar_tensor_tensor(o[:, c, :], o[:, c, :], gain[:, x:x + 1],
                                                           inv[:, c // per_head, :], ALU.mult, ALU.mult))

            @block.gpsimd
            def _(pool):
                for c in range(0, chunks, 2):
                    pair = c // (2 * per_head)
                    pool.wait_ge(gated.sem, base[gated] + c // 2 + 1)
                    done = heads + (pair + 1) * (1 + 2 * per_head)
                    pool.wait_ge(scaled.sem, base[scaled] + done)
                    m.sig("head_gated").on(pool.tensor_tensor(o[:, c:c + 2, :], o[:, c:c + 2, :],
                                                              gates[:, c:c + 2, :], ALU.mult))
                pool.wait_ge(m.sig("head_gated").sem, m.sig("head_gated").n)


D_RWKV = D // 2
PAIRS = D_RWKV // P
HEAD = 64
CHUNK = 64
RANK = 64
GN_EPS = 64e-5
RMS_EPS = 1e-5
LN_EPS = 1e-5
LB_FLOOR = 1e-30
ALPHA = 2.0 ** 0.25
DECAY = float(np.exp(-0.5))
STEPS = [level for level in reversed(range(len(LEVELS))) if 2 * LEVELS[level] <= CHUNK]


def lane(e):
    return slice(e * HEAD, (e + 1) * HEAD)


class Masks64:

    def __init__(self, m, scope):
        n = len(STEPS)
        self.all = m.sb("masks64", [P, n + 3, CHUNK], ctx=scope)
        self.heads = m.sb("same_head", [P, P], ctx=scope)
        made, filled = m.sig("masks64_made"), m.sig("same_head_made")
        with m.block() as block:

            @block.vector
            def _(dve):
                for x, level in enumerate(STEPS + [None, None, len(LEVELS)]):
                    if level is None:
                        continue
                    for e in range(2):
                        made.on(dve.tensor_copy(self.all[lane(e), x, :], m.masks[lane(e), level, lane(e)]))

            @block.gpsimd
            def _(pool):
                filled.on(pool.memset(self.all[:, n:n + 2, :], 1.0))
                filled.on(pool.memset(self.heads[:, :], 0.0))
                pool.wait_ge(filled.sem, filled.n)
                filled.on(pool.memset(self.heads[lane(0), lane(0)], 1.0))
                filled.on(pool.memset(self.heads[lane(1), lane(1)], 1.0))
                pool.wait_ge(filled.sem, filled.n)
                for e in range(2):
                    for x, bound in ((n, -1), (n + 1, 0)):
                        view = self.all[lane(e), x, :]
                        filled.on(pool.affine_select(out=view, in_=view, compare_op=ALU.is_ge, fill=0.0, base=bound,
                                                     pattern=[[1, CHUNK]], channel_multiplier=-1))
                pool.wait_ge(filled.sem, filled.n)
        self.strict, self.causal, self.equal = n, n + 1, n + 2

    def wide(self, x):
        return self.all[:, x:x + 1, :].broadcast_to([P, PAIRS, CHUNK])


def head_sums(pe, m, reducer, x, first_bank, summed):
    for g in range(PAIRS // 2):
        summed.on(pe.matmul(m.ps[:, first_bank + g, :], reducer, x[:, 2 * g:2 * g + 2, :], start=True, stop=True))


def sums_view(m, first_bank):
    return m.ps[:, first_bank:first_bank + PAIRS // 2, :]


def halves(x):
    return x.rearrange("p (g a) t -> p g (a t)", a=2)


def wide_column(col):
    return col.rearrange("p (c a) -> p c a", a=1).broadcast_to([P, PAIRS, SEQ])


def rwkv_vectors(m, dram, proj, masks, sums, alpha, beta, bonus, tmp):
    col = {n: column(m, n + "_2") for n in ("w_decay0", "a0", "k_k", "k_a", "r_k")}
    loaded, tanhed = m.sig("lora_loaded"), m.sig("lora_tanh")
    made, gated, steps = m.sig("lora_made"), m.sig("rwkv_gates"), m.sig("rwkv_steps")
    summed, act_steps = m.sig("rwkv_head_sums"), m.sig("rwkv_act_steps")
    r, k, v = proj[:, 0:PAIRS, :], proj[:, PAIRS:2 * PAIRS, :], proj[:, 2 * PAIRS:3 * PAIRS, :]
    with ExitStack() as scope:
        up = m.sb("lora_up", [P, D_RWKV], ctx=scope)
        small = m.sb("rwkv_small", [P, PAIRS], ctx=scope)
        base = {s: s.n for s in (made, gated, steps, summed, act_steps)}
        with m.block() as block:

            @block.sync
            def _(sp):
                loaded.on(sp.dma_start(up[lane(0), :], dram["w_decay_up_2"][0]), 16)
                loaded.on(sp.dma_start(up[lane(1), :], dram["a_up_2"][0]), 16)

            @block.scalar
            def _(act):
                tanhed.on(act.activation(proj[lane(0), 32, :], proj[lane(0), 32, :], ACT.Tanh))
                for x in range(2 * PAIRS):
                    c, dst, bias = x // 2, (sums, beta)[x % 2], (col["w_decay0"], col["a0"])[x % 2]
                    act.wait_ge(made.sem, base[made] + x + 1)
                    gated.on(act.activation(dst[:, c, :], m.ps[:, x % 4, 0:SEQ], ACT.Sigmoid, bias=bias[:, c:c + 1]))

            @block.tensor
            def _(pe):
                pe.wait_ge(loaded.sem, loaded.n)
                pe.wait_ge(tanhed.sem, tanhed.n)
                for x in range(2 * PAIRS):
                    c, e = x // 2, x % 2
                    if x >= 4:
                        pe.wait_ge(gated.sem, base[gated] + x - 3)
                    made.on(pe.matmul(m.ps[:, x % 4, 0:SEQ], up[lane(e), c * P:(c + 1) * P], proj[lane(e), 32, :],
                                      start=True, stop=True))

            @block.vector
            def _(dve):
                steps.on(dve.tensor_tensor(alpha[:, :, :], k, wide_column(col["k_k"]), ALU.mult))
                dve.wait_ge(steps.sem, base[steps] + 1)
                steps.on(dve.tensor_tensor(tmp[:, :, :], alpha[:, :, :], alpha[:, :, :], ALU.mult))
                steps.on(dve.tensor_scalar(small[:, :], col["k_a"], -1.0, 1.0, ALU.mult, ALU.add))

        base = {s: s.n for s in (steps, summed, act_steps)}
        with m.block() as block:

            @block.tensor
            def _(pe):
                head_sums(pe, m, masks.heads[:, :], tmp, 0, summed)
                pe.wait_ge(steps.sem, base[steps] + 5)
                head_sums(pe, m, masks.heads[:, :], bonus, 4, summed)

            @block.scalar
            def _(act):
                act.wait_ge(summed.sem, base[summed] + 4)
                act_steps.on(act.activation(halves(tmp[:, :, :]), sums_view(m, 0), ACT.Sqrt))

            @block.vector
            def _(dve):
                def step(ins):
                    steps.on(ins)
                    dve.wait_ge(steps.sem, steps.n)

                step(dve.tensor_tensor(bonus[:, :, :], beta[:, :, :], wide_column(col["k_a"]), ALU.mult))
                step(dve.tensor_tensor(bonus[:, :, :], bonus[:, :, :], wide_column(small[:, :]), ALU.add))
                step(dve.tensor_tensor(k, k, bonus[:, :, :], ALU.mult))
                step(dve.tensor_tensor(bonus[:, :, :], r, k, ALU.mult))
                step(dve.tensor_tensor(bonus[:, :, :], bonus[:, :, :], wide_column(col["r_k"]), ALU.mult))
                dve.wait_ge(act_steps.sem, base[act_steps] + 1)
                step(dve.tensor_scalar(tmp[:, :, :], tmp[:, :, :], 1e-12, None, ALU.max))
                step(dve.reciprocal(tmp[:, :, :], tmp[:, :, :]))
                step(dve.tensor_tensor(alpha[:, :, :], alpha[:, :, :], tmp[:, :, :], ALU.mult))
                step(dve.tensor_tensor(beta[:, :, :], beta[:, :, :], alpha[:, :, :], ALU.mult))


def rwkv_decays(m, proj, sums, alpha, beta, bonus, tmp, last):
    steps, act_steps = m.sig("rwkv_steps"), m.sig("rwkv_act_steps")
    r, k, v = proj[:, 0:PAIRS, :], proj[:, PAIRS:2 * PAIRS, :], proj[:, 2 * PAIRS:3 * PAIRS, :]
    base = {s: s.n for s in (steps, act_steps)}
    with m.block() as block:

        @block.vector
        def _(dve):
            steps.on(dve.tensor_copy(tmp[:, :, :], sums[:, :, :]))
            dve.wait_ge(steps.sem, steps.n)
            running_sums(dve, m, sums, PAIRS, [(t, CHUNK) for t in range(0, SEQ, CHUNK)], steps)
            dve.wait_ge(steps.sem, steps.n)
            steps.on(dve.tensor_tensor(tmp[:, :, :], sums[:, :, :], tmp[:, :, :], ALU.subtract))
            exclusive = steps.n
            steps.on(dve.tensor_tensor(halves(bonus[:, :, :]), halves(v), sums_view(m, 4), ALU.mult))
            dve.wait_ge(act_steps.sem, base[act_steps] + 1)
            steps.on(dve.scalar_tensor_tensor(alpha[:, :, :], alpha[:, :, :], -1.0, tmp[:, :, :], ALU.mult, ALU.mult))
            used_alpha = steps.n
            dve.wait_ge(act_steps.sem, base[act_steps] + 2)
            steps.on(dve.tensor_tensor(r, r, tmp[:, :, :], ALU.mult))
            used_r = steps.n
            dve.wait_ge(act_steps.sem, base[act_steps] + 4)
            steps.on(dve.tensor_tensor(k, k, tmp[:, :, :], ALU.mult))
            steps.on(dve.tensor_tensor(beta[:, :, :], beta[:, :, :], tmp[:, :, :], ALU.mult))
            m.marks = (exclusive, used_alpha, used_r)

        @block.scalar
        def _(act):
            exclusive, used_alpha, used_r = m.marks
            act.wait_ge(steps.sem, exclusive)
            act_steps.on(act.activation(tmp[:, :, :], tmp[:, :, :], ACT.Exp, scale=-DECAY))
            act.wait_ge(steps.sem, used_alpha)
            act_steps.on(act.activation(tmp[:, :, :], sums[:, :, :], ACT.Exp, scale=-DECAY))
            act_steps.on(act.activation(last[:, :, :], sums.rearrange("p a (c t) -> p a c t", t=CHUNK)[:, :, :, CHUNK - 1],
                                        ACT.Exp, scale=-DECAY))
            act.wait_ge(steps.sem, used_r)
            act_steps.on(act.activation(tmp[:, :, :], sums[:, :, :], ACT.Exp, scale=DECAY))


class Rwkv:

    def __init__(self, m, scope, proj, last, alpha, beta, masks, out):
        self.m, self.masks, self.last, self.out = m, masks, last, out
        self.r, self.k, self.v = (proj[:, a * PAIRS:(a + 1) * PAIRS, :] for a in range(3))
        self.alpha, self.beta = alpha, beta

        def tile(name, n=2):
            return m.sb(f"rwkv_{name}", [P, n, PAIRS, CHUNK], ctx=scope)

        self.tok = {name: tile(f"{name}_tokens") for name in ("beta", "k", "v")}
        self.lb, self.lk, self.mb, self.mk = (tile(x) for x in ("lb", "lk", "mb", "mk"))
        self.level, self.x, self.xt, self.y = (tile(x) for x in ("level", "x", "xt", "y"))
        self.rhs, self.sa, self.state = (tile(x, 1)[:, 0] for x in ("rhs", "sa", "state"))
        self.fresh = self.rhs

    def flat(self, x):
        return x.rearrange("p a b -> p (a b)")

    def bank(self, b):
        return self.m.ps[:, b, :].rearrange("p (a b) -> p a b", b=CHUNK)

    def heads(self, pe, bank, terms, signal):
        for pair in range(PAIRS):
            for e in range(2):
                for x, (lhs, rhs) in enumerate(terms):
                    mm = pe.matmul(self.bank(bank)[lane(e), pair, :], lhs(e, pair), rhs(e, pair), start=x == 0,
                                   stop=x == len(terms) - 1)
        return signal.on(mm)

    def prepare(self, first):
        m, masks = self.m, self.masks
        made, kept = m.sig("rwkv_products"), m.sig("rwkv_kept")
        copied = m.sig("rwkv_turned")
        ident = m.ident

        def part(x, c):
            t0 = (first + c) * CHUNK
            return lambda e, p: x[lane(e), p, t0:t0 + CHUNK]

        def held(x, c):
            return lambda e, p: x[lane(e), c, p, :]

        def unit(e, p):
            return ident[lane(e), lane(e)]

        jobs = []
        for c in range(2):
            jobs += [((part(self.beta, c), part(self.alpha, c)), self.lb[:, c], masks.strict),
                     ((part(self.k, c), part(self.alpha, c)), self.lk[:, c], masks.strict),
                     ((part(self.beta, c), part(self.r, c)), self.mb[:, c], masks.causal),
                     ((part(self.k, c), part(self.r, c)), self.mk[:, c], masks.causal),
                     ((part(self.beta, c), unit), self.tok["beta"][:, c], None),
                     ((part(self.k, c), unit), self.tok["k"][:, c], None),
                     ((part(self.v, c), unit), self.tok["v"][:, c], None)]
        masked = [x for x, job in enumerate(jobs) if job[2] is not None]
        plain = [x for x, job in enumerate(jobs) if job[2] is None]
        base = {s: s.n for s in (made, kept, copied)}
        with m.block() as block:

            @block.tensor
            def _(pe):
                for x, (term, _, mask) in enumerate(jobs):
                    if x >= 8:
                        if jobs[x - 8][2] is not None:
                            pe.wait_ge(kept.sem, base[kept] + masked.index(x - 8) + 1)
                        else:
                            pe.wait_ge(copied.sem, base[copied] + plain.index(x - 8) + 1)
                    self.heads(pe, x % 8, [term], made)

            @block.vector
            def _(dve):
                for x in masked:
                    dve.wait_ge(made.sem, base[made] + x + 1)
                    kept.on(dve.tensor_tensor(jobs[x][1], self.bank(x % 8), masks.wide(jobs[x][2]), ALU.mult))

            @block.scalar
            def _(act):
                for x in plain:
                    act.wait_ge(made.sem, base[made] + x + 1)
                    copied.on(act.activation(jobs[x][1], self.bank(x % 8), ACT.Copy))

        levelled, y_made, y_kept = m.sig("inverse_levels"), m.sig("inverse_y_made"), m.sig("inverse_y_kept")
        grown, x_kept = m.sig("inverse_grown"), m.sig("inverse_kept")
        base = {s: s.n for s in (levelled, y_made, y_kept, grown, x_kept)}
        last = len(STEPS) - 1
        with m.block() as block:

            @block.gpsimd
            def _(pool):
                for s in range(len(STEPS)):
                    for c in range(2):
                        if s >= 1:
                            pool.wait_ge(y_made.sem, base[y_made] + 2 * (s - 1) + c + 1)
                        if s == 1:
                            pool.wait_ge(x_kept.sem, base[x_kept] + 2 * c + 2)
                        levelled.on(pool.tensor_tensor(self.level[:, c], self.lb[:, c], masks.wide(s), ALU.mult))
                pool.wait_ge(levelled.sem, levelled.n)

            @block.tensor
            def _(pe):
                for s in range(len(STEPS)):
                    for c in range(2):
                        pe.wait_ge(levelled.sem, base[levelled] + 2 * s + c + 1)
                        rhs = unit if s == 0 else held(self.x, c)
                        if s >= 1:
                            pe.wait_ge(x_kept.sem, base[x_kept] + 4 * (s - 1) + 2 * c + 2)
                        self.heads(pe, c, [(held(self.level, c), rhs)], y_made)
                    if s == 0:
                        continue
                    for c in range(2):
                        pe.wait_ge(y_kept.sem, base[y_kept] + 2 * (s - 1) + c + 1)
                        if s < last:
                            self.heads(pe, 2 + 2 * c, [(held(self.xt, c), held(self.y, c))], grown)
                        self.heads(pe, 3 + 2 * c, [(held(self.y, c), held(self.xt, c))], grown)

            @block.scalar
            def _(act):
                for s in range(1, len(STEPS)):
                    for c in range(2):
                        act.wait_ge(y_made.sem, base[y_made] + 2 * s + c + 1)
                        y_kept.on(act.activation(self.y[:, c], self.bank(c), ACT.Copy))

            @block.vector
            def _(dve):
                for c in range(2):
                    dve.wait_ge(y_made.sem, base[y_made] + c + 1)
                    x_kept.on(dve.tensor_tensor(self.x[:, c], self.bank(c), masks.wide(masks.equal), ALU.add))
                    x_kept.on(dve.tensor_tensor(self.xt[:, c], self.level[:, c], masks.wide(masks.equal), ALU.add))
                n = base[grown]
                for s in range(1, len(STEPS)):
                    for c in range(2):
                        n += 1 if s == last else 2
                        dve.wait_ge(grown.sem, n)
                        if s < last:
                            x_kept.on(dve.tensor_tensor(self.x[:, c], self.bank(2 + 2 * c), self.x[:, c], ALU.add))
                        else:
                            x_kept.on(dve.engine_nop())
                        x_kept.on(dve.tensor_tensor(self.xt[:, c], self.bank(3 + 2 * c), self.xt[:, c], ALU.add))

    def scan(self, first):
        m = self.m
        made, kept, advanced = m.sig("scan_products"), m.sig("scan_kept"), m.sig("scan_states")
        stored = m.sig("scan_outputs")
        base = {s: s.n for s in (made, kept, advanced, stored)}

        def held(x, c):
            return lambda e, p: x[lane(e), c, p, :]

        def alone(x):
            return lambda e, p: x[lane(e), p, :]

        def part(x, c):
            t0 = (first + c) * CHUNK
            return lambda e, p: x[lane(e), p, t0:t0 + CHUNK]

        with m.block() as block:

            @block.tensor
            def _(pe):
                for c in range(2):
                    if c:
                        pe.wait_ge(advanced.sem, base[advanced] + 2 * c)
                    self.heads(pe, 0, [(part(self.alpha, c), alone(self.state)),
                                       (held(self.lk, c), held(self.tok["v"], c))], made)
                    pe.wait_ge(kept.sem, base[kept] + 2 * c + 1)
                    self.heads(pe, 1, [(held(self.xt, c), alone(self.rhs))], made)
                    pe.wait_ge(kept.sem, base[kept] + 2 * c + 2)
                    self.heads(pe, 2, [(held(self.tok["beta"], c), alone(self.sa)),
                                       (held(self.tok["k"], c), held(self.tok["v"], c))], made)
                    self.heads(pe, 3 + c, [(alone(self.state), part(self.r, c)),
                                           (alone(self.sa), held(self.mb, c)),
                                           (held(self.tok["v"], c), held(self.mk, c))], made)

            @block.scalar
            def _(act):
                for c in range(2):
                    act.wait_ge(made.sem, base[made] + 4 * c + 1)
                    kept.on(act.activation(self.rhs, self.bank(0), ACT.Copy))
                    act.wait_ge(made.sem, base[made] + 4 * c + 2)
                    kept.on(act.activation(self.sa, self.bank(1), ACT.Copy))
                    act.wait_ge(made.sem, base[made] + 4 * c + 4)
                    t0 = (first + c) * CHUNK
                    stored.on(act.activation(self.out[:, :, t0:t0 + CHUNK], self.bank(3 + c), ACT.Copy))

            @block.vector
            def _(dve):
                for c in range(2):
                    dve.wait_ge(made.sem, base[made] + 4 * c + 3)
                    advanced.on(dve.tensor_tensor(self.fresh, self.bank(2), self.state, ALU.add))
                    dve.wait_ge(advanced.sem, base[advanced] + 2 * c + 1)
                    dve.wait_ge(made.sem, base[made] + 4 * c + 4)
                    decay = self.last[:, :, first + c:first + c + 1].broadcast_to([P, PAIRS, CHUNK])
                    advanced.on(dve.tensor_tensor(self.state, self.fresh, decay, ALU.mult))

    def start(self):
        m = self.m
        cleared = m.sig("state_cleared")
        with m.block() as block:

            @block.vector
            def _(dve):
                cleared.on(dve.memset(self.state, 0.0))


def rwkv_finish(m, masks, o, bonus, z, out):
    gn_w, gn_b = column(m, "ln_x_w_2"), column(m, "ln_x_b_2")
    summed, steps, act_steps = m.sig("rwkv_head_sums"), m.sig("rwkv_steps"), m.sig("rwkv_act_steps")
    base = {s: s.n for s in (summed, steps, act_steps)}
    with ExitStack() as scope:
        sq = m.sb("gn_squares", [P, PAIRS, SEQ], ctx=scope)
        with m.block() as block:

            @block.tensor
            def _(pe):
                head_sums(pe, m, masks.heads[:, :], o, 0, summed)
                pe.wait_ge(act_steps.sem, base[act_steps] + 2)
                head_sums(pe, m, masks.heads[:, :], sq, 4, summed)

            @block.scalar
            def _(act):
                act_steps.on(act.activation(z, z, ACT.Silu))
                act.wait_ge(steps.sem, base[steps] + 1)
                act_steps.on(act.activation(sq[:, :, :], o, ACT.Square))
                act.wait_ge(steps.sem, base[steps] + 2)
                act_steps.on(act.activation(sq[:, :, :], sq[:, :, :], ACT.Sqrt))

            @block.vector
            def _(dve):
                dve.wait_ge(summed.sem, base[summed] + 4)
                steps.on(dve.scalar_tensor_tensor(halves(o), sums_view(m, 0), -1.0 / HEAD, halves(o), ALU.mult,
                                                  ALU.add))
                dve.wait_ge(summed.sem, base[summed] + 8)
                steps.on(dve.tensor_scalar(halves(sq[:, :, :]), sums_view(m, 4), 1.0 / HEAD, GN_EPS, ALU.mult,
                                           ALU.add))
                dve.wait_ge(act_steps.sem, base[act_steps] + 3)
                steps.on(dve.reciprocal(sq[:, :, :], sq[:, :, :]))
                dve.wait_ge(steps.sem, steps.n)
                for c in range(PAIRS):
                    steps.on(dve.scalar_tensor_tensor(o[:, c, :], o[:, c, :], gn_w[:, c:c + 1], sq[:, c, :],
                                                      ALU.mult, ALU.mult))
                for c in range(PAIRS):
                    dve.wait_ge(steps.sem, base[steps] + 3 + c + 1)
                    steps.on(dve.scalar_tensor_tensor(o[:, c, :], o[:, c, :], gn_b[:, c:c + 1], bonus[:, c, :],
                                                      ALU.add, ALU.add))
                dve.wait_ge(steps.sem, steps.n)
                steps.on(dve.tensor_tensor(out, o, z, ALU.mult))


def hgrn_gates(m, proj, b, scope):
    logits = column(m, "lb_logits_2")
    steps, act_steps = m.sig("hgrn_steps"), m.sig("hgrn_act_steps")
    f = proj[:, 8:16, :]
    with ExitStack() as inner:
        bound = m.sb("hgrn_bound", [P, 6, PAIRS], ctx=inner)
        size = m.sb("hgrn_size", [P, PAIRS, SEQ], ctx=inner)
        share, lower, log_lower, log_rest, rest = (bound[:, x, :] for x in range(5))
        marks = {}
        with m.block() as block:

            @block.vector
            def _(dve):
                def step(ins, name=None):
                    steps.on(ins)
                    marks[name] = steps.n

                def settled():
                    dve.wait_ge(steps.sem, steps.n)

                def after(n):
                    dve.wait_ge(act_steps.sem, n)

                step(dve.tensor_tensor(share, logits, logits, ALU.subtract), "centred")
                step(dve.scalar_tensor_tensor(size[:, :, :], f, -1.0, f, ALU.mult, ALU.max), "size")
                after(1)
                step(dve.reciprocal(lower, share))
                settled()
                step(dve.tensor_tensor(share, share, lower, ALU.mult))
                settled()
                step(dve.tensor_tensor(lower, share, share, ALU.subtract))
                settled()
                step(dve.tensor_scalar(rest, lower, -1.0, 1.0, ALU.mult, ALU.add))
                step(dve.tensor_scalar(log_lower, lower, LB_FLOOR, None, ALU.max), "floored")
                after(3)
                step(dve.tensor_scalar(log_lower, log_lower, -60.0 * float(np.log(2.0)), None, ALU.add))
                after(5)
                step(dve.scalar_tensor_tensor(b, f, 0.0, size[:, :, :], ALU.min, ALU.subtract))
                settled()
                step(dve.tensor_tensor(b, b, wide_column(log_rest), ALU.add))
                settled()
                step(dve.tensor_tensor(size[:, :, :], b, wide_column(log_lower), ALU.subtract))
                settled()
                step(dve.scalar_tensor_tensor(size[:, :, :], size[:, :, :], -1.0, size[:, :, :], ALU.mult, ALU.min),
                     "difference")
                step(dve.tensor_tensor(b, b, wide_column(log_lower), ALU.max))
                settled()
                after(7)
                step(dve.tensor_tensor(b, b, size[:, :, :], ALU.add))
                settled()
                running_sums(dve, m, b, PAIRS, TILES[0:2], steps)
                after(8)
                step(dve.tensor_tensor(f, f, wide_column(rest), ALU.mult))

            @block.scalar
            def _(act):
                def step(ins):
                    act_steps.on(ins)

                act.wait_ge(steps.sem, marks["centred"])
                step(act.activation(share, share, ACT.Exp))
                act.wait_ge(steps.sem, marks["size"])
                step(act.activation(size[:, :, :], size[:, :, :], ACT.Exp, scale=-1.0))
                act.wait_ge(steps.sem, marks["floored"])
                step(act.activation(log_lower, log_lower, ACT.Ln, scale=2.0 ** 60))
                step(act.activation(log_rest, rest, ACT.Ln))
                act.wait_ge(act_steps.sem, 2)
                step(act.activation(size[:, :, :], size[:, :, :], ACT.Ln, bias=1.0))
                act.wait_ge(steps.sem, marks["difference"])
                step(act.activation(size[:, :, :], size[:, :, :], ACT.Exp))
                act.wait_ge(act_steps.sem, 6)
                step(act.activation(size[:, :, :], size[:, :, :], ACT.Ln, bias=1.0))
                step(act.activation(f, f, ACT.Sigmoid, scale=-1.0))
                step(act.activation(proj[:, 0:8, :], proj[:, 0:8, :], ACT.Silu))


def layer_norm_out(m, y, out):
    w, b = column(m, "ln_w_2"), column(m, "ln_b_2")
    added, squared, summed = m.sig("ln_added"), m.sig("ln_squared"), m.sig("ln_sums")
    steps, rooted, normed, biased = m.sig("ln_steps"), m.sig("ln_rooted"), m.sig("ln_normed"), m.sig("ln_biased")
    turned, copied, stored = m.sig("out_turned"), m.sig("out_copied"), m.sig("stored")
    centred = m.sig("ln_centred")
    T = SEQ
    with ExitStack() as scope:
        sq = m.sb("ln_squares", [P, DC, T], ctx=scope)
        stats = m.sb("ln_stats", [P, 2, T], ctx=scope)
        mean, rstd = stats[:, 0, :], stats[:, 1, :]
        with m.block() as block:

            @block.vector
            def _(dve):
                for c in range(DC):
                    added.on(dve.scalar_tensor_tensor(y[:, c, :], m.r[:, c, N_META:T1], ALPHA, y[:, c, :], ALU.mult,
                                                      ALU.add))
                dve.wait_ge(summed.sem, 1)
                steps.on(dve.tensor_scalar(mean, m.ps[:, 6, 0:T], 1.0 / D, None, ALU.mult))
                dve.wait_ge(steps.sem, 1)
                for c in range(0, DC, 4):
                    centred.on(dve.tensor_tensor(y[:, c:c + 4, :], y[:, c:c + 4, :],
                                                 stats[:, 0:1, :].broadcast_to([P, 4, T]), ALU.subtract))
                dve.wait_ge(summed.sem, 2)
                steps.on(dve.tensor_scalar(rstd, m.ps[:, 7, 0:T], 1.0 / D, LN_EPS, ALU.mult, ALU.add))
                dve.wait_ge(rooted.sem, 1)
                steps.on(dve.reciprocal(rstd, rstd))
                dve.wait_ge(steps.sem, 3)
                for c in range(DC):
                    normed.on(dve.scalar_tensor_tensor(y[:, c, :], y[:, c, :], w[:, c:c + 1], rstd, ALU.mult,
                                                       ALU.mult))

            @block.scalar
            def _(act):
                for c in range(0, DC, 4):
                    act.wait_ge(centred.sem, c // 4 + 1)
                    squared.on(act.activation(sq[:, c:c + 4, :], y[:, c:c + 4, :], ACT.Square))
                act.wait_ge(steps.sem, 2)
                rooted.on(act.activation(rstd, rstd, ACT.Sqrt))
                for c in range(DC):
                    act.wait_ge(normed.sem, c + 1)
                    biased.on(act.activation(y[:, c, :], y[:, c, :], ACT.Identity, bias=b[:, c:c + 1]))

            @block.tensor
            def _(pe):
                for c in range(DC):
                    pe.wait_ge(added.sem, c + 1)
                    mm = pe.matmul(m.ps[:, 6, 0:T], m.ones[:, :], y[:, c, :], start=c == 0, stop=c == DC - 1)
                summed.on(mm)
                for c in range(DC):
                    if c % 4 == 0:
                        pe.wait_ge(squared.sem, c // 4 + 1)
                    mm = pe.matmul(m.ps[:, 7, 0:T], m.ones[:, :], sq[:, c, :], start=c == 0, stop=c == DC - 1)
                summed.on(mm)

        rows = sq[:, :, :].rearrange("p (j a) t -> p j (a t)", j=2)
        with m.block() as block:

            @block.tensor
            def _(pe):
                for g in range(8):
                    j, c0 = g % 2, 4 * (g // 2)
                    for c in range(4):
                        mm = pe.transpose(m.ps[:, g, c * P:(c + 1) * P], y[:, c0 + c, j * P:(j + 1) * P],
                                          m.ident[:, :])
                    turned.on(mm)

            @block.vector
            def _(dve):
                for g in range(8):
                    j, c0 = g % 2, 4 * (g // 2)
                    dve.wait_ge(turned.sem, g + 1)
                    copied.on(dve.tensor_copy(rows[:, j, c0 * P:(c0 + 4) * P], m.ps[:, g, :]))

            @block.sync
            def _(sp):
                for g in range(8):
                    j, c0 = g % 2, 4 * (g // 2)
                    sp.wait_ge(copied.sem, g + 1)
                    stored.on(sp.dma_start(out[0, j * P:(j + 1) * P, c0 * P:(c0 + 4) * P],
                                           rows[:, j, c0 * P:(c0 + 4) * P]), 16)
                sp.wait_ge(stored.sem, stored.n)


VECTORS = [
    [("ffn1_pre_g", DC), ("ffn1_post_g", DC), ("mix_pre_g", DC), ("mix_post_g", DC), ("ffn2_pre_g", DC),
     ("ffn2_post_g", DC), ("b_gate", GLA_HEADS), ("gla_norm_g", GLA_DV // P)],
    [("shift_mu_2", 33), ("w_decay0_2", 8), ("a0_2", 8), ("k_k_2", 8), ("k_a_2", 8), ("r_k_2", 8),
     ("ln_x_w_2", 8), ("ln_x_b_2", 8), ("lb_logits_2", 8), ("g_norm_w_2", 8)],
    [("ln_w_2", DC), ("ln_b_2", DC)],
]


def set_up(m, dram, first):
    made, loaded = m.sig("constants_made"), m.sig("tokens_loaded")
    params_loaded, turned, copied = m.sig("params_loaded"), m.sig("tokens_turned"), m.sig("turned_copied")
    halved = m.sig("gains_halved")
    loaded0 = loaded.n
    with ExitStack() as scope:
        tokens = m.sb("tokens", [P, 3, D], ctx=scope)
        rows = m.sb("param_rows", [P, 3, P], ctx=scope)
        with m.block() as block:

            @block.sync
            def _(sp):
                head = P - N_META
                meta, x = dram["meta_tokens"], dram["x"][0]
                loaded.on(sp.dma_start(tokens[0:N_META, 0, :], meta), 16)
                loaded.on(sp.dma_start(tokens[N_META:P, 0, :], x[0:head, :]), 16)
                loaded.on(sp.dma_start(tokens[:, 1, :], x[head:head + P, :]), 16)
                loaded.on(sp.dma_start(tokens[0:16, 2, :], x[head + P:SEQ, :]), 16)
                for k in range(RAW):
                    load_unit(m, sp, k, first, k, k)

            @block.scalar
            def _(act):
                act.wait_ge(made.sem, 1)
                for j, group in enumerate(VECTORS):
                    row = 0
                    for name, count in group:
                        src = dram[name][0].rearrange("(r c) -> r c", c=P)
                        params_loaded.on(act.dma_start(rows[row:row + count, j, :], src), 16)
                        m.param[name] = (j, row, count)
                        row += count

            @block.gpsimd
            def _(pool):
                made.on(pool.memset(rows[:, :, :], 0.0))
                made.on(pool.memset(m.ident[:, :], 0.0))
                made.on(pool.memset(m.ones[:, :], 1.0))
                made.on(pool.memset(m.zero[:, :], 0.0))
                pool.wait_ge(made.sem, 3)
                made.on(pool.affine_select(out=m.ident[:, :], in_=m.ident[:, :], compare_op=ALU.not_equal,
                                           fill=1.0, base=0, pattern=[[-1, P]], channel_multiplier=1))
                pool.wait_ge(made.sem, made.n)
                for _ in range(2):
                    pool.nop().then_inc(m.banks_free, 1)
                    pool.nop().then_inc(m.units_done, 1)
                    pool.nop().then_inc(m.hidden_split, 1)
                    pool.nop().then_inc(m.squares_free, 1)
                    pool.nop().then_inc(m.shift_free, 1)

        ready = loaded.n
        turned0, copied0 = turned.n, copied.n
        with m.block() as block:

            @block.tensor
            def _(pe):
                pe.wait_ge(params_loaded.sem, params_loaded.n)
                for j in range(3):
                    mm = pe.transpose(m.ps[:, 7, j * P:(j + 1) * P], rows[:, j, :], m.ident[:, :])
                turned.on(mm)
                pe.wait_ge(loaded.sem, ready)
                for c in range(DC):
                    if c >= 4:
                        pe.wait_ge(copied.sem, copied0 + c - 4 + 2)
                    for j, (t0, n) in enumerate(TILES):
                        mm = pe.transpose(m.ps[:, c % 4, t0:t0 + n], tokens[0:n, j, c * P:(c + 1) * P],
                                          m.ident[0:n, 0:n])
                    turned.on(mm)

            @block.vector
            def _(dve):
                dve.wait_ge(turned.sem, turned0 + 1)
                copied.on(dve.tensor_copy(m.columns[:, :, :].rearrange("p a b -> p (a b)"),
                                          m.ps[:, 7, 0:3 * P]))
                dve.wait_ge(copied.sem, copied0 + 1)
                for x, name in enumerate(("ffn1_post_g", "ffn2_post_g")):
                    halved.on(dve.tensor_scalar(m.half_gain[:, x, :], column(m, name), 0.5, None, ALU.mult))
                for c in range(DC):
                    dve.wait_ge(turned.sem, turned0 + c + 2)
                    copied.on(dve.tensor_copy(m.r[:, c, :], m.ps[:, c % 4, 0:T1]))


def column(m, name):
    j, row, count = m.param[name]
    return m.columns[:, j, row:row + count]


def build(nc, dram, out):
    with ExitStack() as ctx:
        m = Machine(nc, ctx)
        m.param = {}
        m.ps = ctx.enter_context(nc.psum_tensor("ps", [P, 8, 512], F32))
        m.r = m.sb("residual", [P, DC, T1])
        m.open_x("x")
        m.raw = m.sb("w_raw", [P, RAW, DC * P])
        m.w_hi = m.sb("w_hi", [P, SPLIT, DC * P], F32R)
        m.w_lo = m.sb("w_lo", [P, SPLIT, DC * P], F32R)
        m.ident = m.sb("ident", [P, P])
        m.ones = m.sb("ones", [P, P])
        m.zero = m.sb("zero", [P, 1])
        m.columns = m.sb("param_columns", [P, 3, P])
        m.half_gain = m.sb("half_gain", [P, 2, DC])
        m.rstd, m.rstd_post = m.sb("rstd", [P, T1]), m.sb("rstd_post", [P, T1])
        m.sq, m.acc = m.sb("squares", [P, 2, T1]), m.sb("square_sum", [P, T1])
        m.masks = m.sb("masks", [P, len(LEVELS) + 1, P], U8)

        def sem(name):
            return ctx.enter_context(nc.semaphore(name))

        m.raw_loaded = [sem(f"raw_loaded{i}") for i in range(RAW)]
        m.hi_ready, m.lo_ready = sem("hi_ready"), sem("lo_ready")
        m.units_done = sem("units_done")
        m.banks_free = sem("banks_free")
        m.silu_ready, m.hidden_hi = sem("silu_ready"), sem("hidden_hi")
        m.gate_scaled, m.hidden_ready, m.squared = sem("gate_scaled"), sem("hidden_ready"), sem("squared")
        m.squares_free = sem("squares_free")
        m.differed, m.shift_free = sem("differed"), sem("shift_free")
        m.hidden_split = sem("hidden_split")
        stored = m.sig("stored")

        with ExitStack() as scope:
            set_up(m, dram, ffn_stages(m, dram, "ffn1", T1, None, scope, declare=False)[0])
        w_in, w_out = dram["w_in"][0], dram["w_out"][0]
        def gla_stage(out):
            return Project(m, w_in, 4176, 17, T1, out, m.rstd)

        def gate_stage(out):
            return Project(m, w_in, 4176 + 2064, 8, T1, out, m.rstd)

        def out_stage(out, w, rstd=None):
            return Project(m, w, 0, DC, SEQ, out, rstd=rstd)

        def rwkv_stage(out, differences=None):
            return Shifted(m, w_in_2, 0, 33, SEQ, out, column(m, "shift_mu_2"), differences)

        def hgrn_stage(out):
            return Project(m, w_in_2, 33 * P, 32, SEQ, out)

        w_in_2, w_out_2 = dram["w_in_2"][0], dram["w_out_2"][0]
        every, h = m.r[:, :, :], m.r[:, :, N_META:T1]

        y_scope = ctx.enter_context(ExitStack())
        y = m.sb("ffn1_y", [P, DC, T1], ctx=y_scope, side="right")
        feed = make_feed(m, every, T1, column(m, "ffn1_pre_g"), norm=True)
        with ExitStack() as scope:
            m.masks_full = m.sb("masks_full", [P, len(LEVELS) + 1, P], ctx=scope)
            run_ffn(m, dram, "ffn1", T1, y, feed, Project(m, w_in, 0, 33, T1, None), lambda pool: make_masks(m, pool))

        with ExitStack() as scope:
            proj = m.sb("dsa_proj", [P, 33, T1], ctx=scope)
            feed = make_feed(m, every, T1, column(m, "mix_pre_g"), (y, m.half_gain[:, 0, :], m.rstd_post), True)
            dense(m, Project(m, w_in, 0, 33, T1, proj, m.rstd), gla_stage(None), feed)
            y_scope.close()
            o_dsa_scope = ctx.enter_context(ExitStack())
            o_dsa = m.sb("o_dsa", [P, DSA_HEADS, SEQ], ctx=o_dsa_scope, side="right")
            v_tokens = m.sb("dsa_v_tokens", [P, 3, DSA_HEADS * P], ctx=scope)
            bias = m.sb("dsa_bias", [P, 2, T1], ctx=scope)
            to_tokens(m, proj[:, 16:24, :], DSA_HEADS, TILES, v_tokens, "dsa")
            with ExitStack() as inner:
                scores = m.sb("dsa_scores", [P, 2, T1], ctx=inner)
                index_scores(m, proj, scores, inner)
                select_keys(m, scores, bias, inner)
            with ExitStack() as inner:
                attend(m, proj, v_tokens, bias, o_dsa, inner)
        with ExitStack() as scope:
            proj = m.sb("gla_proj", [P, 17, T1], ctx=scope)
            gates = m.sb("gla_gates", [P, 8, T1], ctx=scope)
            dense(m, gla_stage(proj), gate_stage(None))
            dense(m, gate_stage(gates), out_stage(None, w_out))
            with ExitStack() as inner:
                v_tokens = m.sb("gla_v_tokens", [P, 3, GLA_HEADS * GLA_DV], ctx=inner)
                to_tokens(m, proj[:, 8:16, :], 8, TILES, v_tokens, "gla")
                gla(m, dram, proj, gates, v_tokens, inner)
            norm_heads(m, "gla", proj[:, 8:16, N_META:T1], 2, EPS, column(m, "gla_norm_g"), gates[:, :, N_META:T1])
            y = m.sb("mixer_out", [P, DC, SEQ], ctx=y_scope, side="right")
            feed = Feed(m, lambda c: o_dsa[:, c, :] if c < 8 else proj[:, c, N_META:T1], SEQ)
            with ExitStack() as nothing:
                ffn2_first = ffn_stages(m, dram, "ffn2", SEQ, None, nothing, declare=False)[0]
            dense(m, out_stage(y, w_out, m.rstd_post), ffn2_first, feed)

        feed = make_feed(m, h, SEQ, column(m, "ffn2_pre_g"), (y, column(m, "mix_post_g"), m.rstd_post), True)
        run_ffn(m, dram, "ffn2", SEQ, y, feed, rwkv_stage(None))

        with ExitStack() as scope:
            proj = m.sb("rwkv_proj", [P, 33, SEQ], ctx=scope)
            feed = make_feed(m, h, SEQ, None, (y, m.half_gain[:, 1, :], m.rstd_post))
            with ExitStack() as inner:
                differences = m.sb("shift_differences", [P, 2, SEQ], ctx=inner)
                dense(m, rwkv_stage(proj, differences), hgrn_stage(None), feed)
            y_scope.close()
            o_dsa_scope.close()
            m.close_x()
            masks = Masks64(m, scope)
            alpha, beta, bonus = (m.sb(f"rwkv_{x}", [P, PAIRS, SEQ], ctx=scope) for x in ("alpha", "beta", "bonus"))
            last = m.sb("rwkv_last_decay", [P, PAIRS, SEQ // CHUNK], ctx=scope)
            with ExitStack() as inner:
                sums, tmp = (m.sb(f"rwkv_{x}", [P, PAIRS, SEQ], ctx=inner) for x in ("sums", "tmp"))
                rwkv_vectors(m, dram, proj, masks, sums, alpha, beta, bonus, tmp)
                rwkv_decays(m, proj, sums, alpha, beta, bonus, tmp, last)
            with ExitStack() as inner:
                o = proj[:, 2 * PAIRS:3 * PAIRS, :]
                scan = Rwkv(m, inner, proj, last, alpha, beta, masks, o)
                scan.start()
                for first in range(0, SEQ // CHUNK, 2):
                    scan.prepare(first)
                    scan.scan(first)
            o_rwkv = m.sb("o_rwkv", [P, PAIRS, SEQ], side="right")
            rwkv_finish(m, masks, o, bonus, proj[:, 3 * PAIRS:4 * PAIRS, :], o_rwkv[:, :, :])
        m.open_x("x_again")
        with ExitStack() as scope:
            proj = m.sb("hgrn_proj", [P, 32, SEQ], ctx=scope)
            dense(m, hgrn_stage(proj), out_stage(None, w_out_2), make_feed(m, h, SEQ))
            with ExitStack() as inner:
                b = m.sb("hgrn_log_decay", [P, 8, SEQ], ctx=inner)
                m.close_x()
                hgrn_gates(m, proj, b[:, :, :], inner)
                tokens = m.sb("hgrn_tokens", [P, 2, D // 2], ctx=inner)
                to_tokens(m, proj[:, 16:24, :], 8, TILES[0:2], tokens, "hgrn")
                for g in range(2):
                    heads = slice(4 * g, 4 * g + 4)
                    decay_attention(m, f"hgrn{g}", proj[:, heads, :], proj[:, 8 + 4 * g:12 + 4 * g, :], b[:, heads, :],
                                    SEQ, tokens, 4 * g * P, 1, proj, 16 + 4 * g)
            norm_heads(m, "hgrn", proj[:, 16:24, :], 1, RMS_EPS, column(m, "g_norm_w_2"), proj[:, 24:32, :])
            m.open_x("x_out")
            y = m.sb("out_2", [P, DC, SEQ], side="right")
            dense(m, out_stage(y, w_out_2), None,
                  Feed(m, lambda c: o_rwkv[:, c, :] if c < 8 else proj[:, 8 + c, :], SEQ))
        layer_norm_out(m, y, out)


def make_feed(m, h, T, gain=None, update=None, norm=False):
    return Feed(m, lambda c: h[:, c, :], T, gain, update, Norm(m, DC, T, m.rstd) if norm else None)


def ffn_stages(m, dram, name, T, y, scope, declare=True):
    def buffer(part, shape, dt=F32):
        return m.sb(f"{name}_{part}", shape, dt, scope) if declare else None

    h_hi, h_lo = buffer("h_hi", [P, FT // 2, T], F32R), buffer("h_lo", [P, FT // 2, T], F32R)
    silu, hidden = buffer("silu", [P, 2, T]), buffer("hidden", [P, 2, T])
    wg, wu, wd = (dram[f"{name}_w_{x}"][0] for x in ("gate", "up", "down"))
    stages = []
    for half in range(2):
        stages.append(GateUp(m, wg, wu, half, T, h_hi, h_lo, silu, hidden, m.rstd))
        stages.append(Down(m, wd, half, h_hi, h_lo, T, y, m.rstd_post if half else None))
    return stages


def run_ffn(m, dram, name, T, y, feed, following, beside=None):
    with ExitStack() as scope:
        stages = ffn_stages(m, dram, name, T, y, scope)
        for x, (stage, then) in enumerate(zip(stages, stages[1:] + [following])):
            dense(m, stage, then, feed if x == 0 else None, beside if x == 1 else None)





def kernel(**inputs):
    import concourse.bacc as _bacc
    from concourse.bass_utils import run_bass_kernel_spmd as _run

    nc = _bacc.Bacc("TRN2", target_bir_lowering=False, num_devices=1)
    arrays, dram = {}, {}
    for name, value in inputs.items():
        if 0 in value.shape:
            continue
        a = np.ascontiguousarray(value)
        arrays[f"in_{name}"] = a
        dram[name] = nc.dram_tensor(f"in_{name}", a.shape, mybir.dt.from_np(a.dtype), kind="ExternalInput").ap()
    out = nc.dram_tensor("out", (1, SEQ, D), F32, kind="ExternalOutput").ap()
    build(nc, dram, out)
    r = _run(nc, [arrays], core_ids=[0])
    return r.results[0]["out"]
```

```python
from contextlib import ExitStack

import concourse.bass as bass
from concourse import mybir
import numpy as np

ALU = mybir.AluOpType
ACT = mybir.ActivationFunctionType
AX = mybir.AxisListType
F32 = mybir.dt.float32
F32R = mybir.dt.float32r
U8 = mybir.dt.uint8

P = 128
D = 2048
DC = D // P
N_META = 16
SEQ = 256
T1 = N_META + SEQ
D_FF = 5632
FT = D_FF // P
TILES = [(0, 128), (128, 128), (256, 16)]
EPS = 1e-6

DSA_HEADS = 8
IDX_HEADS = 16
IDX_DIM = 64
TOP_K = min(256, SEQ // 4)
GLA_HEADS = 4
GLA_DV = 256
GLA_TAU = 16.0

RANK_COLUMNS, RANK_PLACE = 32, 24
ALPHA = 2.0 ** 0.25
RAW = 4
SPLIT = 2
MASKED = -1.0e30
TAKEN = -3.0e38


class Signal:

    def __init__(self, nc, ctx, name):
        self.sem = ctx.enter_context(nc.semaphore(name))
        self.n = 0

    def on(self, instruction, by=1):
        instruction.then_inc(self.sem, by)
        self.n += by
        return instruction


class Machine:

    def __init__(self, nc, ctx):
        self.nc, self.ctx = nc, ctx
        self.signals = {}
        self.unit = 0
        self.group = 0
        self.pairs = 0
        self.squares = 0
        self.shifted = 0

    def sb(self, name, shape, dt=F32, ctx=None, side="left"):
        return (ctx or self.ctx).enter_context(self.nc.sbuf_tensor(name, shape, dt, side=side))

    def sig(self, name):
        if name not in self.signals:
            self.signals[name] = Signal(self.nc, self.ctx, name)
        return self.signals[name]

    def open_x(self, name):
        self.x_scope = self.ctx.enter_context(ExitStack())
        self.x_hi, self.x_lo = (self.sb(f"{name}_{part}", [P, DC, T1], F32R, self.x_scope, "right") for part in ("hi", "lo"))

    def close_x(self):
        self.x_scope.close()
        self.x_hi = self.x_lo = None

    def dense_bank(self, group, bank):
        return self.ps[:, 4 * (group % 2) + 3 - bank, :]

    def block(self):
        return self.nc.Block(no_gpsimd_drain=True)


def load_unit(m, sp, unit, stage, rel, u):
    src = stage.source(rel, u)
    dst = m.raw[:, unit % RAW, 0:stage.chunks * P].rearrange("p (k c) -> p k c", c=P)
    sp.dma_start(dst, src.rearrange("(k p) c -> p k c", p=P)).then_inc(m.raw_loaded[unit % RAW], 16)


class Norm:

    def __init__(self, m, count, T, rstd, eps=EPS):
        self.m, self.count, self.T, self.rstd, self.eps = m, count, T, rstd, eps
        self.n0 = m.squares
        m.squares += count
        self.summed, self.scaled, self.rooted = m.sig("square_sums"), m.sig("mean_squares"), m.sig("roots")
        self.base = {s: s.n for s in (self.summed, self.scaled, self.rooted)}

    def square_act(self, act, source, c):
        m, n = self.m, self.n0 + c
        act.wait_ge(m.squares_free, n + 1)
        act.activation(m.sq[:, n % 2, 0:self.T], source, ACT.Square).then_inc(m.squared, 1)

    def sum_pe(self, pe, c):
        m, n = self.m, self.n0 + c
        pe.wait_ge(m.squared, n + 1)
        pe.matmul(m.ps[:, 5, 0:self.T], m.ones[:, :], m.sq[:, n % 2, 0:self.T], start=c == 0,
                  stop=c == self.count - 1).then_inc(m.squares_free, 1)

    def clear(self, pool):
        cleared = self.m.sig("acc_cleared")
        cleared.on(pool.memset(self.m.acc[:, 0:self.T], 0.0))
        pool.wait_ge(cleared.sem, cleared.n)

    def add_pool(self, pool, source, i, u, per_body):
        m, n, at = self.m, self.n0 + u, per_body * i
        acc, sq = m.acc[:, 0:self.T], m.sq[:, n % 2, 0:self.T]
        pool.tensor_tensor(sq, source, source, ALU.mult).then_inc(m.squared, 1)
        pool.wait_ge(m.squared, n + at + 1)
        pool.wait_ge(m.squares_free, n + at + 2)
        pool.tensor_tensor(acc, acc, sq, ALU.add).then_inc(m.squares_free, 1)

    def finish_pe(self, pe):
        pe.wait_ge(self.m.squares_free, self.n0 + self.count + 2)
        self.summed.on(pe.matmul(self.m.ps[:, 5, 0:self.T], self.m.ones[:, :], self.m.acc[:, 0:self.T],
                                 start=True, stop=True))

    def finish_dve(self, dve, fed):
        if fed:
            dve.wait_ge(self.m.squares_free, self.n0 + self.count + 2)
        else:
            dve.wait_ge(self.summed.sem, self.base[self.summed] + 1)
        self.scaled.on(dve.tensor_scalar(self.rstd[:, 0:self.T], self.m.ps[:, 5, 0:self.T],
                                         1.0 / (self.count * P), self.eps, ALU.mult, ALU.add))
        dve.wait_ge(self.rooted.sem, self.base[self.rooted] + 1)
        self.scaled.on(dve.reciprocal(self.rstd[:, 0:self.T], self.rstd[:, 0:self.T]))
        dve.wait_ge(self.scaled.sem, self.base[self.scaled] + 2)

    def finish_act(self, act):
        act.wait_ge(self.scaled.sem, self.base[self.scaled] + 1)
        self.rooted.on(act.activation(self.rstd[:, 0:self.T], self.rstd[:, 0:self.T], ACT.Sqrt))


class Feed:

    def __init__(self, m, h, T, gain=None, update=None, norm=None):
        self.m, self.h, self.T, self.gain, self.update, self.norm = m, h, T, gain, update, norm
        self.scaled, self.added = m.sig("update_scaled"), m.sig("residual_added")
        self.high, self.low = m.sig("x_high"), m.sig("x_low")
        self.base = {s: s.n for s in (self.scaled, self.added, self.high, self.low)}

    def dve(self, dve, middle):
        base = self.base
        for c in range(DC + 1):
            if self.update is not None and c < DC:
                y, gain, rstd = self.update
                self.scaled.on(dve.scalar_tensor_tensor(y[:, c, 0:self.T], y[:, c, 0:self.T], gain[:, c:c + 1],
                                                        rstd[:, 0:self.T], ALU.mult, ALU.mult))
            if c == DC // 2:
                middle()
            if c >= 1:
                k = c - 1
                dve.wait_ge(self.high.sem, base[self.high] + k + 1)
                hi, lo = (x[:, k, 0:self.T] for x in (self.m.x_hi, self.m.x_lo))
                if self.gain is None:
                    self.low.on(dve.tensor_tensor(lo, self.h(k), hi.bitcast(F32), ALU.subtract))
                else:
                    self.low.on(dve.scalar_tensor_tensor(lo, self.h(k), self.gain[:, k:k + 1],
                                                         hi.bitcast(F32), ALU.mult, ALU.subtract))

    def act(self, act, middle):
        for c in range(DC):
            if self.update is not None:
                act.wait_ge(self.added.sem, self.base[self.added] + c + 1)
            hi = self.m.x_hi[:, c, 0:self.T]
            if self.gain is None:
                self.high.on(act.activation(hi, self.h(c), ACT.Copy))
            else:
                self.high.on(act.activation(hi, self.h(c), ACT.Copy, scale=self.gain[:, c:c + 1]))
            if c == DC // 2:
                middle()
            if self.norm is not None:
                self.norm.square_act(act, self.h(c), c)

    def pool(self, pool):
        for c in range(DC if self.update is not None else 0):
            pool.wait_ge(self.scaled.sem, self.base[self.scaled] + c + 1)
            self.added.on(pool.tensor_tensor(self.h(c), self.h(c), self.update[0][:, c, 0:self.T], ALU.add))
        if self.update is not None:
            pool.wait_ge(self.added.sem, self.added.n)

    def before_chunk(self, pe, k):
        pe.wait_ge(self.low.sem, self.base[self.low] + k + 1)
        if self.norm is not None and k >= 1:
            self.norm.sum_pe(pe, k - 1)


class Ring:

    def __init__(self, m, stage, following):
        self.m, self.stage, self.following = m, stage, following
        self.n0, self.g0, self.count = m.unit, m.group, stage.count
        stage.n0, stage.g0, stage.p0 = m.unit, m.group, m.pairs
        m.unit += stage.count
        m.group += stage.count // stage.per_group
        m.pairs += stage.pairs

    def load(self, sp, i, u):
        m, n = self.m, self.n0 + u
        if isinstance(i, int) and 4 * i + u + RAW >= self.count:
            k = 4 * i + u + RAW - self.count
            if self.following is None:
                return
            stage, rel, parity = self.following, k, k
        else:
            stage, rel, parity = self.stage, 4 * i + u + RAW, u
        sp.wait_ge(m.lo_ready, n + 4 * i + 1)
        load_unit(m, sp, n, stage, rel, parity)

    def next_chunks(self, i, u):
        if isinstance(i, int) and 4 * i + u == self.count - 1:
            return None if self.following is None else self.following.chunks
        return self.stage.chunks

    def high(self, act, i, u, chunks):
        if chunks is None:
            return
        m, n = self.m, self.n0 + u
        act.wait_ge(m.raw_loaded[n % RAW], 16 * (n // RAW + 1) + 16 * i)
        act.wait_ge(m.units_done, n + 4 * i + 1)
        act.activation(m.w_hi[:, n % SPLIT, 0:chunks * P], m.raw[:, n % RAW, 0:chunks * P],
                       ACT.Copy).then_inc(m.hi_ready, 1)

    def low(self, dve, i, u, chunks):
        if chunks is None:
            return
        m, n = self.m, self.n0 + u
        dve.wait_ge(m.hi_ready, n + 4 * i + 1)
        dve.tensor_tensor(m.w_lo[:, n % SPLIT, 0:chunks * P], m.raw[:, n % RAW, 0:chunks * P],
                          m.w_hi[:, n % SPLIT, 0:chunks * P].bitcast(F32), ALU.subtract).then_inc(m.lo_ready, 1)

    def multiply(self, pe, i, u, before_chunk=None):
        m, stage, n, T = self.m, self.stage, self.n0 + u, self.stage.T
        bank, start, stop = stage.bank(u)
        group = self.g0 + u // stage.per_group
        out = m.dense_bank(group, bank)[:, 0:T]
        pe.wait_ge(m.lo_ready, n + 4 * i + 1)
        if u % stage.per_group == 0:
            pe.wait_ge(m.banks_free, group + (4 // stage.per_group) * i + 1)
        x_hi, x_lo = stage.moving(u)
        for k in range(stage.chunks):
            if before_chunk is not None:
                before_chunk(k)
            w_hi = m.w_hi[:, n % SPLIT, k * P:(k + 1) * P]
            w_lo = m.w_lo[:, n % SPLIT, k * P:(k + 1) * P]
            first, last = start and k == 0, stop and k == stage.chunks - 1
            pe.matmul(out, w_hi, x_hi[:, k, 0:T], start=first, stop=False)
            pe.matmul(out, w_hi, x_lo[:, k, 0:T], start=False, stop=False)
            mm = pe.matmul(out, w_lo, x_hi[:, k, 0:T], start=False, stop=last)
        mm.then_inc(m.units_done, 1)


def dense(m, stage, following, feed=None, beside=None, stretches=None):
    ring = Ring(m, stage, following)
    if stage.norm_rstd is not None:
        stage.norm = Norm(m, stage.tiles, stage.T, stage.norm_rstd)
    count = stage.count
    first = 1 if feed is not None else 0
    last = first if stretches is not None else max(count // 4 - 1, first)

    def over(eng, body):
        for u in range(4 * first):
            body(0, u)
        if last > first:
            with eng.Fori(first, last) as i:
                for u in range(4):
                    body(i, u)
        for rel in range(4 * last, count):
            body(rel // 4, rel % 4)

    def beginning(i, u):
        return feed is not None and isinstance(i, int) and (i, u) == (0, 0)

    with m.block() as block:

        @block.sync
        def _(sp):
            if stretches is not None:
                stretches.sp(sp)
            over(sp, lambda i, u: ring.load(sp, i, u))

        @block.scalar
        def _(act):
            others = iter(()) if stretches is None else stretches.act(act)

            def step(i, u):
                if not beginning(i, u):
                    ring.high(act, i, u + 1, ring.next_chunks(i, u))
                stage.evacuate_act(act, i, u)
                next(others, None)

            if ring.n0 == 0:
                ring.high(act, 0, 0, stage.chunks)
            if feed is not None:
                feed.act(act, lambda: ring.high(act, 0, 1, stage.chunks))
                if feed.norm is not None:
                    feed.norm.finish_act(act)
            over(act, step)
            if stage.norm is not None:
                stage.norm.finish_act(act)

        @block.vector
        def _(dve):
            others = iter(()) if stretches is None else stretches.dve(dve)

            def step(i, u):
                if not beginning(i, u):
                    ring.low(dve, i, u + 1, ring.next_chunks(i, u))
                stage.evacuate_dve(dve, i, u)
                next(others, None)

            if ring.n0 == 0:
                ring.low(dve, 0, 0, stage.chunks)
            if feed is not None:
                feed.dve(dve, lambda: ring.low(dve, 0, 1, stage.chunks))
                if feed.norm is not None:
                    feed.norm.finish_dve(dve, True)
            over(dve, step)
            if stage.norm is not None:
                stage.norm.finish_dve(dve, False)

        @block.gpsimd
        def _(pool):
            if feed is not None:
                feed.pool(pool)
            if beside is not None:
                beside(pool)
            if stage.norm is not None:
                stage.norm.clear(pool)
            if stage.evacuate_pool is not None:
                over(pool, lambda i, u: stage.evacuate_pool(pool, i, u))
                stage.settle_pool(pool)
            if stage.norm is not None:
                pool.wait_ge(m.squares_free, m.squares + 2)

        @block.tensor
        def _(pe):
            others = iter(()) if stretches is None else stretches.pe(pe)

            def multiply(i, u):
                if beginning(i, u):
                    ring.multiply(pe, i, u, lambda k: feed.before_chunk(pe, k))
                    if feed.norm is not None:
                        feed.norm.sum_pe(pe, DC - 1)
                else:
                    ring.multiply(pe, i, u)
                next(others, None)

            over(pe, multiply)
            if stage.norm is not None:
                stage.norm.finish_pe(pe)


class Project:

    per_group, pairs, chunks = 1, 0, DC

    def __init__(self, m, weights, first_column, count, T, out, scale=None, rstd=None):
        self.m, self.w, self.c0, self.count, self.T = m, weights, first_column, count, T
        self.out, self.scale = out, scale
        if rstd is None:
            self.evacuate_pool = None
        self.norm, self.norm_rstd, self.tiles = None, rstd, count

    def source(self, rel, u):
        return self.w[0:DC * P, bass.ds(self.c0 + rel * P, P)]

    def moving(self, u):
        return self.m.x_hi, self.m.x_lo

    def bank(self, u):
        return 0, True, True

    def tile(self, i, u):
        return self.out[:, bass.ds(4 * i + u, 1), 0:self.T].rearrange("p a t -> p (a t)")

    def evacuate_act(self, act, i, u):
        m = self.m
        if self.scale is None:
            act.wait_ge(m.units_done, self.n0 + 4 * i + u + 1 + SPLIT)
            act.activation(self.tile(i, u), m.dense_bank(self.g0 + u, 0)[:, 0:self.T],
                           ACT.Copy).then_inc(m.banks_free, 1)
    def evacuate_dve(self, dve, i, u):
        m = self.m
        if self.scale is not None:
            dve.wait_ge(m.units_done, self.n0 + 4 * i + u + 1 + SPLIT)
            dve.tensor_tensor(self.tile(i, u), m.dense_bank(self.g0 + u, 0)[:, 0:self.T],
                              self.scale[:, 0:self.T], ALU.mult).then_inc(m.banks_free, 1)

    def evacuate_pool(self, pool, i, u):
        pool.wait_ge(self.m.banks_free, self.g0 + 4 * i + u + 1 + 2)
        self.norm.add_pool(pool, self.tile(i, u), i, u, 4)

    def settle_pool(self, pool):
        pass


class Residual(Project):

    def __init__(self, m, weights, count, T, out, h):
        super().__init__(m, weights, 0, count, T, out)
        self.h, self.evacuate_pool, self.added = h, self.add, m.sig("outputs_added")

    def evacuate_act(self, act, i, u):
        pass

    def evacuate_dve(self, dve, i, u):
        m = self.m
        h = self.h[:, bass.ds(4 * i + u, 1), :].rearrange("p a t -> p (a t)")
        dve.wait_ge(m.units_done, self.n0 + 4 * i + u + 1 + SPLIT)
        dve.scalar_tensor_tensor(self.tile(i, u), h, ALPHA, m.dense_bank(self.g0 + u, 0)[:, 0:self.T], ALU.mult,
                                 ALU.add).then_inc(m.banks_free, 1)

    def add(self, pool, i, u):
        acc = self.m.acc[:, 0:self.T]
        pool.wait_ge(self.m.banks_free, self.g0 + 4 * i + u + 1 + 2)
        if isinstance(i, int) and (i, u) == (0, 0):
            pool.tensor_copy(acc, self.tile(i, u)).then_inc(self.added.sem, 1)
            return
        pool.wait_ge(self.added.sem, 4 * i + u)
        pool.tensor_tensor(acc, acc, self.tile(i, u), ALU.add).then_inc(self.added.sem, 1)

    def settle_pool(self, pool):
        pool.wait_ge(self.added.sem, self.count)


class Shifted(Project):

    def __init__(self, m, weights, first_column, count, T, out, mu, differences):
        super().__init__(m, weights, first_column, count, T, out)
        self.s0 = m.shifted
        m.shifted += count if out is not None else 0
        self.mu, self.d, self.evacuate_pool = mu, differences, self.difference

    def column_tile(self, rel):
        return RANK_COLUMNS if isinstance(rel, int) and rel == 16 else rel

    def source(self, rel, u):
        return super().source(self.column_tile(rel), u)

    def tile(self, i, u):
        tensor, place = self.out(4 * i + u)
        return tensor[:, bass.ds(place, 1), :].rearrange("p a t -> p (a t)")

    def difference(self, pool, i, u):
        m, d, T = self.m, self.d[:, (self.s0 + u) % 2, :], self.T
        y = self.tile(i, u)
        pool.wait_ge(m.banks_free, self.g0 + 4 * i + u + 1 + 2)
        pool.wait_ge(m.shift_free, self.s0 + 4 * i + u + 1)
        pool.tensor_tensor(d[:, 0:1], m.zero[:, :], y[:, 0:1], ALU.subtract).then_inc(m.differed, 1)
        pool.tensor_tensor(d[:, 1:T], y[:, 0:T - 1], y[:, 1:T], ALU.subtract).then_inc(m.differed, 1)

    def settle_pool(self, pool):
        pool.wait_ge(self.m.differed, 2 * (self.s0 + self.count))

    def evacuate_dve(self, dve, i, u):
        m, y = self.m, self.tile(i, u)
        dve.wait_ge(m.differed, 2 * self.s0 + 8 * i + 2 * u + 2)
        mu = self.mu[:, bass.ds(self.column_tile(4 * i + u), 1)]
        dve.scalar_tensor_tensor(y, self.d[:, (self.s0 + u) % 2, :], mu, y, ALU.mult, ALU.add).then_inc(m.shift_free, 1)


class GateUp:

    per_group, pairs, norm, norm_rstd = 2, FT // 2, None, None

    def __init__(self, m, w_gate, w_up, half, T, h_hi, h_lo, silu, hidden, rstd):
        self.m, self.wg, self.wu, self.half, self.T = m, w_gate, w_up, half, T
        self.h_hi, self.h_lo = h_hi, h_lo
        self.silu, self.hidden, self.rstd = silu, hidden, rstd
        self.chunks, self.count = DC, FT

    def source(self, rel, u):
        w = self.wu if u % 2 else self.wg
        first = self.half * (FT // 2) * P
        return w[:, bass.ds(first + (rel - u % 2) * (P // 2), P)]

    def moving(self, u):
        return self.m.x_hi, self.m.x_lo

    def bank(self, u):
        return u % 2, True, True

    def evacuate_act(self, act, i, u):
        m = self.m
        if u % 2 == 1:
            pair = self.p0 + u // 2
            gate = self.silu[:, pair % 2, 0:self.T]
            act.wait_ge(m.gate_scaled, pair + 2 * i + 1)
            act.activation(gate, gate, ACT.Silu).then_inc(m.silu_ready, 1)

    def evacuate_dve(self, dve, i, u):
        m = self.m
        group, pair = self.g0 + u // 2, self.p0 + u // 2
        rstd, hidden = self.rstd[:, 0:self.T], self.hidden[:, pair % 2, 0:self.T]
        gate = self.silu[:, pair % 2, 0:self.T]
        dve.wait_ge(m.units_done, self.n0 + 4 * i + u + 1 + SPLIT)
        if u % 2 == 0:
            dve.wait_ge(m.hidden_split, pair + 2 * i + 1)
            dve.tensor_tensor(gate, m.dense_bank(group, 0)[:, 0:self.T], rstd, ALU.mult).then_inc(m.gate_scaled, 1)
        else:
            dve.tensor_tensor(hidden, m.dense_bank(group, 1)[:, 0:self.T], rstd, ALU.mult).then_inc(m.banks_free, 1)
            dve.wait_ge(m.banks_free, group + 2 * i + 1 + 2)
            dve.wait_ge(m.silu_ready, pair + 2 * i + 1)
            dve.tensor_tensor(hidden, hidden, gate, ALU.mult).then_inc(m.hidden_ready, 1)

    def evacuate_pool(self, pool, i, u):
        m = self.m
        if u % 2 == 1:
            pair = self.p0 + u // 2
            hidden = self.hidden[:, pair % 2, 0:self.T]
            hi = self.h_hi[:, bass.ds(2 * i + u // 2, 1), 0:self.T].rearrange("p a t -> p (a t)")
            lo = self.h_lo[:, bass.ds(2 * i + u // 2, 1), 0:self.T].rearrange("p a t -> p (a t)")
            pool.wait_ge(m.hidden_ready, pair + 2 * i + 1)
            pool.tensor_copy(hi, hidden).then_inc(m.hidden_hi, 1)
            pool.wait_ge(m.hidden_hi, pair + 2 * i + 1)
            pool.tensor_tensor(lo, hidden, hi.bitcast(F32), ALU.subtract).then_inc(m.hidden_split, 1)


    def settle_pool(self, pool):
        pool.wait_ge(self.m.hidden_split, self.m.pairs + 2)


class Down:

    per_group, pairs = 2, 0

    def __init__(self, m, w_down, half, h_hi, h_lo, T, y, rstd=None):
        self.m, self.w, self.half, self.T, self.y = m, w_down, half, T, y
        self.h = (h_hi, h_lo)
        self.chunks, self.count = FT // 4, 2 * DC
        self.norm, self.norm_rstd, self.tiles = None, rstd, DC
        if rstd is None:
            self.evacuate_pool = None

    def source(self, rel, u):
        first = (self.half * 2 + u % 2) * self.chunks * P
        cols = bass.ds((rel - u % 2) * (P // 2), P)
        return self.w[first:first + self.chunks * P, cols]

    def moving(self, u):
        a = (u % 2) * self.chunks
        return tuple(h[:, a:a + self.chunks, 0:self.T] for h in self.h)

    def bank(self, u):
        return 0, u % 2 == 0, u % 2 == 1

    def tile(self, i, u):
        return self.y[:, bass.ds(2 * i + u // 2, 1), 0:self.T].rearrange("p a t -> p (a t)")

    def evacuate_act(self, act, i, u):
        m, group = self.m, self.g0 + u // 2
        if u % 2 == 1 and self.half == 0:
            act.wait_ge(m.units_done, self.n0 + 4 * i + u + 1 + SPLIT)
            act.activation(self.tile(i, u), m.dense_bank(group, 0)[:, 0:self.T], ACT.Copy).then_inc(m.banks_free, 1)

    def evacuate_dve(self, dve, i, u):
        m, group = self.m, self.g0 + u // 2
        if u % 2 == 1 and self.half == 1:
            dve.wait_ge(m.units_done, self.n0 + 4 * i + u + 1 + SPLIT)
            dve.tensor_tensor(self.tile(i, u), m.dense_bank(group, 0)[:, 0:self.T], self.tile(i, u),
                              ALU.add).then_inc(m.banks_free, 1)

    def evacuate_pool(self, pool, i, u):
        if u % 2 == 1:
            pool.wait_ge(self.m.banks_free, self.g0 + u // 2 + 2 * i + 1 + 2)
            self.norm.add_pool(pool, self.tile(i, u), i, u // 2, 2)

    def settle_pool(self, pool):
        pass


QUERIES = [(N_META, P), (N_META + P, P)]
FREE_BANKS = [0, 1, 4, 5, 2, 6]
OUT_BANKS = [4, 5, 2, 6, 0, 1]
LEVELS = [64, 32, 16, 8, 4, 2, 1]


def make_masks(m, pool):
    made, full = m.sig("masks_made"), m.masks_full
    made.on(pool.memset(full[:, :, :], 0.0))
    pool.wait_ge(made.sem, made.n)
    for level, h in enumerate(LEVELS):
        view = full[:, level, :].rearrange("p (n a h) -> p n a h", a=2, h=h)[:, :, 1, :]
        made.on(pool.memset(view, 1.0))
        blocks = P // (2 * h)
        for base, sign in ((0, 1), (h - 1, -1)):
            pool.wait_ge(made.sem, made.n)
            made.on(pool.affine_select(out=view, in_=view, compare_op=ALU.is_ge, fill=0.0, base=base,
                                       pattern=[[-2 * h * sign, blocks]] * (blocks > 1) + [[0, h]] * (h > 1),
                                       channel_multiplier=sign))
    made.on(pool.tensor_copy(full[:, len(LEVELS), :], m.ident[:, :]))
    pool.wait_ge(made.sem, made.n)
    made.on(pool.tensor_copy(m.masks[:, :, :], full[:, :, :]))
    pool.wait_ge(made.sem, made.n)


def to_tokens(m, source, chunks, tiles, tokens, name):
    turned = m.sig("chunks_turned")
    bank = FREE_BANKS
    copied = [m.sig("turned_copied_act"), m.sig("turned_copied_dve")]
    groups = [(j, c) for j in range(len(tiles)) for c in range(0, chunks, 4)]
    turned0, copied0 = turned.n, [c.n for c in copied]
    with m.block() as block:

        @block.tensor
        def _(pe):
            for g, (j, c0) in enumerate(groups):
                t0, n = tiles[j]
                if g >= 4:
                    pe.wait_ge(copied[g % 2].sem, copied0[g % 2] + (g - 4) // 2 + 1)
                for c in range(4):
                    mm = pe.transpose(m.ps[0:n, bank[g % 4], c * P:(c + 1) * P], source[:, c0 + c, t0:t0 + n],
                                      m.ident[:, :])
                turned.on(mm)

        def copy(eng, parity):
            for g, (j, c0) in enumerate(groups):
                if g % 2 == parity:
                    n = tiles[j][1]
                    dst, src = tokens[0:n, j, c0 * P:(c0 + 4) * P], m.ps[0:n, bank[g % 4], :]
                    eng.wait_ge(turned.sem, turned0 + g + 1)
                    done = eng.activation(dst, src, ACT.Copy) if parity == 0 else eng.tensor_copy(dst, src)
                    copied[parity].on(done)

        @block.scalar
        def _(act):
            copy(act, 0)

        @block.vector
        def _(dve):
            copy(dve, 1)


def index_scores(m, proj, scores, scope):
    ik2 = m.sb("idx_keys", [P, T1], ctx=scope)
    weights = m.sb("idx_weights", [P, len(QUERIES), IDX_HEADS], ctx=scope)
    rectified = m.sb("idx_rectified", [P, 2, T1], ctx=scope)
    keys, turned, scaled = m.sig("idx_keys_copied"), m.sig("idx_weights_turned"), m.sig("idx_weights_scaled")
    made, relued, added = m.sig("idx_logits_made"), m.sig("idx_relued"), m.sig("idx_added")
    masked = m.sig("idx_masked")
    with m.block() as block:

        @block.scalar
        def _(act):
            keys.on(act.activation(ik2[0:IDX_DIM, :], proj[0:IDX_DIM, 32, :], ACT.Copy))
            keys.on(act.activation(ik2[IDX_DIM:P, :], proj[0:IDX_DIM, 32, :], ACT.Copy))

        @block.tensor
        def _(pe):
            w = proj[IDX_DIM:IDX_DIM + IDX_HEADS, 32, :]
            for j, (t0, n) in enumerate(QUERIES):
                mm = pe.matmul(m.ps[0:n, 2, j * 32:j * 32 + IDX_HEADS], w[:, t0:t0 + n],
                               m.ident[IDX_DIM:IDX_DIM + IDX_HEADS, IDX_DIM:IDX_DIM + IDX_HEADS],
                               start=True, stop=True)
            turned.on(mm)

        @block.vector
        def _(dve):
            dve.wait_ge(turned.sem, turned.n)
            for j, (t0, n) in enumerate(QUERIES):
                scaled.on(dve.tensor_scalar(weights[0:n, j, :], m.ps[0:n, 2, j * 32:j * 32 + IDX_HEADS],
                                            float(IDX_HEADS) ** -0.5, None, ALU.mult))

    order = [(j, h) for j in range(len(QUERIES)) for h in range(IDX_HEADS)]
    made0, relued0, added0 = made.n, relued.n, added.n
    with m.block() as block:

        @block.tensor
        def _(pe):
            for x, (j, h) in enumerate(order):
                (t0, n), half = QUERIES[j], (h % 2) * IDX_DIM
                if x >= 4:
                    pe.wait_ge(relued.sem, relued0 + x - 3)
                made.on(pe.matmul(m.ps[0:n, FREE_BANKS[x % 4], 0:t0 + n], proj[half:half + IDX_DIM, 24 + h // 2, t0:t0 + n],
                                  ik2[half:half + IDX_DIM, 0:t0 + n], start=True, stop=True))

        @block.scalar
        def _(act):
            for x, (j, h) in enumerate(order):
                t0, n = QUERIES[j]
                act.wait_ge(made.sem, made0 + x + 1)
                if x >= 2:
                    act.wait_ge(added.sem, added0 + x - 1)
                relued.on(act.activation(rectified[0:n, x % 2, 0:t0 + n], m.ps[0:n, FREE_BANKS[x % 4], 0:t0 + n], ACT.Relu,
                                         scale=float(IDX_DIM) ** -0.5))

        @block.vector
        def _(dve):
            for x, (j, h) in enumerate(order):
                t0, n = QUERIES[j]
                src, acc = rectified[0:n, x % 2, 0:t0 + n], scores[0:n, j, 0:t0 + n]
                dve.wait_ge(relued.sem, relued0 + x + 1)
                if h == 0:
                    added.on(dve.tensor_scalar(acc, src, weights[0:n, j, h:h + 1], None, ALU.mult))
                else:
                    dve.wait_ge(added.sem, added0 + x)
                    added.on(dve.scalar_tensor_tensor(acc, src, weights[0:n, j, h:h + 1], acc, ALU.mult, ALU.add))

        @block.gpsimd
        def _(pool):
            for j, (t0, n) in enumerate(QUERIES):
                acc = scores[0:n, j, 0:t0 + n]
                pool.wait_ge(added.sem, added0 + (j + 1) * IDX_HEADS)
                masked.on(pool.affine_select(out=acc, in_=acc, compare_op=ALU.is_ge, fill=MASKED, base=t0,
                                             pattern=[[-1, t0 + n]], channel_multiplier=1))
            pool.wait_ge(masked.sem, masked.n)


class SelectKeys:

    def __init__(self, m, scores, bias, scope):
        self.m, self.scores, self.bias = m, scores, bias
        self.best = m.sb("topk_best", [P, len(QUERIES), 8], ctx=scope)
        self.found, self.flagged, self.biased = m.sig("topk_steps"), m.sig("topk_flagged"), m.sig("topk_biased")

    def sp(self, sp):
        pass

    def act(self, act):
        return iter(())

    def pe(self, pe):
        return iter(())

    def dve(self, dve):
        found = self.found
        for j, (t0, n) in enumerate(QUERIES):
            row, top = self.scores[0:n, j, 0:t0 + n], self.best[0:n, j, :]
            for x in range(TOP_K // 8):
                if found.n:
                    dve.wait_ge(found.sem, found.n)
                found.on(dve.max(top, row))
                dve.wait_ge(found.sem, found.n)
                found.on(dve.match_replace(row, top, row, TAKEN))
                if x % 2 == 1 and x < TOP_K // 8 - 1:
                    yield
            dve.wait_ge(found.sem, found.n)
            self.flagged.on(dve.tensor_scalar(self.bias[0:n, j, 0:t0 + n], row, TAKEN, 1.0, ALU.is_equal,
                                              ALU.subtract))
            yield

    def pool(self, pool):
        biased = self.biased
        for j, (t0, n) in enumerate(QUERIES):
            row = self.bias[0:n, j, 0:t0 + n]
            pool.wait_ge(self.flagged.sem, j + 1)
            biased.on(pool.tensor_scalar(row, row, -MASKED, None, ALU.mult))
            pool.wait_ge(biased.sem, biased.n)
            biased.on(pool.affine_select(out=row, in_=row, compare_op=ALU.is_ge, fill=MASKED, base=t0,
                                         pattern=[[-1, t0 + n]], channel_multiplier=1))
        pool.wait_ge(biased.sem, biased.n)


def attend(m, proj, v_tokens, bias, o, scope):
    H = DSA_HEADS
    logits = proj[:, 24:24 + H, :]
    turned_p = m.sb("attn_turned", [P, len(TILES), H, P], ctx=scope)
    small = m.sb("attn_small", [P, 4, H], ctx=scope)
    negated, total, inverse = small[:, 1, :], small[:, 2, :], small[:, 3, :]
    made, biased, peaked = m.sig("attn_products"), m.sig("attn_biased"), m.sig("attn_peaks")
    exped, inverted, normed = m.sig("attn_exps"), m.sig("attn_inverted"), m.sig("attn_normed")
    turned, copied, out_made, out_copied = (m.sig("attn_turned"), m.sig("attn_turned_copied"),
                                            m.sig("attn_outputs"), m.sig("attn_outputs_copied"))
    for j, (t0, n) in enumerate(QUERIES):
        N = t0 + n
        keys = [(s0, min(P, N - s0)) for s0 in range(0, N, P)]
        q0 = t0 - N_META
        base = {s: s.n for s in (made, biased, peaked, exped, inverted, normed, turned, copied, out_made,
                                 out_copied)}
        groups = [(half, i) for half in range(2) for i in range(len(keys))]
        with m.block() as block:

            @block.tensor
            def _(pe):
                for h in range(H):
                    if h >= 3:
                        pe.wait_ge(biased.sem, base[biased] + h - 2)
                    made.on(pe.matmul(m.ps[0:n, h % 3, 0:N], proj[:, h, t0:t0 + n], proj[:, H + h, 0:N],
                                      start=True, stop=True))
                for g, (half, i) in enumerate(groups):
                    s0, sn = keys[i]
                    if g >= 2:
                        pe.wait_ge(copied.sem, base[copied] + g - 1)
                    for h in range(4 * half, 4 * half + 4):
                        pe.wait_ge(normed.sem, base[normed] + h + 1)
                        mm = pe.transpose(m.ps[0:sn, 4 + g % 2, (h % 4) * P:(h % 4) * P + n],
                                          logits[0:n, h, s0:s0 + sn], m.ident[0:n, 0:n])
                    turned.on(mm)
                for half in range(2):
                    pe.wait_ge(copied.sem, base[copied] + (half + 1) * len(keys))
                    for h in range(4 * half, 4 * half + 4):
                        for i in range(len(keys)):
                            sn = keys[i][1]
                            mm = pe.matmul(m.ps[:, half, (h % 4) * P:(h % 4) * P + n],
                                           v_tokens[0:sn, i, h * P:(h + 1) * P], turned_p[0:sn, i, h, 0:n],
                                           start=i == 0, stop=i == len(keys) - 1)
                    out_made.on(mm)

            @block.vector
            def _(dve):
                for h in range(H):
                    dve.wait_ge(made.sem, base[made] + h + 1)
                    biased.on(dve.scalar_tensor_tensor(logits[0:n, h, 0:N], m.ps[0:n, h % 3, 0:N],
                                                       float(P) ** -0.5, bias[0:n, j, 0:N], ALU.mult, ALU.add))
                dve.wait_ge(biased.sem, biased.n)
                peaked.on(dve.tensor_reduce(small[0:n, 0, :], logits[0:n, :, 0:N], AX.X, ALU.max))
                dve.wait_ge(peaked.sem, peaked.n)
                peaked.on(dve.tensor_scalar(negated[0:n, :], small[0:n, 0, :], -1.0, None, ALU.mult))
                for half in range(2):
                    dve.wait_ge(exped.sem, base[exped] + 4 * half + 4)
                    inverted.on(dve.reciprocal(inverse[0:n, 4 * half:4 * half + 4],
                                               total[0:n, 4 * half:4 * half + 4]))
                    dve.wait_ge(inverted.sem, inverted.n)
                    for h in range(4 * half, 4 * half + 4):
                        normed.on(dve.tensor_scalar(logits[0:n, h, 0:N], logits[0:n, h, 0:N],
                                                    inverse[0:n, h:h + 1], None, ALU.mult))
                for half in range(2):
                    dve.wait_ge(out_made.sem, base[out_made] + half + 1)
                    out_copied.on(dve.tensor_copy(
                        o[:, 4 * half:4 * half + 4, q0:q0 + n],
                        m.ps[:, half, :].rearrange("p (h q) -> p h q", h=4)[:, :, 0:n]))

            @block.scalar
            def _(act):
                act.wait_ge(peaked.sem, base[peaked] + 2)
                for h in range(H):
                    exped.on(act.activation(logits[0:n, h, 0:N], logits[0:n, h, 0:N], ACT.Exp,
                                            bias=negated[0:n, h:h + 1], accum_out=total[0:n, h:h + 1]))
                for g, (half, i) in enumerate(groups):
                    sn = keys[i][1]
                    act.wait_ge(turned.sem, base[turned] + g + 1)
                    copied.on(act.activation(
                        turned_p[0:sn, i, 4 * half:4 * half + 4, 0:n],
                        m.ps[0:sn, 4 + g % 2, :].rearrange("p (h q) -> p h q", h=4)[:, :, 0:n], ACT.Copy))


def decay_attention(m, name, q, k, b, T, v_tokens, v0, dv_chunks, out, out0):
    H = 4
    tiles = TILES[0:2] if T == SEQ else TILES
    L = len(LEVELS)
    diff_q, diff_k, exped = m.sig("decay_diff_later"), m.sig("decay_diff_earlier"), m.sig("decay_exps")
    q_made, k_made, paired, chosen = (m.sig("decayed_q"), m.sig("decayed_k"), m.sig("decay_pairs"),
                                      m.sig("decay_chosen"))
    cleared = m.sig("decay_cleared")
    with ExitStack() as scope:
        a = m.sb(f"{name}_a", [P, 2, H, P], ctx=scope)
        a_tail = m.sb(f"{name}_a_tail", [16, H, 16], ctx=scope)
        e = m.sb(f"{name}_e", [P, 2, H, T], ctx=scope)
        qe = m.sb(f"{name}_qe", [P, 2, H, T], ctx=scope)
        ke = m.sb(f"{name}_ke", [P, 2, H, T], ctx=scope)
        base = {s: s.n for s in (diff_q, diff_k, exped, q_made, k_made, paired, chosen)}

        def span(level):
            h = LEVELS[level]
            n = T if T % (2 * h) == 0 else SEQ
            v = b[:, :, 0:n].rearrange("p g (n a h) -> p g n a h", a=2, h=h)
            d = e[:, level % 2, :, 0:n].rearrange("p g (n a h) -> p g n a h", a=2, h=h)
            edge = v[:, :, :, 0, h - 1:h].broadcast_to([P, H, n // (2 * h), h])
            return n, v, d, edge

        with m.block() as block:

            @block.tensor
            def _(pe):
                for level in range(L + 1):
                    if level < L:
                        pe.wait_ge(q_made.sem, base[q_made] + level + 1)
                        pe.wait_ge(k_made.sem, base[k_made] + level + 1)
                        n, lhs, rhs = span(level)[0], ke[:, level % 2, :, :], qe[:, level % 2, :, :]
                    else:
                        n, lhs, rhs = T, k, q
                    if level >= 2:
                        pe.wait_ge(chosen.sem, base[chosen] + 3 * (level - 1))
                    for j, (t0, tn) in enumerate(tiles):
                        if t0 >= n:
                            continue
                        for h in range(H):
                            mm = pe.matmul(m.ps[0:tn, 4 * (level % 2) + j, h * tn:(h + 1) * tn],
                                           lhs[:, h, t0:t0 + tn], rhs[:, h, t0:t0 + tn], start=True, stop=True)
                    paired.on(mm)

            @block.vector
            def _(dve):
                def diff(level):
                    n, v, d, edge = span(level)
                    if level >= 2:
                        dve.wait_ge(q_made.sem, base[q_made] + level - 1)
                        dve.wait_ge(k_made.sem, base[k_made] + level - 1)
                    diff_q.on(dve.tensor_tensor(d[:, :, :, 1, :], v[:, :, :, 1, :], edge, ALU.subtract))

                def choose(level):
                    n = T if level == L else span(level)[0]
                    dve.wait_ge(paired.sem, base[paired] + level + 1)
                    if level == 0:
                        dve.wait_ge(cleared.sem, cleared.n + 2)
                    else:
                        dve.wait_ge(chosen.sem, base[chosen] + 3 * level)
                    for j in range(3):
                        if j < len(tiles) and tiles[j][0] < n:
                            tn = tiles[j][1]
                            dst = a[:, j, :, :] if j < 2 else a_tail[:, :, :]
                            mask = m.masks[0:tn, level:level + 1, 0:tn].broadcast_to([tn, H, tn])
                            src = m.ps[0:tn, 4 * (level % 2) + j, 0:H * tn].rearrange("p (h t) -> p h t", h=H)
                            chosen.on(dve.copy_predicated(dst, mask, src))
                        else:
                            chosen.on(dve.engine_nop())

                diff(0)
                for level in range(L):
                    if level + 1 < L:
                        diff(level + 1)
                    n = span(level)[0]
                    dve.wait_ge(exped.sem, base[exped] + level + 1)
                    if level >= 2:
                        dve.wait_ge(paired.sem, base[paired] + level - 1)
                    q_made.on(dve.tensor_tensor(qe[:, level % 2, :, 0:n], q[:, :, 0:n], e[:, level % 2, :, 0:n],
                                                ALU.mult))
                    if level >= 1:
                        choose(level - 1)
                choose(L - 1)
                choose(L)

            @block.gpsimd
            def _(pool):
                cleared.on(pool.memset(a[:, :, :, :], 0.0))
                cleared.on(pool.memset(a_tail[:, :, :], 0.0))

                def diff(level):
                    n, v, d, edge = span(level)
                    if level >= 2:
                        pool.wait_ge(q_made.sem, base[q_made] + level - 1)
                        pool.wait_ge(k_made.sem, base[k_made] + level - 1)
                    diff_k.on(pool.tensor_tensor(d[:, :, :, 0, :], edge, v[:, :, :, 0, :], ALU.subtract))

                diff(0)
                for level in range(L):
                    if level + 1 < L:
                        diff(level + 1)
                    n = span(level)[0]
                    pool.wait_ge(exped.sem, base[exped] + level + 1)
                    if level >= 2:
                        pool.wait_ge(paired.sem, base[paired] + level - 1)
                    k_made.on(pool.tensor_tensor(ke[:, level % 2, :, 0:n], k[:, :, 0:n], e[:, level % 2, :, 0:n],
                                                 ALU.mult))
                pool.wait_ge(k_made.sem, k_made.n)

            @block.scalar
            def _(act):
                for level in range(L):
                    n = span(level)[0]
                    act.wait_ge(diff_q.sem, base[diff_q] + level + 1)
                    act.wait_ge(diff_k.sem, base[diff_k] + level + 1)
                    exped.on(act.activation(e[:, level % 2, :, 0:n], e[:, level % 2, :, 0:n], ACT.Exp))

        a_next = m.sb(f"{name}_a_next", [P, H, P], ctx=scope)
        a_last = m.sb(f"{name}_a_last", [P, 2, H, 16], ctx=scope)
        kx, qx, kx_far = ke[:, 0, :, :], qe[:, 0, :, :], ke[:, 1, :, 0:P]
        far = m.sb(f"{name}_far", [P, H], ctx=scope)
        n_early = P * (len(tiles) - 1)
        n_late = T - P
        three = len(tiles) == 3
        base = {s: s.n for s in (exped, q_made, k_made, paired, chosen)}
        with m.block() as block:

            @block.scalar
            def _(act):
                exped.on(act.activation(e[:, 1, :, 0:n_late], b[:, :, P:T], ACT.Exp))
                for i in range(len(tiles) - 1):
                    for h in range(H):
                        exped.on(act.activation(e[:, 0, h, i * P:(i + 1) * P], b[:, h, i * P:(i + 1) * P], ACT.Exp,
                                                bias=b[:, h, (i + 1) * P - 1:(i + 1) * P], scale=-1.0))
                if three:
                    exped.on(act.activation(far[:, :], b[:, :, 2 * P - 1], ACT.Exp))

            @block.vector
            def _(dve):
                dve.wait_ge(exped.sem, base[exped] + 1)
                q_made.on(dve.tensor_tensor(qx[:, :, 0:n_late], q[:, :, P:T], e[:, 1, :, 0:n_late], ALU.mult))
                dve.wait_ge(exped.sem, base[exped] + 1 + H * (len(tiles) - 1) + three)
                k_made.on(dve.tensor_tensor(kx[:, :, 0:n_early], k[:, :, 0:n_early], e[:, 0, :, 0:n_early], ALU.mult))
                if three:
                    dve.wait_ge(k_made.sem, k_made.n)
                    k_made.on(dve.tensor_tensor(kx_far, kx[:, :, 0:P],
                                                far[:, :].rearrange("p (h a) -> p h a", a=1).broadcast_to([P, H, P]),
                                                ALU.mult))
                dve.wait_ge(paired.sem, base[paired] + 1)
                chosen.on(dve.tensor_copy(a_next[:, :, :].rearrange("p h t -> p (h t)"), m.ps[:, 0, :]))
                if three:
                    chosen.on(dve.tensor_copy(a_last[:, :, :, :].rearrange("p i h t -> p (i h t)"),
                                              m.ps[:, 1, 0:2 * H * 16]))
                for g in range(len(tiles) * dv_chunks):
                    j, c = g // dv_chunks, g % dv_chunks
                    t0, tn = tiles[j]
                    dve.wait_ge(paired.sem, base[paired] + 2 + g)
                    dst = out[:, out0:out0 + H * dv_chunks, t0:t0 + tn]
                    dst = dst.rearrange("p (h c) t -> p h c t", c=dv_chunks)[:, :, c, :]
                    chosen.on(dve.tensor_copy(dst, m.ps[:, OUT_BANKS[g], 0:H * tn].rearrange("p (h t) -> p h t", h=H)))

            @block.tensor
            def _(pe):
                pe.wait_ge(q_made.sem, base[q_made] + 1)
                pe.wait_ge(k_made.sem, base[k_made] + 1 + three)
                for h in range(H):
                    mm = pe.matmul(m.ps[:, 0, h * P:(h + 1) * P], kx[:, h, 0:P], qx[:, h, 0:P], start=True, stop=True)
                if three:
                    for h in range(H):
                        pe.matmul(m.ps[:, 1, h * 16:(h + 1) * 16], kx_far[:, h, :], qx[:, h, P:P + 16],
                                  start=True, stop=True)
                        mm = pe.matmul(m.ps[:, 1, (H + h) * 16:(H + h + 1) * 16], kx[:, h, P:2 * P],
                                       qx[:, h, P:P + 16], start=True, stop=True)
                paired.on(mm)
                pe.wait_ge(chosen.sem, base[chosen] + 1 + three)
                for g in range(len(tiles) * dv_chunks):
                    j, c = g // dv_chunks, g % dv_chunks
                    tn = tiles[j][1]
                    for h in range(H):
                        for i in range(j + 1):
                            sn = tiles[i][1]
                            if i == j:
                                pairs = a[:, j, h, :] if j < 2 else a_tail[:, h, :]
                            else:
                                pairs = a_next[:, h, :] if j == 1 else a_last[:, i, h, :]
                            col = v0 + (h * dv_chunks + c) * P
                            mm = pe.matmul(m.ps[:, OUT_BANKS[g], h * tn:(h + 1) * tn], v_tokens[0:sn, i, col:col + P],
                                           pairs, start=i == 0, stop=i == j)
                    paired.on(mm)


class GlaGates:

    H = GLA_HEADS
    BANKS = (0, 1, 2, 4)

    def __init__(self, m, dram, q, ranks, b, scope):
        self.m, self.q, self.ranks, self.b, self.source = m, q, ranks, b, dram["w_gate_up"][0]
        self.steps, self.made, self.logs = m.sig("gla_steps"), m.sig("gla_gate_logits"), m.sig("gla_logs")
        self.loaded = m.sig("gla_gate_up_loaded")
        self.up = m.sb("gla_gate_up", [16, self.H * P], ctx=scope)
        self.size = m.sb("gla_gate_size", [P, self.H, T1], ctx=scope)

    def sp(self, sp):
        self.loaded.on(sp.dma_start(self.up[:, :], self.source), 16)

    def pe(self, pe):
        pe.wait_ge(self.loaded.sem, 16)
        for h, bank in enumerate(self.BANKS):
            self.made.on(pe.matmul(self.m.ps[:, bank, 0:T1], self.up[:, h * P:(h + 1) * P], self.ranks,
                                   start=True, stop=True))
        yield

    def dve(self, dve):
        m, b, size, q, steps, H = self.m, self.b, self.size[:, :, :], self.q, self.steps, self.H
        bias = column(m, "b_gate")
        for h, bank in enumerate(self.BANKS):
            dve.wait_ge(self.made.sem, h + 1)
            steps.on(dve.tensor_scalar(b[:, h, :], m.ps[:, bank, 0:T1], bias[:, h:h + 1], None, ALU.add))
        yield
        dve.wait_ge(steps.sem, H)
        steps.on(dve.scalar_tensor_tensor(size, b, -1.0, b, ALU.mult, ALU.max))
        yield
        steps.on(dve.tensor_scalar(q, q, float(P) ** -0.5, None, ALU.mult))
        yield
        dve.wait_ge(self.logs.sem, 2)
        steps.on(dve.scalar_tensor_tensor(b, b, 0.0, size, ALU.min, ALU.subtract))
        dve.wait_ge(steps.sem, steps.n)
        yield
        steps.on(dve.tensor_scalar(b, b, 1.0 / GLA_TAU, None, ALU.mult))
        dve.wait_ge(steps.sem, steps.n)
        yield
        running_sums(dve, m, b, H, TILES, steps)

    def act(self, act):
        yield
        act.wait_ge(self.steps.sem, self.H + 1)
        self.logs.on(act.activation(self.size[:, :, :], self.size[:, :, :], ACT.Exp, scale=-1.0))
        yield
        act.wait_ge(self.logs.sem, 1)
        self.logs.on(act.activation(self.size[:, :, :], self.size[:, :, :], ACT.Ln, bias=1.0))


def running_sums(dve, m, b, heads, tiles, steps):
    for h in range(heads):
        for t0, n in tiles:
            steps.on(dve.tensor_tensor_scan(b[:, h, t0:t0 + n], m.ones[:, 0:n], b[:, h, t0:t0 + n], 0.0,
                                            ALU.mult, ALU.add))


def norm_heads(m, name, o, per_head, eps, gain, gates):
    squared, summed, scaled = m.sig("head_squares"), m.sig("head_sums"), m.sig("head_norm_steps")
    rooted, gated, spread = m.sig("head_roots"), m.sig("head_gates"), m.sig("head_rstd_spread")
    cleared, selected, normed = m.sig("head_place_cleared"), m.sig("head_selected"), m.sig("heads_normed")
    chunks, T = o.shape[1], o.shape[2]
    heads = chunks // per_head
    share = P // heads
    cols = gain.shape[1]
    with ExitStack() as scope:
        sq = m.sb(f"{name}_head_squares", [P, chunks, T], ctx=scope)
        inv = m.sb(f"{name}_head_rstd", [P, T], ctx=scope)
        place = m.sb(f"{name}_head_place", [P, 2 * P - share], ctx=scope)
        select = m.sb(f"{name}_head_select", [P, heads, P], ctx=scope)
        base = {s: s.n for s in (squared, summed, scaled, rooted, gated, spread, cleared, selected, normed)}
        with m.block() as block:

            @block.scalar
            def _(act):
                for h in range(heads):
                    part = slice(h * per_head, (h + 1) * per_head)
                    squared.on(act.activation(sq[:, part, :], o[:, part, :], ACT.Square))
                act.wait_ge(scaled.sem, base[scaled] + 1)
                rooted.on(act.activation(inv[:, :], inv[:, :], ACT.Sqrt))
                for c in range(0, chunks, 2):
                    gated.on(act.activation(gates[:, c:c + 2, :], gates[:, c:c + 2, :], ACT.Silu))

            @block.tensor
            def _(pe):
                pe.wait_ge(cleared.sem, base[cleared] + 2)
                for h in range(heads):
                    pe.wait_ge(squared.sem, base[squared] + h + 1)
                    window = place[:, P - share - h * share:2 * P - share - h * share]
                    for c in range(per_head):
                        mm = pe.matmul(m.ps[:, 0, 0:T], window, sq[:, h * per_head + c, :],
                                       start=h == 0 and c == 0, stop=h == heads - 1 and c == per_head - 1)
                summed.on(mm)
                pe.wait_ge(scaled.sem, base[scaled] + 2)
                pe.wait_ge(selected.sem, base[selected] + 1)
                for h in range(heads):
                    half = slice((h % 2) * T, (h % 2 + 1) * T)
                    spread.on(pe.matmul(m.ps[:, 1 + h // 2, half], select[:, h, :], inv[:, :], start=True, stop=True))

            @block.vector
            def _(dve):
                rows = m.ident[:, :].rearrange("p (h a) -> p h a", a=share)[:, :, 0:1].broadcast_to([P, heads, P])
                selected.on(dve.tensor_copy(select[:, :, :], rows))
                dve.wait_ge(summed.sem, base[summed] + 1)
                scaled.on(dve.tensor_scalar(inv[:, :], m.ps[:, 0, 0:T], 1.0 / (per_head * P), eps, ALU.mult, ALU.add))
                dve.wait_ge(rooted.sem, base[rooted] + 1)
                scaled.on(dve.reciprocal(inv[:, :], inv[:, :]))
                for c in range(chunks):
                    h, x = c // per_head, c % cols
                    dve.wait_ge(spread.sem, base[spread] + 2 * (h // 2) + 2)
                    normed.on(dve.scalar_tensor_tensor(o[:, c, :], o[:, c, :], gain[:, x:x + 1],
                                                       m.ps[:, 1 + h // 2, (h % 2) * T:(h % 2 + 1) * T],
                                                       ALU.mult, ALU.mult))

            @block.gpsimd
            def _(pool):
                cleared.on(pool.memset(place[:, :], 0.0))
                pool.wait_ge(cleared.sem, base[cleared] + 1)
                cleared.on(pool.memset(place[:, P - share:P], 1.0))
                for c in range(0, chunks, 2):
                    pool.wait_ge(gated.sem, base[gated] + c // 2 + 1)
                    pool.wait_ge(normed.sem, base[normed] + c + 2)
                    m.sig("head_gated").on(pool.tensor_tensor(o[:, c:c + 2, :], o[:, c:c + 2, :],
                                                              gates[:, c:c + 2, :], ALU.mult))
                pool.wait_ge(m.sig("head_gated").sem, m.sig("head_gated").n)


D_RWKV = D // 2
PAIRS = D_RWKV // P
HEAD = 64
CHUNK = 64
RANK = 64
GN_EPS = 64e-5
RMS_EPS = 1e-5
LN_EPS = 1e-5
LB_FLOOR = 1e-30
DECAY = float(np.exp(-0.5))
STEPS = [level for level in reversed(range(len(LEVELS))) if 2 * LEVELS[level] <= CHUNK]


def lane(e):
    return slice(e * HEAD, (e + 1) * HEAD)


class Masks64:

    def __init__(self, m, scope, outer):
        n = len(STEPS)
        self.heads = m.sb("same_head", [P, P], ctx=outer)
        self.all = m.sb("masks64", [P, n + 3, CHUNK], ctx=scope)
        made, filled = m.sig("masks64_made"), m.sig("same_head_made")
        with m.block() as block:

            @block.vector
            def _(dve):
                for x, level in enumerate(STEPS + [None, None, len(LEVELS)]):
                    if level is None:
                        continue
                    for e in range(2):
                        made.on(dve.tensor_copy(self.all[lane(e), x, :], m.masks[lane(e), level, lane(e)]))

            @block.gpsimd
            def _(pool):
                filled.on(pool.memset(self.all[:, n:n + 2, :], 1.0))
                filled.on(pool.memset(self.heads[:, :], 0.0))
                pool.wait_ge(filled.sem, filled.n)
                filled.on(pool.memset(self.heads[lane(0), lane(0)], 1.0))
                filled.on(pool.memset(self.heads[lane(1), lane(1)], 1.0))
                pool.wait_ge(filled.sem, filled.n)
                for e in range(2):
                    for x, bound in ((n, -1), (n + 1, 0)):
                        view = self.all[lane(e), x, :]
                        filled.on(pool.affine_select(out=view, in_=view, compare_op=ALU.is_ge, fill=0.0, base=bound,
                                                     pattern=[[1, CHUNK]], channel_multiplier=-1))
                pool.wait_ge(filled.sem, filled.n)
        self.strict, self.causal, self.equal = n, n + 1, n + 2

    def wide(self, x):
        return self.all[:, x:x + 1, :].broadcast_to([P, PAIRS, CHUNK])


def head_sums(pe, m, reducer, x, banks, summed, first=0):
    for g, bank in enumerate(banks, first):
        summed.on(pe.matmul(m.ps[:, bank, :], reducer, x[:, 2 * g:2 * g + 2, :], start=True, stop=True))


def sums_view(m, first_bank):
    return m.ps[:, first_bank:first_bank + PAIRS // 2, :]


def halves(x):
    return x.rearrange("p (g a) t -> p g (a t)", a=2)


def wide_column(col):
    return col.rearrange("p (c a) -> p c a", a=1).broadcast_to([P, PAIRS, SEQ])


class RwkvVectors:

    LORA_BANKS = (0, 1, 2, 4)
    KK_BANKS, BONUS_BANKS = (5, 6), (5, 6, 0, 1)
    SCANS = PAIRS * SEQ // CHUNK
    KK, KK_NORMED, BONUS = 2, 13, 19
    SQUARED, HALF_ROOTED, ROOTED, DECAYS, LAST, INVERSES = 1, 3, 5, 6, 7, 8

    def __init__(self, m, dram, proj, masks, alpha, beta, bonus, last, scope, shifted):
        self.m, self.masks, self.alpha, self.beta, self.bonus, self.last = m, masks, alpha, beta, bonus, last
        self.up_sources = dram["w_decay_up_2"][0], dram["a_up_2"][0]
        self.shifted = shifted
        self.col = {n: column(m, n + "_2") for n in ("w_decay0", "a0", "k_k", "k_a", "r_k")}
        self.r, self.k, self.v = (proj[:, a * PAIRS:(a + 1) * PAIRS, :] for a in range(3))
        self.ranks = proj[:, RANK_PLACE, :]
        self.up = m.sb("lora_up", [P, D_RWKV], ctx=scope)
        self.small = m.sb("rwkv_small", [P, PAIRS], ctx=scope)
        self.sums, self.tmp = (m.sb(f"rwkv_{x}", [P, PAIRS, SEQ], ctx=scope) for x in ("sums", "tmp"))
        self.loaded, self.tanhed = m.sig("lora_loaded"), m.sig("lora_tanh")
        self.made, self.gated, self.steps = m.sig("lora_made"), m.sig("rwkv_gates"), m.sig("rwkv_steps")
        self.summed, self.act_steps = m.sig("rwkv_head_sums"), m.sig("rwkv_act_steps")
        self.scanned = m.sig("rwkv_running_sums")

    def sp(self, sp):
        for e in range(2):
            self.loaded.on(sp.dma_start(self.up[lane(e), :], self.up_sources[e]), 16)

    def act(self, act):
        m, tmp, sums, act_steps, steps = self.m, self.tmp[:, :, :], self.sums, self.act_steps, self.steps
        ranks = self.ranks[lane(0), :]
        self.tanhed.on(act.activation(ranks, ranks, ACT.Tanh))
        yield
        for x in range(2 * PAIRS):
            c, dst, bias = x // 2, (sums, self.beta)[x % 2], (self.col["w_decay0"], self.col["a0"])[x % 2]
            act.wait_ge(self.made.sem, x + 1)
            self.gated.on(act.activation(dst[:, c, :], m.ps[:, self.LORA_BANKS[x % 4], 0:SEQ], ACT.Sigmoid,
                                         bias=bias[:, c:c + 1]))
            if x % 4 == 3:
                if x == 3:
                    act.wait_ge(steps.sem, self.KK)
                    act_steps.on(act.activation(tmp, self.alpha[:, :, :], ACT.Square))
                if x in (7, 11):
                    for n, bank in enumerate(self.KK_BANKS):
                        g = 2 * (x // 4 - 1) + n
                        act.wait_ge(self.summed.sem, g + 1)
                        act_steps.on(act.activation(halves(tmp)[:, g, :], m.ps[:, bank, :], ACT.Sqrt))
                yield
        for _ in range(4):
            yield
        act.wait_ge(self.scanned.sem, self.SCANS)
        act.wait_ge(steps.sem, self.KK_NORMED)
        act_steps.on(act.activation(tmp, sums[:, :, :], ACT.Exp, scale=-DECAY))
        yield
        ends = sums.rearrange("p a (c t) -> p a c t", t=CHUNK)[:, :, :, CHUNK - 1]
        act_steps.on(act.activation(self.last[:, :, :], ends, ACT.Exp, scale=-DECAY))
        act.wait_ge(act_steps.sem, self.LAST)
        act_steps.on(act.activation(sums[:, :, :], sums[:, :, :], ACT.Exp, scale=DECAY))

    def pe(self, pe):
        m, made = self.m, self.made
        yield
        pe.wait_ge(self.loaded.sem, self.loaded.n)
        pe.wait_ge(self.tanhed.sem, self.tanhed.n)
        for x in range(2 * PAIRS):
            c, e = x // 2, x % 2
            if x >= 4:
                pe.wait_ge(self.gated.sem, x - 3)
            made.on(pe.matmul(m.ps[:, self.LORA_BANKS[x % 4], 0:SEQ], self.up[lane(e), c * P:(c + 1) * P],
                              self.ranks[lane(e), :], start=True, stop=True))
            if x in (7, 11):
                pe.wait_ge(self.act_steps.sem, self.SQUARED if x == 7 else self.HALF_ROOTED)
                head_sums(pe, m, self.masks.heads[:, :], self.tmp, self.KK_BANKS, self.summed, 2 * (x // 4 - 1))
            if x % 4 == 3:
                yield
        for _ in range(9):
            yield
        pe.wait_ge(self.steps.sem, self.BONUS)
        pe.wait_ge(self.gated.sem, 2 * PAIRS)
        pe.wait_ge(self.act_steps.sem, self.ROOTED)
        head_sums(pe, m, self.masks.heads[:, :], self.bonus, self.BONUS_BANKS, self.summed)

    def dve(self, dve):
        m, steps, r, k = self.m, self.steps, self.r, self.k
        alpha, beta, bonus, tmp, sums = (x[:, :, :] for x in (self.alpha, self.beta, self.bonus, self.tmp, self.sums))

        def step(ins):
            steps.on(ins)
            dve.wait_ge(steps.sem, steps.n)

        def after(n):
            dve.wait_ge(self.act_steps.sem, n)

        step(dve.tensor_scalar(self.small[:, :], self.col["k_a"], -1.0, 1.0, ALU.mult, ALU.add))
        step(dve.tensor_tensor(alpha, k, wide_column(self.col["k_k"]), ALU.mult))
        yield
        def invert(g):
            after(self.SQUARED + g + 1)
            lengths = halves(tmp)[:, g, :]
            step(dve.tensor_scalar(lengths, lengths, 1e-12, None, ALU.max))
            step(dve.reciprocal(lengths, lengths))

        for g in range(4):
            yield
            dve.wait_ge(self.gated.sem, 4 * g + 4)
            running_sums(dve, m, sums[:, 2 * g:2 * g + 2, :], 2, [(t, CHUNK) for t in range(0, SEQ, CHUNK)],
                         self.scanned)
            if g:
                invert(g - 1)
        yield
        step(dve.tensor_tensor(bonus, beta, wide_column(self.col["k_a"]), ALU.mult))
        invert(3)
        yield
        step(dve.tensor_tensor(bonus, bonus, wide_column(self.small[:, :]), ALU.add))
        yield
        step(dve.tensor_tensor(alpha, alpha, tmp, ALU.mult))
        yield
        step(dve.tensor_tensor(beta, beta, alpha, ALU.mult))
        yield
        step(dve.tensor_tensor(k, k, bonus, ALU.mult))
        yield
        after(self.DECAYS)
        by_chunk, decays = (x.rearrange("p a (c t) -> p (a c) t", t=CHUNK) for x in (alpha, tmp))
        step(dve.scalar_tensor_tensor(by_chunk[:, :, 1:CHUNK], by_chunk[:, :, 1:CHUNK], -1.0,
                                      decays[:, :, 0:CHUNK - 1], ALU.mult, ALU.mult))
        step(dve.tensor_scalar(by_chunk[:, :, 0], by_chunk[:, :, 0], -1.0, None, ALU.mult))
        yield
        step(dve.tensor_tensor(bonus, r, k, ALU.mult))
        yield
        step(dve.tensor_tensor(bonus, bonus, wide_column(self.col["r_k"]), ALU.mult))
        step(dve.tensor_tensor(r, r, tmp, ALU.mult))
        yield
        after(self.INVERSES)
        step(dve.tensor_tensor(k, k, sums, ALU.mult))
        yield
        step(dve.tensor_tensor(beta, beta, sums, ALU.mult))
        dve.wait_ge(m.shift_free, self.shifted + 2)
        for g, bank in enumerate(self.BONUS_BANKS):
            dve.wait_ge(self.summed.sem, 4 + g + 1)
            step(dve.tensor_tensor(halves(bonus)[:, g, :], halves(self.v)[:, g, :], m.ps[:, bank, :], ALU.mult))


class Rwkv:

    CHUNKS = SEQ // CHUNK
    LEVEL_COUNT = len(STEPS)
    MASKED_JOBS, PLAIN_JOBS = 4, 3
    SCAN_PARTS = (2, 2, 2, 3)
    PAUSES = 3 * LEVEL_COUNT - 3
    Y_BANK, X_BANK, XT_BANK, RHS_BANK, SA_BANK, STATE_BANK, JOB_BANK = range(7)
    OUT_BANK = RHS_BANK

    def __init__(self, m, scope, proj, last, alpha, beta, masks, out):
        self.m, self.masks, self.last, self.out = m, masks, last, out
        self.r, self.k, self.v = (proj[:, a * PAIRS:(a + 1) * PAIRS, :] for a in range(3))
        self.alpha, self.beta = alpha, beta

        def tile(name, n=2):
            return m.sb(f"rwkv_{name}", [P, n, PAIRS, CHUNK], ctx=scope)

        self.tok = {name: tile(f"{name}_tokens") for name in ("beta", "k", "v")}
        self.lb, self.lk, self.mb, self.mk = (tile(x) for x in ("lb", "lk", "mb", "mk"))
        self.xt = tile("xt")
        self.level = tile("level")
        self.x, self.y = (tile(x, 1)[:, 0] for x in ("x", "y"))
        self.rhs, self.sa, self.state = (tile(x, 1)[:, 0] for x in ("rhs", "sa", "state"))
        self.fresh = self.rhs

    def bank(self, b):
        return self.m.ps[:, b, :].rearrange("p (a b) -> p a b", b=CHUNK)

    def heads(self, pe, bank, terms, signal, part=(0, 1)):
        n, of = part
        for pair in range(n * PAIRS // of, (n + 1) * PAIRS // of):
            for e in range(2):
                for x, (lhs, rhs) in enumerate(terms):
                    mm = pe.matmul(self.bank(bank)[lane(e), pair, :], lhs(e, pair), rhs(e, pair), start=x == 0,
                                   stop=x == len(terms) - 1)
        if n == of - 1:
            signal.on(mm)

    def turn(self, pe, bank, x, signal):
        for pair in range(PAIRS):
            pe.transpose(self.bank(bank)[lane(0), pair, :], x(0, pair), self.m.ident[lane(0), lane(0)])
            mm = pe.matmul(self.bank(bank)[lane(1), pair, :], x(1, pair), self.m.ident[lane(1), lane(1)], start=True,
                           stop=True)
        signal.on(mm)

    def jobs(self, c):
        masks, b = self.masks, c % 2

        def part(x):
            return lambda e, p: x[lane(e), p, c * CHUNK:(c + 1) * CHUNK]

        return [(part(self.beta), part(self.alpha), self.lb[:, b], masks.strict),
                (part(self.beta), None, self.tok["beta"][:, b], None),
                (part(self.k), part(self.alpha), self.lk[:, b], masks.strict),
                (part(self.k), None, self.tok["k"][:, b], None),
                (part(self.beta), part(self.r), self.mb[:, b], masks.causal),
                (part(self.v), None, self.tok["v"][:, b], None),
                (part(self.k), part(self.r), self.mk[:, b], masks.causal)]

    def pause(self, i, n, scan, job):
        steps = []
        if i >= 1:
            steps += [(scan, i - 1, g, (n, of)) for g, of in enumerate(self.SCAN_PARTS) for n in range(of)]
        if i + 1 < self.CHUNKS:
            for x in range(self.MASKED_JOBS + self.PLAIN_JOBS):
                of = 1 if x % 2 else 2
                steps += [(job, i + 1, x, (n, of)) for n in range(of)]
        if len(steps) <= self.PAUSES:
            here = steps[n:n + 1]
        else:
            here = steps[n * len(steps) // self.PAUSES:(n + 1) * len(steps) // self.PAUSES]
        for step, c, x, part in here:
            step(c, x, part)

    def run(self):
        m, masks, CHUNKS, LEVEL_COUNT = self.m, self.masks, self.CHUNKS, self.LEVEL_COUNT
        MASKED_JOBS, PLAIN_JOBS, JOBS = self.MASKED_JOBS, self.PLAIN_JOBS, self.MASKED_JOBS + self.PLAIN_JOBS
        last = LEVEL_COUNT - 1
        cleared, levelled = m.sig("rwkv_cleared"), m.sig("inverse_levels")
        y_made, y_kept = m.sig("inverse_y_made"), m.sig("inverse_y_kept")
        x_grown, xt_grown = m.sig("inverse_x_grown"), m.sig("inverse_xt_grown")
        x_kept, xt_kept = m.sig("inverse_x_kept"), m.sig("inverse_xt_kept")
        job_made, job_kept, job_copied = m.sig("rwkv_products"), m.sig("rwkv_kept"), m.sig("rwkv_turned")
        made, kept = m.sig("scan_products"), m.sig("scan_kept")
        advanced, stored = m.sig("scan_states"), m.sig("scan_outputs")

        def alone(x):
            return lambda e, p: x[lane(e), p, :]

        def tokens(x, c):
            return lambda e, p: x[lane(e), p, c * CHUNK:(c + 1) * CHUNK]

        with m.block() as block:

            @block.gpsimd
            def _(pool):
                cleared.on(pool.memset(self.state, 0.0))
                for i in range(CHUNKS):
                    pool.wait_ge(job_kept.sem, MASKED_JOBS * i + 1)
                    for s in range(LEVEL_COUNT):
                        n = LEVEL_COUNT * i + s
                        if s == 2:
                            pool.wait_ge(xt_kept.sem, LEVEL_COUNT * i + 1)
                        elif n >= 2:
                            pool.wait_ge(y_made.sem, last * i + s - (1 if s < 2 else 2))
                        levelled.on(pool.tensor_tensor(self.level[:, n % 2], self.lb[:, i % 2], masks.wide(s),
                                                       ALU.mult))
                pool.wait_ge(levelled.sem, levelled.n)

            @block.tensor
            def _(pe):
                def job(c, x, part=(0, 1)):
                    left, right, _, _ = self.jobs(c)[x]
                    if x % 2 == 0 and part[0] == 0 and MASKED_JOBS * c + x // 2 > 0:
                        pe.wait_ge(job_kept.sem, MASKED_JOBS * c + x // 2)
                    if x % 2 == 1 and PLAIN_JOBS * c + x // 2 > 0:
                        pe.wait_ge(job_copied.sem, PLAIN_JOBS * c + x // 2)
                    if x % 2 == 0:
                        self.heads(pe, self.JOB_BANK, [(left, right)], job_made, part)
                    else:
                        self.turn(pe, self.JOB_BANK + 1, left, job_made)

                def scan(c, g, part=(0, 1)):
                    def held(x):
                        return lambda e, p: x[lane(e), c % 2, p, :]

                    first = part[0] == 0
                    if g == 0:
                        if first:
                            pe.wait_ge(job_kept.sem, MASKED_JOBS * (c + 1))
                            pe.wait_ge(job_copied.sem, PLAIN_JOBS * (c + 1))
                            pe.wait_ge(cleared.sem, 1)
                        if first and c:
                            pe.wait_ge(advanced.sem, 2 * c)
                            pe.wait_ge(stored.sem, c)
                        self.heads(pe, self.RHS_BANK, [(tokens(self.alpha, c), alone(self.state)),
                                                       (held(self.lk), held(self.tok["v"]))], made, part)
                    if g == 1:
                        if first:
                            pe.wait_ge(kept.sem, 2 * c + 1)
                            pe.wait_ge(xt_kept.sem, LEVEL_COUNT * (c + 1))
                        self.heads(pe, self.SA_BANK, [(held(self.xt), alone(self.rhs))], made, part)
                    if g >= 2 and first:
                        pe.wait_ge(kept.sem, 2 * c + 2)
                    if g == 2 and c < CHUNKS - 1:
                        self.heads(pe, self.STATE_BANK, [(held(self.tok["beta"]), alone(self.sa)),
                                                         (held(self.tok["k"]), held(self.tok["v"]))], made, part)
                    if g == 3:
                        self.heads(pe, self.OUT_BANK, [(alone(self.state), tokens(self.r, c)),
                                                       (alone(self.sa), held(self.mb)),
                                                       (held(self.tok["v"]), held(self.mk))], made, part)

                for x in range(JOBS):
                    job(0, x)
                for i in range(CHUNKS):
                    for s in range(LEVEL_COUNT):
                        n = LEVEL_COUNT * i + s
                        xt = alone(self.xt[:, i % 2])
                        if s >= 1:
                            pe.wait_ge(levelled.sem, n + 1)
                            pe.wait_ge(x_kept.sem, last * i + s)
                            self.heads(pe, self.Y_BANK, [(alone(self.level[:, n % 2]), alone(self.x))], y_made)
                            self.pause(i, 3 * s - 2, scan, job)
                            pe.wait_ge(y_kept.sem, last * i + s)
                            pe.wait_ge(xt_kept.sem, n)
                            self.heads(pe, self.XT_BANK, [(alone(self.y), xt)], xt_grown)
                            self.pause(i, 3 * s - 1, scan, job)
                        if s < last:
                            pe.wait_ge(xt_kept.sem, n + 1)
                            self.turn(pe, self.X_BANK, xt, x_grown)
                            self.pause(i, 3 * s, scan, job)
                for g in range(len(self.SCAN_PARTS)):
                    scan(CHUNKS - 1, g)

            @block.scalar
            def _(act):
                def job(c, x, part=(0, 1)):
                    if x % 2 == 1:
                        act.wait_ge(job_made.sem, JOBS * c + x + 1)
                        job_copied.on(act.activation(self.jobs(c)[x][2], self.bank(self.JOB_BANK + 1), ACT.Copy))

                def scan(c, g, part=None):
                    if part and part[0] < part[1] - 1:
                        return
                    if g == 0:
                        act.wait_ge(made.sem, 4 * c + 1)
                        kept.on(act.activation(self.rhs, self.bank(self.RHS_BANK), ACT.Copy))
                    if g == 1:
                        act.wait_ge(made.sem, 4 * c + 2)
                        kept.on(act.activation(self.sa, self.bank(self.SA_BANK), ACT.Copy))
                    if g == 3:
                        act.wait_ge(made.sem, 4 * c + (4 if c < CHUNKS - 1 else 3))
                        stored.on(act.activation(self.out[:, :, c * CHUNK:(c + 1) * CHUNK], self.bank(self.OUT_BANK),
                                                 ACT.Copy))

                for x in range(JOBS):
                    job(0, x)
                for i in range(CHUNKS):
                    for s in range(LEVEL_COUNT):
                        if s >= 1:
                            act.wait_ge(y_made.sem, last * i + s)
                            y_kept.on(act.activation(self.y, self.bank(self.Y_BANK), ACT.Copy))
                            self.pause(i, 3 * s - 2, scan, job)
                            self.pause(i, 3 * s - 1, scan, job)
                        if s < last:
                            act.wait_ge(x_grown.sem, last * i + s + 1)
                            x_kept.on(act.activation(self.x, self.bank(self.X_BANK), ACT.Copy))
                            self.pause(i, 3 * s, scan, job)
                for g in range(len(self.SCAN_PARTS)):
                    scan(CHUNKS - 1, g)

            @block.vector
            def _(dve):
                def job(c, x, part=(1, 2)):
                    if x % 2 == 0 and part == (1, 2):
                        _, _, out, mask = self.jobs(c)[x]
                        dve.wait_ge(job_made.sem, JOBS * c + x + 1)
                        job_kept.on(dve.tensor_tensor(out, self.bank(self.JOB_BANK), masks.wide(mask), ALU.mult))

                def scan(c, g, part=None):
                    if c == CHUNKS - 1 or (part and part[0] < part[1] - 1):
                        return
                    if g == 2:
                        dve.wait_ge(made.sem, 4 * c + 3)
                        advanced.on(dve.tensor_tensor(self.fresh, self.bank(self.STATE_BANK), self.state, ALU.add))
                    if g == 3:
                        dve.wait_ge(advanced.sem, 2 * c + 1)
                        dve.wait_ge(made.sem, 4 * c + 4)
                        decay = self.last[:, :, c:c + 1].broadcast_to([P, PAIRS, CHUNK])
                        advanced.on(dve.tensor_tensor(self.state, self.fresh, decay, ALU.mult))

                for x in range(JOBS):
                    job(0, x)
                for i in range(CHUNKS):
                    for s in range(LEVEL_COUNT):
                        xt = self.xt[:, i % 2]
                        if s == 0:
                            dve.wait_ge(levelled.sem, LEVEL_COUNT * i + 1)
                            xt_kept.on(dve.tensor_tensor(xt, self.level[:, LEVEL_COUNT * i % 2],
                                                         masks.wide(masks.equal), ALU.add))
                        else:
                            self.pause(i, 3 * s - 2, scan, job)
                            dve.wait_ge(xt_grown.sem, last * i + s)
                            xt_kept.on(dve.tensor_tensor(xt, self.bank(self.XT_BANK), xt, ALU.add))
                            self.pause(i, 3 * s - 1, scan, job)
                        if s < last:
                            self.pause(i, 3 * s, scan, job)
                for g in range(len(self.SCAN_PARTS)):
                    scan(CHUNKS - 1, g)


class RwkvFinish:

    SUM_BANKS, SQUARE_BANKS = (0, 1, 2, 4), (5, 6, 0, 1)
    GROUPS = PAIRS // 2

    def __init__(self, m, same_head, o, bonus, z, scope):
        self.m, self.same_head, self.o, self.bonus, self.z = m, same_head, o, bonus, z
        self.gn_w, self.gn_b = column(m, "ln_x_w_2"), column(m, "ln_x_b_2")
        self.summed, self.steps = m.sig("gn_sums"), m.sig("gn_steps")
        self.act_steps = m.sig("gn_act_steps")
        self.sq = m.sb("gn_squares", [P, PAIRS, SEQ], ctx=scope)

    def sp(self, sp):
        pass

    def pe(self, pe):
        head_sums(pe, self.m, self.same_head, self.o, self.SUM_BANKS, self.summed)
        yield
        yield
        yield
        pe.wait_ge(self.act_steps.sem, 2)
        head_sums(pe, self.m, self.same_head, self.sq, self.SQUARE_BANKS, self.summed)

    def act(self, act):
        act_steps, sq = self.act_steps, self.sq[:, :, :]
        act_steps.on(act.activation(self.z, self.z, ACT.Silu))
        yield
        yield
        act.wait_ge(self.steps.sem, self.GROUPS)
        act_steps.on(act.activation(sq, self.o, ACT.Square))
        yield
        yield
        yield
        act.wait_ge(self.steps.sem, 2 * self.GROUPS)
        act_steps.on(act.activation(sq, sq, ACT.Sqrt))

    def dve(self, dve):
        m, o, sq, steps, GROUPS = self.m, self.o, self.sq, self.steps, self.GROUPS
        yield
        for g, bank in enumerate(self.SUM_BANKS):
            dve.wait_ge(self.summed.sem, g + 1)
            steps.on(dve.scalar_tensor_tensor(halves(o)[:, g, :], m.ps[:, bank, :], -1.0 / HEAD, halves(o)[:, g, :],
                                              ALU.mult, ALU.add))
        yield
        yield
        yield
        for g, bank in enumerate(self.SQUARE_BANKS):
            dve.wait_ge(self.summed.sem, GROUPS + g + 1)
            steps.on(dve.tensor_scalar(halves(sq[:, :, :])[:, g, :], m.ps[:, bank, :], 1.0 / HEAD, GN_EPS, ALU.mult,
                                       ALU.add))
        yield
        yield
        dve.wait_ge(self.act_steps.sem, 3)
        for g in range(GROUPS):
            steps.on(dve.reciprocal(halves(sq[:, :, :])[:, g, :], halves(sq[:, :, :])[:, g, :]))
            yield
        dve.wait_ge(steps.sem, 3 * GROUPS)
        for c in range(PAIRS):
            steps.on(dve.scalar_tensor_tensor(o[:, c, :], o[:, c, :], self.gn_w[:, c:c + 1], sq[:, c, :], ALU.mult,
                                              ALU.mult))
        yield
        for c in range(PAIRS):
            dve.wait_ge(steps.sem, 3 * GROUPS + c + 1)
            steps.on(dve.scalar_tensor_tensor(o[:, c, :], o[:, c, :], self.gn_b[:, c:c + 1], self.bonus[:, c, :],
                                              ALU.add, ALU.add))
        yield
        dve.wait_ge(steps.sem, steps.n)
        steps.on(dve.tensor_tensor(o, o, self.z, ALU.mult))


class HgrnGates:

    CENTRED, SIZED, FLOORED, DIFFERENCE = 1, 2, 7, 12

    def __init__(self, m, proj, b, scope):
        self.m, self.b = m, b
        self.steps, self.act_steps = m.sig("hgrn_steps"), m.sig("hgrn_act_steps")
        self.logits = column(m, "lb_logits_2")
        self.q, self.f = proj[:, 0:PAIRS, :], proj[:, PAIRS:2 * PAIRS, :]
        bound = m.sb("hgrn_bound", [P, 5, PAIRS], ctx=scope)
        self.size = m.sb("hgrn_size", [P, PAIRS, SEQ], ctx=scope)
        self.share, self.lower, self.log_lower, self.log_rest, self.rest = (bound[:, x, :] for x in range(5))

    def sp(self, sp):
        pass

    def pe(self, pe):
        return iter(())

    def dve(self, dve):
        m, b, f, logits, size = self.m, self.b, self.f, self.logits, self.size[:, :, :]
        share, lower, rest = self.share, self.lower, self.rest
        log_lower, log_rest, steps, act_steps = self.log_lower, self.log_rest, self.steps, self.act_steps

        def step(ins):
            steps.on(ins)

        def settled():
            dve.wait_ge(steps.sem, steps.n)

        def after(n):
            dve.wait_ge(act_steps.sem, n)

        step(dve.tensor_tensor(share, logits, logits, ALU.subtract))
        step(dve.scalar_tensor_tensor(size, f, -1.0, f, ALU.mult, ALU.max))
        yield
        after(1)
        step(dve.reciprocal(lower, share))
        settled()
        step(dve.tensor_tensor(share, share, lower, ALU.mult))
        settled()
        step(dve.tensor_tensor(lower, share, share, ALU.subtract))
        settled()
        step(dve.tensor_scalar(rest, lower, -1.0, 1.0, ALU.mult, ALU.add))
        step(dve.tensor_scalar(log_lower, lower, LB_FLOOR, None, ALU.max))
        yield
        yield
        after(3)
        step(dve.tensor_scalar(log_lower, log_lower, -60.0 * float(np.log(2.0)), None, ALU.add))
        yield
        after(5)
        step(dve.scalar_tensor_tensor(b, f, 0.0, size, ALU.min, ALU.subtract))
        settled()
        yield
        step(dve.tensor_tensor(b, b, wide_column(log_rest), ALU.add))
        settled()
        yield
        step(dve.tensor_tensor(size, b, wide_column(log_lower), ALU.subtract))
        settled()
        yield
        step(dve.scalar_tensor_tensor(size, size, -1.0, size, ALU.mult, ALU.min))
        yield
        step(dve.tensor_tensor(b, b, wide_column(log_lower), ALU.max))
        settled()
        yield
        yield
        after(7)
        step(dve.tensor_tensor(b, b, size, ALU.add))
        settled()
        yield
        for h in range(0, PAIRS, 2):
            running_sums(dve, m, b[:, h:h + 2, :], 2, TILES[0:2], steps)
            yield
        after(8)
        step(dve.tensor_tensor(f, f, wide_column(rest), ALU.mult))

    def act(self, act):
        f, size, share, act_steps = self.f, self.size[:, :, :], self.share, self.act_steps

        def step(ins):
            act_steps.on(ins)

        def after(n):
            act.wait_ge(self.steps.sem, n)

        after(self.CENTRED)
        step(act.activation(share, share, ACT.Exp))
        yield
        after(self.SIZED)
        step(act.activation(size, size, ACT.Exp, scale=-1.0))
        yield
        after(self.FLOORED)
        step(act.activation(self.log_lower, self.log_lower, ACT.Ln, scale=2.0 ** 60))
        step(act.activation(self.log_rest, self.rest, ACT.Ln))
        yield
        act.wait_ge(act_steps.sem, 2)
        step(act.activation(size, size, ACT.Ln, bias=1.0))
        yield
        yield
        yield
        yield
        yield
        after(self.DIFFERENCE)
        step(act.activation(size, size, ACT.Exp))
        yield
        act.wait_ge(act_steps.sem, 6)
        step(act.activation(size, size, ACT.Ln, bias=1.0))
        yield
        step(act.activation(f, f, ACT.Sigmoid, scale=-1.0))
        yield
        step(act.activation(self.q, self.q, ACT.Silu))


def layer_norm_out(m, y, out):
    w, b = column(m, "ln_w_2"), column(m, "ln_b_2")
    squared, summed = m.sig("ln_squared"), m.sig("ln_sums")
    steps, rooted, normed, biased = m.sig("ln_steps"), m.sig("ln_rooted"), m.sig("ln_normed"), m.sig("ln_biased")
    turned, stored, centred = m.sig("out_turned"), m.sig("stored"), m.sig("ln_centred")
    copied = [m.sig("out_copied_act"), m.sig("out_copied_dve")]
    T = SEQ
    groups = [(c0, j) for c0 in range(0, DC, 4) for j in range(T // P)]
    with ExitStack() as scope:
        sq = m.sb("ln_squares", [P, DC, T], ctx=scope)
        stats = m.sb("ln_stats", [P, 2, T], ctx=scope)
        mean, rstd = stats[:, 0, :], stats[:, 1, :]
        rows = sq[:, :, :].rearrange("p (j a) t -> p j (a t)", j=2)

        def copy(eng, parity):
            for g, (c0, j) in enumerate(groups):
                if g % 2 == parity:
                    eng.wait_ge(turned.sem, g + 1)
                    dst, src = rows[:, j, c0 * P:(c0 + 4) * P], m.ps[:, g, :]
                    copied[parity].on(eng.activation(dst, src, ACT.Copy) if parity == 0 else eng.tensor_copy(dst, src))

        with m.block() as block:

            @block.vector
            def _(dve):
                dve.wait_ge(summed.sem, 1)
                steps.on(dve.tensor_scalar(mean, m.ps[:, 6, 0:T], 1.0 / D, None, ALU.mult))
                dve.wait_ge(steps.sem, 1)
                for c in range(0, DC, 4):
                    centred.on(dve.tensor_tensor(y[:, c:c + 4, :], y[:, c:c + 4, :],
                                                 stats[:, 0:1, :].broadcast_to([P, 4, T]), ALU.subtract))
                dve.wait_ge(summed.sem, 2)
                steps.on(dve.tensor_scalar(rstd, m.ps[:, 7, 0:T], 1.0 / D, LN_EPS, ALU.mult, ALU.add))
                dve.wait_ge(rooted.sem, 1)
                steps.on(dve.reciprocal(rstd, rstd))
                dve.wait_ge(steps.sem, 3)
                for c in range(DC):
                    normed.on(dve.scalar_tensor_tensor(y[:, c, :], y[:, c, :], w[:, c:c + 1], rstd, ALU.mult,
                                                       ALU.mult))
                copy(dve, 1)

            @block.scalar
            def _(act):
                for c in range(0, DC, 4):
                    act.wait_ge(centred.sem, c // 4 + 1)
                    squared.on(act.activation(sq[:, c:c + 4, :], y[:, c:c + 4, :], ACT.Square))
                act.wait_ge(steps.sem, 2)
                rooted.on(act.activation(rstd, rstd, ACT.Sqrt))
                for c in range(DC):
                    act.wait_ge(normed.sem, c + 1)
                    biased.on(act.activation(y[:, c, :], y[:, c, :], ACT.Identity, bias=b[:, c:c + 1]))
                copy(act, 0)

            @block.tensor
            def _(pe):
                summed.on(pe.matmul(m.ps[:, 6, 0:T], m.ones[:, :], m.acc[:, 0:T], start=True, stop=True))
                for c in range(DC):
                    if c % 4 == 0:
                        pe.wait_ge(squared.sem, c // 4 + 1)
                    mm = pe.matmul(m.ps[:, 7, 0:T], m.ones[:, :], sq[:, c, :], start=c == 0, stop=c == DC - 1)
                summed.on(mm)
                for g, (c0, j) in enumerate(groups):
                    pe.wait_ge(biased.sem, c0 + 4)
                    for c in range(4):
                        mm = pe.transpose(m.ps[:, g, c * P:(c + 1) * P], y[:, c0 + c, j * P:(j + 1) * P],
                                          m.ident[:, :])
                    turned.on(mm)

            @block.sync
            def _(sp):
                for g, (c0, j) in enumerate(groups):
                    sp.wait_ge(copied[g % 2].sem, g // 2 + 1)
                    stored.on(sp.dma_start(out[0, j * P:(j + 1) * P, c0 * P:(c0 + 4) * P],
                                           rows[:, j, c0 * P:(c0 + 4) * P]), 16)
                sp.wait_ge(stored.sem, stored.n)


VECTORS = [
    [("ffn1_pre_g", DC), ("ffn1_post_g", DC), ("mix_pre_g", DC), ("mix_post_g", DC), ("ffn2_pre_g", DC),
     ("ffn2_post_g", DC), ("b_gate", GLA_HEADS), ("gla_norm_g", GLA_DV // P)],
    [("shift_mu_2", 33), ("w_decay0_2", 8), ("a0_2", 8), ("k_k_2", 8), ("k_a_2", 8), ("r_k_2", 8),
     ("ln_x_w_2", 8), ("ln_x_b_2", 8), ("lb_logits_2", 8), ("g_norm_w_2", 8)],
    [("ln_w_2", DC), ("ln_b_2", DC)],
]


def set_up(m, dram, first):
    made, loaded = m.sig("constants_made"), m.sig("tokens_loaded")
    params_loaded, turned, copied = m.sig("params_loaded"), m.sig("tokens_turned"), m.sig("turned_copied")
    halved = m.sig("gains_halved")
    with ExitStack() as scope:
        tokens = m.sb("tokens", [P, 3, D], ctx=scope)
        rows = m.sb("param_rows", [P, 3, P], ctx=scope)
        vectors = []
        for j, group in enumerate(VECTORS):
            row = 0
            for name, count in group:
                m.param[name] = (j, row, count)
                vectors.append((name, j, row, count))
                row += count
        ROWS_CLEARED, CONSTANTS, IDENTITY = 1, 4, 5
        TOKEN_LOADS = 4
        with m.block() as block:

            @block.sync
            def _(sp):
                head = P - N_META
                meta, x = dram["meta_tokens"], dram["x"][0]
                loaded.on(sp.dma_start(tokens[0:N_META, 0, :], meta), 16)
                loaded.on(sp.dma_start(tokens[N_META:P, 0, :], x[0:head, :]), 16)
                loaded.on(sp.dma_start(tokens[:, 1, :], x[head:head + P, :]), 16)
                loaded.on(sp.dma_start(tokens[0:16, 2, :], x[head + P:SEQ, :]), 16)
                load_unit(m, sp, 0, first, 0, 0)
                sp.wait_ge(made.sem, ROWS_CLEARED)
                for name, j, row, count in vectors:
                    src = dram[name][0].rearrange("(r c) -> r c", c=P)
                    params_loaded.on(sp.dma_start(rows[row:row + count, j, :], src), 16)
                for k in range(1, RAW):
                    load_unit(m, sp, k, first, k, k)

            @block.gpsimd
            def _(pool):
                made.on(pool.memset(rows[:, :, :], 0.0))
                made.on(pool.memset(m.ident[:, :], 0.0))
                made.on(pool.memset(m.ones[:, :], 1.0))
                made.on(pool.memset(m.zero[:, :], 0.0))
                pool.wait_ge(made.sem, CONSTANTS)
                made.on(pool.affine_select(out=m.ident[:, :], in_=m.ident[:, :], compare_op=ALU.not_equal,
                                           fill=1.0, base=0, pattern=[[-1, P]], channel_multiplier=1))
                pool.wait_ge(made.sem, IDENTITY)
                for _ in range(2):
                    pool.nop().then_inc(m.banks_free, 1)
                    pool.nop().then_inc(m.units_done, 1)
                    pool.nop().then_inc(m.hidden_split, 1)
                    pool.nop().then_inc(m.squares_free, 1)
                    pool.nop().then_inc(m.shift_free, 1)

            @block.tensor
            def _(pe):
                pe.wait_ge(made.sem, IDENTITY)
                pe.wait_ge(loaded.sem, 16 * TOKEN_LOADS)
                for c in range(DC):
                    if c >= 4:
                        pe.wait_ge(copied.sem, c - 3)
                    for j, (t0, n) in enumerate(TILES):
                        mm = pe.transpose(m.ps[:, c % 4, t0:t0 + n], tokens[0:n, j, c * P:(c + 1) * P],
                                          m.ident[0:n, 0:n])
                    turned.on(mm)
                pe.wait_ge(params_loaded.sem, 16 * len(vectors))
                for j in range(3):
                    mm = pe.transpose(m.ps[:, 7, j * P:(j + 1) * P], rows[:, j, :], m.ident[:, :])
                turned.on(mm)

            @block.vector
            def _(dve):
                for c in range(DC):
                    dve.wait_ge(turned.sem, c + 1)
                    copied.on(dve.tensor_copy(m.r[:, c, :], m.ps[:, c % 4, 0:T1]))
                dve.wait_ge(turned.sem, DC + 1)
                copied.on(dve.tensor_copy(m.columns[:, :, :].rearrange("p a b -> p (a b)"),
                                          m.ps[:, 7, 0:3 * P]))
                dve.wait_ge(copied.sem, DC + 1)
                for x, name in enumerate(("ffn1_post_g", "ffn2_post_g")):
                    halved.on(dve.tensor_scalar(m.half_gain[:, x, :], column(m, name), 0.5, None, ALU.mult))


def column(m, name):
    j, row, count = m.param[name]
    return m.columns[:, j, row:row + count]


def build(nc, dram, out):
    with ExitStack() as ctx:
        m = Machine(nc, ctx)
        m.param = {}
        m.ps = ctx.enter_context(nc.psum_tensor("ps", [P, 8, 512], F32))
        m.r = m.sb("residual", [P, DC, T1])
        m.open_x("x")
        m.raw = m.sb("w_raw", [P, RAW, DC * P])
        m.w_hi = m.sb("w_hi", [P, SPLIT, DC * P], F32R)
        m.w_lo = m.sb("w_lo", [P, SPLIT, DC * P], F32R)
        m.ident = m.sb("ident", [P, P])
        m.ones = m.sb("ones", [P, P])
        m.zero = m.sb("zero", [P, 1])
        m.columns = m.sb("param_columns", [P, 3, P])
        m.half_gain = m.sb("half_gain", [P, 2, DC])
        m.rstd, m.rstd_post = m.sb("rstd", [P, T1]), m.sb("rstd_post", [P, T1])
        m.sq, m.acc = m.sb("squares", [P, 2, T1]), m.sb("square_sum", [P, T1])
        m.masks = m.sb("masks", [P, len(LEVELS) + 1, P], U8)

        def sem(name):
            return ctx.enter_context(nc.semaphore(name))

        m.raw_loaded = [sem(f"raw_loaded{i}") for i in range(RAW)]
        m.hi_ready, m.lo_ready = sem("hi_ready"), sem("lo_ready")
        m.units_done = sem("units_done")
        m.banks_free = sem("banks_free")
        m.silu_ready, m.hidden_hi = sem("silu_ready"), sem("hidden_hi")
        m.gate_scaled, m.hidden_ready, m.squared = sem("gate_scaled"), sem("hidden_ready"), sem("squared")
        m.squares_free = sem("squares_free")
        m.differed, m.shift_free = sem("differed"), sem("shift_free")
        m.hidden_split = sem("hidden_split")
        stored = m.sig("stored")

        with ExitStack() as scope:
            set_up(m, dram, ffn_stages(m, dram, "ffn1", T1, None, scope, declare=False)[0])
        w_in, w_out = dram["w_in"][0], dram["w_out"][0]
        def qk_stage(out):
            return Project(m, w_in, 4176, 8, T1, out, m.rstd)

        def v_stage(out):
            return Project(m, w_in, 4176 + 8 * P, 9, T1, out, m.rstd)

        def gate_stage(out):
            return Project(m, w_in, 4176 + 2064, 8, T1, out, m.rstd)

        def out_stage(out, w, rstd=None):
            return Project(m, w, 0, DC, SEQ, out, rstd=rstd)

        def rwkv_stage(out, differences=None):
            def place(rel):
                return out, RANK_PLACE if isinstance(rel, int) and rel == 16 else rel

            return Shifted(m, w_in_2, 0, 17, SEQ, None if out is None else place, column(m, "shift_mu_2"), differences)

        def rwkv_gate_stage(out, z=None, differences=None):
            def place(rel):
                return (out, 2 * PAIRS + rel) if rel < PAIRS else (z, rel - PAIRS)

            return Shifted(m, w_in_2, 16 * P, 16, SEQ, None if out is None else place,
                           column(m, "shift_mu_2")[:, 16:32], differences)

        def hgrn_stage(out):
            return Project(m, w_in_2, 33 * P, 16, SEQ, out)

        def hgrn_gate_stage(out):
            return Project(m, w_in_2, (33 + 16) * P, 16, SEQ, None if out is None else out[:, 16:32, :])

        w_in_2, w_out_2 = dram["w_in_2"][0], dram["w_out_2"][0]
        every, h = m.r[:, :, :], m.r[:, :, N_META:T1]

        y_scope = ctx.enter_context(ExitStack())
        y = m.sb("ffn1_y", [P, DC, T1], ctx=y_scope, side="right")
        feed = make_feed(m, every, T1, column(m, "ffn1_pre_g"), norm=True)
        with ExitStack() as scope:
            m.masks_full = m.sb("masks_full", [P, len(LEVELS) + 1, P], ctx=scope)
            run_ffn(m, dram, "ffn1", T1, y, feed, Project(m, w_in, 0, 33, T1, None), lambda pool: make_masks(m, pool))

        mixer_scope = ctx.enter_context(ExitStack())
        gla_qk = m.sb("gla_qk", [P, 8, T1], ctx=mixer_scope)
        with ExitStack() as scope:
            proj = m.sb("dsa_proj", [P, 33, T1], ctx=scope)
            feed = make_feed(m, every, T1, column(m, "mix_pre_g"), (y, m.half_gain[:, 0, :], m.rstd_post), True)
            dense(m, Project(m, w_in, 0, 33, T1, proj, m.rstd), qk_stage(None), feed)
            y_scope.close()
            o_dsa_scope = ctx.enter_context(ExitStack())
            o_dsa = m.sb("o_dsa", [P, DSA_HEADS, SEQ], ctx=o_dsa_scope, side="right")
            v_tokens = m.sb("dsa_v_tokens", [P, 3, DSA_HEADS * P], ctx=scope)
            bias = m.sb("dsa_bias", [P, 2, T1], ctx=scope)
            to_tokens(m, proj[:, 16:24, :], DSA_HEADS, TILES, v_tokens, "dsa")
            with ExitStack() as inner:
                scores = m.sb("dsa_scores", [P, 2, T1], ctx=inner)
                index_scores(m, proj, scores, inner)
                selection = SelectKeys(m, scores, bias, inner)
                dense(m, qk_stage(gla_qk), v_stage(None), beside=selection.pool, stretches=selection)
            with ExitStack() as inner:
                attend(m, proj, v_tokens, bias, o_dsa, inner)
        with mixer_scope as scope:
            proj = m.sb("gla_proj", [P, 9, T1], ctx=scope)
            gates = m.sb("gla_gates", [P, 8, T1], ctx=scope)
            b = m.sb("gla_log_decay", [P, GLA_HEADS, T1], ctx=scope)
            dense(m, v_stage(proj), gate_stage(None))
            q, k = gla_qk[:, 0:GLA_HEADS, :], gla_qk[:, GLA_HEADS:2 * GLA_HEADS, :]
            with ExitStack() as inner:
                dense(m, gate_stage(gates), out_stage(None, w_out),
                      stretches=GlaGates(m, dram, q, proj[0:16, 8, :], b[:, :, :], inner))
            with ExitStack() as inner:
                v_tokens = m.sb("gla_v_tokens", [P, 3, GLA_HEADS * GLA_DV], ctx=inner)
                to_tokens(m, proj[:, 0:8, :], 8, TILES, v_tokens, "gla")
                decay_attention(m, "gla", q, k, b, T1, v_tokens, 0, 2, proj, 0)
            norm_heads(m, "gla", proj[:, 0:8, N_META:T1], 2, EPS, column(m, "gla_norm_g"), gates[:, :, N_META:T1])
            y = m.sb("mixer_out", [P, DC, SEQ], ctx=y_scope, side="right")
            feed = Feed(m, lambda c: o_dsa[:, c, :] if c < 8 else proj[:, c - 8, N_META:T1], SEQ)
            with ExitStack() as nothing:
                ffn2_first = ffn_stages(m, dram, "ffn2", SEQ, None, nothing, declare=False)[0]
            dense(m, out_stage(y, w_out, m.rstd_post), ffn2_first, feed)

        feed = make_feed(m, h, SEQ, column(m, "ffn2_pre_g"), (y, column(m, "mix_post_g"), m.rstd_post), True)
        run_ffn(m, dram, "ffn2", SEQ, y, feed, rwkv_stage(None))

        finish_scope = ctx.enter_context(ExitStack())
        z, bonus = (m.sb(f"rwkv_{x}", [P, PAIRS, SEQ], ctx=finish_scope) for x in ("z", "bonus"))
        with ExitStack() as scope:
            masks = Masks64(m, scope, finish_scope)
            proj = m.sb("rwkv_proj", [P, 3 * PAIRS + 1, SEQ], ctx=scope)
            feed = make_feed(m, h, SEQ, None, (y, m.half_gain[:, 1, :], m.rstd_post))
            differences = m.sb("shift_differences", [P, 2, SEQ], ctx=scope)
            dense(m, rwkv_stage(proj, differences), rwkv_gate_stage(None), feed)
            y_scope.close()
            o_dsa_scope.close()
            alpha, beta = (m.sb(f"rwkv_{x}", [P, PAIRS, SEQ], ctx=scope) for x in ("alpha", "beta"))
            last = m.sb("rwkv_last_decay", [P, PAIRS, SEQ // CHUNK], ctx=scope)
            with ExitStack() as inner:
                stage = rwkv_gate_stage(proj, z, differences)
                dense(m, stage, hgrn_stage(None),
                      stretches=RwkvVectors(m, dram, proj, masks, alpha, beta, bonus, last, inner, m.shifted))
            m.close_x()
            o_rwkv = m.sb("o_rwkv", [P, PAIRS, SEQ], side="right")
            with ExitStack() as inner:
                Rwkv(m, inner, proj, last, alpha, beta, masks, o_rwkv).run()
        m.open_x("x_again")
        with ExitStack() as scope:
            proj = m.sb("hgrn_proj", [P, 32, SEQ], ctx=scope)
            with ExitStack() as inner:
                dense(m, hgrn_stage(proj), hgrn_gate_stage(None), make_feed(m, h, SEQ),
                      stretches=RwkvFinish(m, masks.heads[:, :], o_rwkv[:, :, :], bonus[:, :, :], z[:, :, :], inner))
            with ExitStack() as inner:
                b = m.sb("hgrn_log_decay", [P, 8, SEQ], ctx=inner)
                with ExitStack() as gates:
                    dense(m, hgrn_gate_stage(proj), out_stage(None, w_out_2), stretches=HgrnGates(m, proj, b[:, :, :], gates))
                m.close_x()
                tokens = m.sb("hgrn_tokens", [P, 2, D // 2], ctx=inner)
                to_tokens(m, proj[:, 16:24, :], 8, TILES[0:2], tokens, "hgrn")
                for g in range(2):
                    heads = slice(4 * g, 4 * g + 4)
                    decay_attention(m, f"hgrn{g}", proj[:, heads, :], proj[:, 8 + 4 * g:12 + 4 * g, :], b[:, heads, :],
                                    SEQ, tokens, 4 * g * P, 1, proj, 16 + 4 * g)
            norm_heads(m, "hgrn", proj[:, 16:24, :], 1, RMS_EPS, column(m, "g_norm_w_2"), proj[:, 24:32, :])
            m.open_x("x_out")
            y = m.sb("out_2", [P, DC, SEQ], side="right")
            dense(m, Residual(m, w_out_2, DC, SEQ, y, h), None,
                  Feed(m, lambda c: o_rwkv[:, c, :] if c < 8 else proj[:, 8 + c, :], SEQ))
        layer_norm_out(m, y, out)


def make_feed(m, h, T, gain=None, update=None, norm=False):
    return Feed(m, lambda c: h[:, c, :], T, gain, update, Norm(m, DC, T, m.rstd) if norm else None)


def ffn_stages(m, dram, name, T, y, scope, declare=True):
    def buffer(part, shape, dt=F32):
        return m.sb(f"{name}_{part}", shape, dt, scope) if declare else None

    h_hi, h_lo = buffer("h_hi", [P, FT // 2, T], F32R), buffer("h_lo", [P, FT // 2, T], F32R)
    silu, hidden = buffer("silu", [P, 2, T]), buffer("hidden", [P, 2, T])
    wg, wu, wd = (dram[f"{name}_w_{x}"][0] for x in ("gate", "up", "down"))
    stages = []
    for half in range(2):
        stages.append(GateUp(m, wg, wu, half, T, h_hi, h_lo, silu, hidden, m.rstd))
        stages.append(Down(m, wd, half, h_hi, h_lo, T, y, m.rstd_post if half else None))
    return stages


def run_ffn(m, dram, name, T, y, feed, following, beside=None):
    with ExitStack() as scope:
        stages = ffn_stages(m, dram, name, T, y, scope)
        for x, (stage, then) in enumerate(zip(stages, stages[1:] + [following])):
            dense(m, stage, then, feed if x == 0 else None, beside if x == 1 else None)





def kernel(**inputs):
    import concourse.bacc as _bacc
    from concourse.bass_utils import run_bass_kernel_spmd as _run

    nc = _bacc.Bacc("TRN2", target_bir_lowering=False, num_devices=1)
    arrays, dram = {}, {}
    for name, value in inputs.items():
        if 0 in value.shape:
            continue
        a = np.ascontiguousarray(value)
        arrays[f"in_{name}"] = a
        dram[name] = nc.dram_tensor(f"in_{name}", a.shape, mybir.dt.from_np(a.dtype), kind="ExternalInput").ap()
    out = nc.dram_tensor("out", (1, SEQ, D), F32, kind="ExternalOutput").ap()
    build(nc, dram, out)
    r = _run(nc, [arrays], core_ids=[0])
    return r.results[0]["out"]
```
